# Optimizing a Trainium2 kernel written in Bass

```python
import math
import jax, jax.numpy as jnp
from jax import lax
import numpy as np

D_MODEL = 1024
BATCH = 1
SEQ = 256
DEPTH = 2

GRID_W = 64
CTX_LEN = 256
N_EVEN = (DEPTH + 1) // 2
N_ODD = DEPTH // 2

C_HYENA = D_MODEL // 2
C_NA = D_MODEL - C_HYENA
NA_HEAD_DIM = 32
NA_HEADS = C_NA // NA_HEAD_DIM
NA_WIN_R = 8
NA_WIN_C = 16
NA_QB = 16
NA_BAND = NA_QB + NA_WIN_C
HYENA_ORDER = 2
HYENA_SHORT = 3
HYENA_EMB = 33
HYENA_BANDS = (HYENA_EMB - 1) // 2
HYENA_FILTER_HID = 64
HYENA_FAST_DECAY = 0.3
HYENA_SLOW_DECAY = 1.5
HYENA_TARGET = 1e-2
F_GROUPS = 4
D_FF = 2816
N_EXPERTS = 8
TOP_K = 2
D_FF_EXPERT = 3584
N_MOD = 6
EPS = 1e-6
NEG_INF = -1e30


def rmsnorm(x, g):
    x32 = x.astype(jnp.float32)
    y = x32 * lax.rsqrt(jnp.mean(x32 * x32, axis=-1, keepdims=True) + EPS)
    return (y * g.astype(jnp.float32)).astype(x.dtype)

def modulate(h, shift, scale):
    return h * (1 + scale) + shift

def ada_params(cvec, w, b):
    return jnp.split(jax.nn.silu(cvec) @ w + b, N_MOD, axis=-1)

def swiglu(h, w1, w3, w2):
    return (jax.nn.silu(h @ w1) * (h @ w3)) @ w2

def moe_swiglu(h, w_router, b_router, w1, w3, w2):
    logits = (h @ w_router).astype(jnp.float32) + b_router.astype(jnp.float32)
    top_val, top_idx = lax.top_k(logits, TOP_K)
    top_w = jax.nn.softmax(top_val, axis=-1)
    gate = jnp.einsum('blk,blke->ble', top_w,
                      jax.nn.one_hot(top_idx, N_EXPERTS, dtype=jnp.float32)).astype(h.dtype)
    out = jnp.zeros_like(h)
    for e in range(N_EXPERTS):
        out = out + gate[..., e:e + 1] * swiglu(h, w1[e], w3[e], w2[e])
    return out

def hyena_filters(L, w1, b1, w2, b2, w3, freq):
    f32 = jnp.float32
    w1, b1, w2, b2, w3, freq = (a.astype(f32) for a in (w1, b1, w2, b2, w3, freq))
    t = jnp.linspace(0.0, 1.0, L, dtype=f32)[:, None]
    bands = jnp.linspace(1e-4, HYENA_BANDS - 1, HYENA_BANDS, dtype=f32)
    ang = (2.0 * math.pi / L) * jnp.arange(L, dtype=f32)[:, None] * bands[None, :]
    feats = jnp.concatenate([t, jnp.cos(ang), -jnp.sin(ang)], axis=-1)
    h = jnp.sin(freq[0] * (feats @ w1 + b1))
    h = jnp.sin(freq[1] * (h @ w2 + b2))
    h = (h @ w3).reshape(L, HYENA_ORDER, 2, C_HYENA)
    deltas = jnp.abs(jnp.linspace(math.log(HYENA_TARGET) / HYENA_SLOW_DECAY,
                                  math.log(HYENA_TARGET) / HYENA_FAST_DECAY, C_HYENA, dtype=f32))
    h = h * jnp.exp(-t * deltas[None, :])[:, None, None, :]
    k = jnp.concatenate([h[:, :, 0], jnp.zeros((1, HYENA_ORDER, C_HYENA), f32), h[:0:-1, :, 1]], axis=0)
    return k / (jnp.sum(jnp.abs(k), axis=0, keepdims=True) + EPS)

def long_conv(u, k, skip):
    L = u.shape[1]
    u32 = u.astype(jnp.float32)
    U = jnp.fft.rfft(u32, n=2 * L, axis=1)
    K = jnp.fft.rfft(k, axis=0)
    y = jnp.fft.irfft(U * K[None], n=2 * L, axis=1)[:, :L]
    return (y + u32 * skip.astype(jnp.float32)).astype(u.dtype)

def hyena_mixer(z, short_w, short_b, f_w1, f_b1, f_w2, f_b2, f_w3, f_freq, skip):
    L = z.shape[1]
    zp = jnp.pad(z, ((0, 0), (1, 1), (0, 0)))
    z = zp[:, :-2] * short_w[0] + zp[:, 1:-1] * short_w[1] + zp[:, 2:] * short_w[2] + short_b
    v, x1, x2 = jnp.split(z, 3, axis=-1)
    filt = hyena_filters(L, f_w1, f_b1, f_w2, f_b2, f_w3, f_freq)
    y = x1 * long_conv(v, filt[:, 0], skip[0])
    y = x2 * long_conv(y, filt[:, 1], skip[1])
    return y

def to_heads(t):
    B, L, _ = t.shape
    return t.reshape(B, L, NA_HEADS, NA_HEAD_DIM).transpose(0, 2, 1, 3)

def to_grid(t, rows):
    B = t.shape[0]
    return t.reshape(B, rows, GRID_W, NA_HEADS, NA_HEAD_DIM).transpose(0, 3, 1, 2, 4)

def context_attention(q, k, v):
    s = jnp.einsum('bhqd,bhkd->bhqk', q, k).astype(jnp.float32) * (NA_HEAD_DIM ** -0.5)
    p = jax.nn.softmax(s, axis=-1).astype(v.dtype)
    o = jnp.einsum('bhqk,bhkd->bhqd', p, v)
    B, H, L, dh = o.shape
    return o.transpose(0, 2, 1, 3).reshape(B, L, H * dh)

def neighborhood_attention(q, k, v, k_ctx, v_ctx, rpb):
    B, H, rows, W, dh = q.shape
    win_r = min(NA_WIN_R, rows)
    ncb = W // NA_QB
    scale = dh ** -0.5
    qcol = jnp.arange(W).reshape(ncb, NA_QB)
    c_start = jnp.clip(qcol - NA_WIN_C // 2, 0, W - NA_WIN_C)
    band_start = jnp.clip(jnp.arange(ncb) * NA_QB - NA_WIN_C // 2, 0, W - NA_BAND)
    band_cols = band_start[:, None] + jnp.arange(NA_BAND)
    kcol = band_cols[:, None, :]
    col_ok = (kcol >= c_start[..., None]) & (kcol < c_start[..., None] + NA_WIN_C)
    col_idx = jnp.clip(kcol - qcol[..., None] + NA_WIN_C - 1, 0, 2 * NA_WIN_C - 2)
    rpb32 = rpb.astype(jnp.float32)
    n_loc = win_r * NA_BAND

    def one_row(r):
        r0 = jnp.clip(r - win_r // 2, 0, rows - win_r)
        q_r = lax.dynamic_index_in_dim(q, r, axis=2, keepdims=False).reshape(B, H, ncb, NA_QB, dh)
        k_r = jnp.take(lax.dynamic_slice_in_dim(k, r0, win_r, axis=2), band_cols, axis=3)
        v_r = jnp.take(lax.dynamic_slice_in_dim(v, r0, win_r, axis=2), band_cols, axis=3)
        row_idx = r0 + jnp.arange(win_r) - r + NA_WIN_R - 1
        bias = rpb32[:, row_idx[None, None, :, None], col_idx[:, :, None, :]]
        s_loc = jnp.einsum('bhjqd,bhrjkd->bhjqrk', q_r, k_r).astype(jnp.float32) * scale + bias
        s_loc = jnp.where(col_ok[:, :, None, :], s_loc, NEG_INF)
        s_ctx = jnp.einsum('bhjqd,bhcd->bhjqc', q_r, k_ctx).astype(jnp.float32) * scale
        logits = jnp.concatenate([s_loc.reshape(B, H, ncb, NA_QB, n_loc), s_ctx], axis=-1)
        p = jax.nn.softmax(logits, axis=-1).astype(v.dtype)
        p_loc = p[..., :n_loc].reshape(B, H, ncb, NA_QB, win_r, NA_BAND)
        o = (jnp.einsum('bhjqrk,bhrjkd->bhjqd', p_loc, v_r)
             + jnp.einsum('bhjqc,bhcd->bhjqd', p[..., n_loc:], v_ctx))
        return o.reshape(B, H, W, dh)

    out = lax.map(one_row, jnp.arange(rows))
    return out.transpose(1, 0, 3, 2, 4).reshape(B, rows * W, H * dh)

def fourier_mix(h):
    B, L, D = h.shape
    hg = h.astype(jnp.float32).reshape(B, L, F_GROUPS, D // F_GROUPS)
    y = jnp.fft.fftn(hg, axes=(1, 3), norm='ortho').real
    return y.reshape(B, L, D).astype(h.dtype)

def first_inputs(seed: int = 0) -> dict:
    key = jax.random.key(seed)
    ks = iter(jax.random.split(key, 32))
    f32 = jnp.float32
    D = D_MODEL

    def dense(shape, fan_in):
        return jax.random.normal(next(ks), shape, f32) * (fan_in ** -0.5)

    def small(shape, s):
        return jax.random.normal(next(ks), shape, f32) * s

    return {
        'x': small((BATCH, SEQ, D), 1.0),
        'c': small((BATCH, D), 1.0),
        'ctx': small((BATCH, CTX_LEN, D), 1.0),
        'c_ctx': small((D,), 1.0),
        'w_ada': dense((DEPTH, D, N_MOD * D), D),
        'b_ada': small((DEPTH, N_MOD * D), 0.02),
        'norm_g': 1.0 + small((DEPTH, 2, D), 0.02),
        'w_in': dense((N_EVEN, D, 3 * C_HYENA + 3 * C_NA), D),
        'hy_short_w': dense((N_EVEN, HYENA_SHORT, 3 * C_HYENA), HYENA_SHORT),
        'hy_short_b': small((N_EVEN, 3 * C_HYENA), 0.02),
        'hy_f_w1': dense((N_EVEN, HYENA_EMB, HYENA_FILTER_HID), HYENA_EMB),
        'hy_f_b1': small((N_EVEN, HYENA_FILTER_HID), 0.02),
        'hy_f_w2': dense((N_EVEN, HYENA_FILTER_HID, HYENA_FILTER_HID), HYENA_FILTER_HID),
        'hy_f_b2': small((N_EVEN, HYENA_FILTER_HID), 0.02),
        'hy_f_w3': dense((N_EVEN, HYENA_FILTER_HID, HYENA_ORDER * 2 * C_HYENA), HYENA_FILTER_HID),
        'hy_f_freq': 1.0 + small((N_EVEN, 2, HYENA_FILTER_HID), 0.02),
        'hy_skip': small((N_EVEN, HYENA_ORDER, C_HYENA), 0.5),
        'na_rpb': small((N_EVEN, NA_HEADS, 2 * NA_WIN_R - 1, 2 * NA_WIN_C - 1), 0.1),
        'w_mix_out': dense((N_EVEN, D, D), D),
        'ffn_w1': dense((N_EVEN, D, D_FF), D),
        'ffn_w3': dense((N_EVEN, D, D_FF), D),
        'ffn_w2': dense((N_EVEN, D_FF, D), D_FF),
        'w_fourier': dense((N_ODD, D, D), D),
        'w_router': dense((N_ODD, D, N_EXPERTS), D),
        'b_router': small((N_ODD, N_EXPERTS), 0.01),
        'moe_w1': dense((N_ODD, N_EXPERTS, D, D_FF_EXPERT), D),
        'moe_w3': dense((N_ODD, N_EXPERTS, D, D_FF_EXPERT), D),
        'moe_w2': dense((N_ODD, N_EXPERTS, D_FF_EXPERT, D), D_FF_EXPERT),
        'final_g': 1.0 + small((D,), 0.02),
    }

def first_block(x, c, ctx, c_ctx, w_ada, b_ada, norm_g, w_in, hy_short_w, hy_short_b,
              hy_f_w1, hy_f_b1, hy_f_w2, hy_f_b2, hy_f_w3, hy_f_freq, hy_skip, na_rpb,
              w_mix_out, ffn_w1, ffn_w3, ffn_w2, w_fourier, w_router, b_router,
              moe_w1, moe_w3, moe_w2, final_g):
    rows = x.shape[1] // GRID_W
    kv_off = 3 * C_HYENA + C_NA
    xc = ctx
    for layer in range(DEPTH):
        even = layer % 2 == 0
        update_ctx = any(l % 2 == 0 for l in range(layer + 1, DEPTH))
        g_mix, g_ffn = norm_g[layer, 0], norm_g[layer, 1]
        sh1, sc1, gt1, sh2, sc2, gt2 = ada_params(c[:, None, :], w_ada[layer], b_ada[layer])
        if even or update_ctx:
            csh1, csc1, cgt1, csh2, csc2, cgt2 = ada_params(c_ctx[None, None, :], w_ada[layer], b_ada[layer])
        if even:
            i = layer // 2
            hy = (hy_short_w[i], hy_short_b[i], hy_f_w1[i], hy_f_b1[i], hy_f_w2[i], hy_f_b2[i],
                  hy_f_w3[i], hy_f_freq[i], hy_skip[i])
            h = modulate(rmsnorm(x, g_mix), sh1, sc1)
            z = h @ w_in[i]
            q, k, v = jnp.split(z[..., 3 * C_HYENA:], 3, axis=-1)
            hc = modulate(rmsnorm(xc, g_mix), csh1, csc1)
            if update_ctx:
                zc = hc @ w_in[i]
                kvc = zc[..., kv_off:]
            else:
                kvc = hc @ w_in[i][:, kv_off:]
            kc, vc = jnp.split(kvc, 2, axis=-1)
            kc, vc = to_heads(kc), to_heads(vc)
            y_na = neighborhood_attention(to_grid(q, rows), to_grid(k, rows), to_grid(v, rows), kc, vc, na_rpb[i])
            y_hy = hyena_mixer(z[..., :3 * C_HYENA], *hy)
            x = x + gt1 * (jnp.concatenate([y_hy, y_na], axis=-1) @ w_mix_out[i])
            if update_ctx:
                yc_na = context_attention(to_heads(zc[..., 3 * C_HYENA:kv_off]), kc, vc)
                yc_hy = hyena_mixer(zc[..., :3 * C_HYENA], *hy)
                xc = xc + cgt1 * (jnp.concatenate([yc_hy, yc_na], axis=-1) @ w_mix_out[i])
            x = x + gt2 * swiglu(modulate(rmsnorm(x, g_ffn), sh2, sc2), ffn_w1[i], ffn_w3[i], ffn_w2[i])
            if update_ctx:
                xc = xc + cgt2 * swiglu(modulate(rmsnorm(xc, g_ffn), csh2, csc2), ffn_w1[i], ffn_w3[i], ffn_w2[i])
        else:
            j = layer // 2
            x = x + gt1 * (fourier_mix(modulate(rmsnorm(x, g_mix), sh1, sc1)) @ w_fourier[j])
            x = x + gt2 * moe_swiglu(modulate(rmsnorm(x, g_ffn), sh2, sc2), w_router[j], b_router[j],
                                     moe_w1[j], moe_w3[j], moe_w2[j])
            if update_ctx:
                xc = xc + cgt1 * (fourier_mix(modulate(rmsnorm(xc, g_mix), csh1, csc1)) @ w_fourier[j])
                xc = xc + cgt2 * moe_swiglu(modulate(rmsnorm(xc, g_ffn), csh2, csc2), w_router[j], b_router[j],
                                            moe_w1[j], moe_w3[j], moe_w2[j])
    return rmsnorm(x, final_g)


N_MIXERS = 2
N_RET = (DEPTH + 1) // 2
N_S5 = DEPTH // 2
RET_HEADS = 4
RET_DK = D_MODEL // RET_HEADS
RET_DV = 2 * RET_DK
RET_QK = RET_HEADS * RET_DK
RET_V = RET_HEADS * RET_DV
RET_PROJ = 2 * RET_QK + 2 * RET_V
RET_CHUNK = 128
ROPE_BASE = 10000.0
S5_GROUP = 16
S5_GROUPS = D_MODEL // S5_GROUP
S5_STATE = 64
DT_MIN = 1e-3
DT_MAX = 1e-1
CONV_W = 3


def rms_norm(x):
    xf = x.astype(jnp.float32)
    return (xf * lax.rsqrt(jnp.mean(xf * xf, axis=-1, keepdims=True) + EPS)).astype(x.dtype)

def rotary(t, pos):
    half = t.shape[-1] // 2
    inv_freq = jnp.power(ROPE_BASE, -jnp.arange(half, dtype=jnp.float32) / half)
    ang = pos.astype(jnp.float32)[..., None] * inv_freq
    cos = jnp.cos(ang)[:, :, None, :]
    sin = jnp.sin(ang)[:, :, None, :]
    t1 = t[..., :half].astype(jnp.float32)
    t2 = t[..., half:].astype(jnp.float32)
    return jnp.concatenate([t1 * cos - t2 * sin, t1 * sin + t2 * cos], axis=-1).astype(t.dtype)

def retention_chunkwise(q, k, v):
    bsz, L = q.shape[0], q.shape[1]
    nc = L // RET_CHUNK
    log_gamma = jnp.log1p(-jnp.exp2(-5.0 - jnp.arange(RET_HEADS, dtype=jnp.float32)))
    idx = jnp.arange(RET_CHUNK, dtype=jnp.float32)
    diff = idx[:, None] - idx[None, :]
    intra = jnp.where(diff[None] >= 0,
                      jnp.exp(log_gamma[:, None, None] * jnp.maximum(diff, 0.0)[None]), 0.0)
    cross = jnp.exp(log_gamma[:, None] * (idx + 1.0))
    to_state = jnp.exp(log_gamma[:, None] * (RET_CHUNK - 1.0 - idx))
    chunk_decay = jnp.exp(log_gamma * RET_CHUNK)

    def to_chunks(t):
        return t.reshape(bsz, nc, RET_CHUNK, RET_HEADS, t.shape[-1]).transpose(1, 0, 3, 2, 4)

    def step(state, qkv):
        qc, kc, vc = qkv
        s = jnp.einsum('bhnd,bhmd->bhnm', qc, kc) * intra[None]
        o = (jnp.einsum('bhnm,bhmv->bhnv', s, vc)
             + jnp.einsum('bhnd,bhdv->bhnv', qc, state) * cross[None, :, :, None])
        state = (chunk_decay[None, :, None, None] * state
                 + jnp.einsum('bhmd,bhmv->bhdv', kc * to_state[None, :, :, None], vc))
        return state, o

    state0 = jnp.zeros((bsz, RET_HEADS, RET_DK, RET_DV), jnp.float32)
    _, o = lax.scan(step, state0, (to_chunks(q), to_chunks(k), to_chunks(v)))
    return o.transpose(1, 0, 3, 2, 4).reshape(bsz, L, RET_HEADS, RET_DV)

def retention_mixer(h, pos, w_in, w_out):
    bsz, L, _ = h.shape
    proj = h @ w_in
    q, k, v, g = jnp.split(proj, [RET_QK, 2 * RET_QK, 2 * RET_QK + RET_V], axis=-1)
    q = rotary(q.reshape(bsz, L, RET_HEADS, RET_DK), pos)
    k = rotary(k.reshape(bsz, L, RET_HEADS, RET_DK), pos) * (RET_DK ** -0.5)
    v = v.reshape(bsz, L, RET_HEADS, RET_DV)
    o = retention_chunkwise(q.astype(jnp.float32), k.astype(jnp.float32), v.astype(jnp.float32))
    mu = jnp.mean(o, axis=-1, keepdims=True)
    oc = o - mu
    o = oc * lax.rsqrt(jnp.mean(oc * oc, axis=-1, keepdims=True) + EPS)
    o = o.reshape(bsz, L, RET_V).astype(h.dtype)
    return (jax.nn.silu(g) * o) @ w_out

def s5_mixer(h, w_in, lam_re, lam_im, log_dt, b_re, b_im, c_re, c_im, d_skip, w_glu):
    bsz, L, _ = h.shape
    u = (h @ w_in).astype(jnp.float32)
    ug = u.reshape(bsz, L, S5_GROUPS, S5_GROUP)
    dt = jnp.exp(log_dt.astype(jnp.float32))[:, None]
    lr = lam_re.astype(jnp.float32)
    li = lam_im.astype(jnp.float32)
    mag = jnp.exp(lr * dt)
    ar = mag * jnp.cos(li * dt)
    ai = mag * jnp.sin(li * dt)
    nr = ar - 1.0
    den = lr * lr + li * li
    fr = (nr * lr + ai * li) / den
    fi = (ai * lr - nr * li) / den
    br = b_re.astype(jnp.float32)
    bi = b_im.astype(jnp.float32)
    bbr = fr[..., None] * br - fi[..., None] * bi
    bbi = fr[..., None] * bi + fi[..., None] * br
    bu_r = jnp.einsum('blgi,gpi->lbgp', ug, bbr)
    bu_i = jnp.einsum('blgi,gpi->lbgp', ug, bbi)
    a_r = jnp.broadcast_to(ar[None, None], (L, 1, S5_GROUPS, S5_STATE))
    a_i = jnp.broadcast_to(ai[None, None], (L, 1, S5_GROUPS, S5_STATE))

    def combine(e1, e2):
        a1r, a1i, b1r, b1i = e1
        a2r, a2i, b2r, b2i = e2
        return (a2r * a1r - a2i * a1i,
                a2r * a1i + a2i * a1r,
                a2r * b1r - a2i * b1i + b2r,
                a2r * b1i + a2i * b1r + b2i)

    _, _, s_r, s_i = lax.associative_scan(combine, (a_r, a_i, bu_r, bu_i), axis=0)
    y = (jnp.einsum('lbgp,gip->blgi', s_r, c_re.astype(jnp.float32))
         - jnp.einsum('lbgp,gip->blgi', s_i, c_im.astype(jnp.float32)))
    y = y.reshape(bsz, L, D_MODEL) + d_skip.astype(jnp.float32) * u
    y = jax.nn.gelu(y).astype(h.dtype)
    ya, yb = jnp.split(y @ w_glu, 2, axis=-1)
    return ya * jax.nn.sigmoid(yb)

def conv_ffn(h, w_up, conv_w, conv_b, w_down):
    val, gate = jnp.split(h @ w_up, 2, axis=-1)
    gate = lax.conv_general_dilated(gate, conv_w.astype(gate.dtype), window_strides=(1,),
                                    padding=[(CONV_W - 1, 0)],
                                    dimension_numbers=('NWC', 'WIO', 'NWC'),
                                    feature_group_count=D_FF) + conv_b
    return (jax.nn.silu(gate) * val) @ w_down

def second_inputs(seed: int = 0) -> dict:
    key = jax.random.key(seed)
    ks = jax.random.split(key, 24)
    f32 = jnp.float32
    nrm = lambda k, shape, s: jax.random.normal(k, shape, f32) * s
    x = nrm(ks[0], (BATCH, SEQ, D_MODEL), 1.0)
    c = nrm(ks[1], (BATCH, D_MODEL), 1.0)
    offset = jax.random.randint(ks[2], (BATCH, 1), 0, 1024, dtype=jnp.int32)
    pos = offset + jnp.arange(SEQ, dtype=jnp.int32)[None, :]
    ada_w = nrm(ks[3], (DEPTH, D_MODEL, 6 * D_MODEL), D_MODEL ** -0.5)
    ada_b = nrm(ks[4], (DEPTH, 6 * D_MODEL), 0.02)
    ret_w_in = nrm(ks[5], (N_RET, D_MODEL, RET_PROJ), D_MODEL ** -0.5)
    ret_w_out = nrm(ks[6], (N_RET, RET_V, D_MODEL), RET_V ** -0.5)
    s5_w_in = nrm(ks[7], (N_S5, D_MODEL, D_MODEL), D_MODEL ** -0.5)
    s5_lam_re = -0.5 * jnp.exp(nrm(ks[8], (N_S5, S5_GROUPS, S5_STATE), 0.02))
    s5_lam_im = (math.pi * jnp.arange(S5_STATE, dtype=f32))[None, None, :] + nrm(ks[9], (N_S5, S5_GROUPS, S5_STATE), 0.01)
    s5_log_dt = jax.random.uniform(ks[10], (N_S5, S5_GROUPS), f32, math.log(DT_MIN), math.log(DT_MAX))
    s5_b_re = nrm(ks[11], (N_S5, S5_GROUPS, S5_STATE, S5_GROUP), (2 * S5_GROUP) ** -0.5)
    s5_b_im = nrm(ks[12], (N_S5, S5_GROUPS, S5_STATE, S5_GROUP), (2 * S5_GROUP) ** -0.5)
    s5_c_re = nrm(ks[13], (N_S5, S5_GROUPS, S5_GROUP, S5_STATE), S5_STATE ** -0.5)
    s5_c_im = nrm(ks[14], (N_S5, S5_GROUPS, S5_GROUP, S5_STATE), S5_STATE ** -0.5)
    s5_d = nrm(ks[15], (N_S5, D_MODEL), 1.0)
    s5_w_glu = nrm(ks[16], (N_S5, D_MODEL, 2 * D_MODEL), D_MODEL ** -0.5)
    ffn_w_up = nrm(ks[17], (DEPTH, D_MODEL, 2 * D_FF), D_MODEL ** -0.5)
    ffn_conv_w = nrm(ks[18], (DEPTH, CONV_W, 1, D_FF), CONV_W ** -0.5)
    ffn_conv_b = nrm(ks[19], (DEPTH, D_FF), 0.02)
    ffn_w_down = nrm(ks[20], (DEPTH, D_FF, D_MODEL), D_FF ** -0.5)
    final_norm_g = 1.0 + nrm(ks[21], (D_MODEL,), 0.02)
    return {"x": x, "c": c, "pos": pos, "ada_w": ada_w, "ada_b": ada_b,
            "ret_w_in": ret_w_in, "ret_w_out": ret_w_out,
            "s5_w_in": s5_w_in, "s5_lam_re": s5_lam_re, "s5_lam_im": s5_lam_im,
            "s5_log_dt": s5_log_dt, "s5_b_re": s5_b_re, "s5_b_im": s5_b_im,
            "s5_c_re": s5_c_re, "s5_c_im": s5_c_im, "s5_d": s5_d, "s5_w_glu": s5_w_glu,
            "ffn_w_up": ffn_w_up, "ffn_conv_w": ffn_conv_w, "ffn_conv_b": ffn_conv_b,
            "ffn_w_down": ffn_w_down, "final_norm_g": final_norm_g}

def second_block(x, c, pos, ada_w, ada_b, ret_w_in, ret_w_out, s5_w_in, s5_lam_re, s5_lam_im,
              s5_log_dt, s5_b_re, s5_b_im, s5_c_re, s5_c_im, s5_d, s5_w_glu,
              ffn_w_up, ffn_conv_w, ffn_conv_b, ffn_w_down, final_norm_g):
    cond = jax.nn.silu(c)
    for i in range(DEPTH):
        mod = cond @ ada_w[i] + ada_b[i]
        sh1, sc1, g1, sh2, sc2, g2 = jnp.split(mod[:, None, :], 6, axis=-1)
        h = rms_norm(x) * (1.0 + sc1) + sh1
        j = i // N_MIXERS
        if i % N_MIXERS == 0:
            y = retention_mixer(h, pos, ret_w_in[j], ret_w_out[j])
        else:
            y = s5_mixer(h, s5_w_in[j], s5_lam_re[j], s5_lam_im[j], s5_log_dt[j],
                         s5_b_re[j], s5_b_im[j], s5_c_re[j], s5_c_im[j], s5_d[j], s5_w_glu[j])
        x = x + g1 * y
        h = rms_norm(x) * (1.0 + sc2) + sh2
        x = x + g2 * conv_ffn(h, ffn_w_up[i], ffn_conv_w[i], ffn_conv_b[i], ffn_w_down[i])
    return rms_norm(x) * final_norm_g


def setup_inputs(seed=0):
    out = dict(first_inputs(seed))
    for name, value in second_inputs(seed + 1).items():
        if name != "x":
            out[name + "_2"] = value
    return out


def reference(
    x, c, ctx, c_ctx, w_ada, b_ada, norm_g, w_in, hy_short_w, hy_short_b, hy_f_w1, hy_f_b1,
    hy_f_w2, hy_f_b2, hy_f_w3, hy_f_freq, hy_skip, na_rpb, w_mix_out, ffn_w1, ffn_w3, ffn_w2,
    w_fourier, w_router, b_router, moe_w1, moe_w3, moe_w2, final_g, c_2, pos_2, ada_w_2,
    ada_b_2, ret_w_in_2, ret_w_out_2, s5_w_in_2, s5_lam_re_2, s5_lam_im_2, s5_log_dt_2,
    s5_b_re_2, s5_b_im_2, s5_c_re_2, s5_c_im_2, s5_d_2, s5_w_glu_2, ffn_w_up_2, ffn_conv_w_2,
    ffn_conv_b_2, ffn_w_down_2, final_norm_g_2,
):
    x = first_block(
        x, c, ctx, c_ctx, w_ada, b_ada, norm_g, w_in, hy_short_w, hy_short_b, hy_f_w1, hy_f_b1,
        hy_f_w2, hy_f_b2, hy_f_w3, hy_f_freq, hy_skip, na_rpb, w_mix_out, ffn_w1, ffn_w3,
        ffn_w2, w_fourier, w_router, b_router, moe_w1, moe_w3, moe_w2, final_g,
    )
    return second_block(
        x, c_2, pos_2, ada_w_2, ada_b_2, ret_w_in_2, ret_w_out_2, s5_w_in_2, s5_lam_re_2,
        s5_lam_im_2, s5_log_dt_2, s5_b_re_2, s5_b_im_2, s5_c_re_2, s5_c_im_2, s5_d_2,
        s5_w_glu_2, ffn_w_up_2, ffn_conv_w_2, ffn_conv_b_2, ffn_w_down_2, final_norm_g_2,
    )


_drawn_inputs = setup_inputs


def setup_inputs(seed=0):
    import zlib

    import numpy as np

    out = dict(_drawn_inputs(seed))
    spreads = {}
    factors = {'hy_f_b1': 2.96,
     'hy_f_b2': 3.605,
     'na_rpb': 4.767,
     's5_lam_re_2': 64.0,
     's5_log_dt_2': 120.672,
     's5_b_re_2': 192.016,
     's5_b_im_2': 23.382,
     's5_c_re_2': 172.856,
     's5_c_im_2': 25.269,
     'ffn_conv_b_2': 5.171,
     'final_norm_g_2': 22.693,
     'hy_f_freq': 3.258,
     's5_lam_im_2': 5.511,
     'hy_short_b': 2.702,
     'b_router': 2.708}
    for name, (base, spread) in spreads.items():
        noise = np.random.default_rng([zlib.crc32(name.encode()), seed]).standard_normal(out[name].shape)
        drawn = base * np.exp(spread * noise) if base else spread * noise
        out[name] = __import__('jax').numpy.asarray(drawn.astype(out[name].dtype))
    for name, factor in factors.items():
        out[name] = (out[name] * factor).astype(out[name].dtype)
    return out
```

```python
import math
from contextlib import ExitStack

import numpy as np

import concourse.bass as bass
from concourse import mybir

F32 = mybir.dt.float32
I32 = mybir.dt.int32
U32 = mybir.dt.uint32
ACT = mybir.ActivationFunctionType
ALU = mybir.AluOpType
AX = mybir.AxisListType

P = 128
D = 1024
KD = D // P
SEQ = 256
TT = SEQ // P
EPS = 1e-6
NEG = -1e30
BANK = 512
N_MOD = 6

CH = 512
HY_BANDS = 16
HY_EMB = 2 * HY_BANDS + 1
HY_HID = 64
HY_CHUNKS = 3 * CH // P
GRID_W = 64
GRID_R = SEQ // GRID_W
WIN_R, WIN_C = 8, 16
RPB_R, RPB_C = 2 * WIN_R - 1, 2 * WIN_C - 1
HEADS = 16
HEAD_DIM = 32
FF = 2816
FF_CHUNKS = FF // P
EXPERTS = 8
FFE = 3584
RET_HEADS = 4
RET_DK = 256
RET_DV = 512
S5_GROUP = 16
S5_STATE = 64
S5_TILES = D // S5_GROUP * S5_STATE // P

RING = 7
TILE = 2048

TWO_PI = 2 * math.pi
MAGIC = 1.5 * 2.0 ** 23
PI_CLAMP = 3.1415925
PI_A = 6.28125
PI_B = float(np.float32(math.floor((TWO_PI - PI_A) * 2 ** 21) / 2 ** 21))
PI_C = float(np.float32(TWO_PI - PI_A - PI_B))

STOP = 99


class Chain:

    def __init__(self, eng, own):
        self.eng, self.own, self.n = eng, own, {}

    def step(self, ins, sem=None):
        sem = sem or self.own
        self.n[sem.name] = self.n.get(sem.name, 0) + 1
        ins.then_inc(sem, 1)
        return sem, self.n[sem.name]

    def link(self, ins, sem=None):
        self.eng.wait_ge(*self.step(ins, sem))


class LoopChain:

    def __init__(self, eng, own, rnd, per):
        self.eng, self.own, self.rnd, self.per, self.n = eng, own, rnd, per, 0

    def link(self, ins):
        self.n += 1
        ins.then_inc(self.own, 1)
        self.eng.wait_ge(self.own, self.rnd * self.per + self.n)


class Stream:

    def __init__(self, items, landed, done):
        self.items, self.landed, self.done = items, landed, done
        self.first = {}
        for i, it in enumerate(items):
            self.first.setdefault(it[0], i)

    def need(self, pe, i):
        pe.wait_ge(self.landed[i % RING], 16 * (i // RING + 1))

    def wait_done(self, eng, i):
        eng.wait_ge(self.done, i + 1)


def ada_tiles(name, w):
    return [(name, w[BANK * h:BANK * (h + 1), BANK * n:BANK * (n + 1)], 4) for n in range(N_MOD * D // BANK) for h in range(2)]


def col_tile(name, w, j):
    return (name, w[:, 256 * j:256 * (j + 1)], 8)


def half_tiles(name, w, col):
    return [(name, w[BANK * h:BANK * (h + 1), col:col + BANK], 4) for h in range(2)]


def row_tiles(name, w):
    rows = TILE * P // w.shape[1]
    return [(name, w[rows * j:rows * (j + 1), :], rows // P) for j in range(w.shape[0] // rows)]


MOE_CHUNKS = FFE // BANK


def moe_order():
    order = []
    for c in range(MOE_CHUNKS + 1):
        if c < MOE_CHUNKS:
            order += [("w1", c, 0), ("w1", c, 1), ("w3", c, 0), ("w3", c, 1)]
        if c >= 1:
            order += [("w2", c - 1, 0), ("w2", c - 1, 1)]
    return order


def build(nc, A, out):
    with ExitStack() as ctx:
        def sb(name, shape, dt=F32):
            return ctx.enter_context(nc.sbuf_tensor(name, shape, dt))

        sems = {}

        def sem(name):
            if name not in sems:
                sems[name] = ctx.enter_context(nc.semaphore(name))
            return sems[name]

        wa, wi = A["w_ada"], A["w_in"][0]
        items = ada_tiles("ada0", wa[0])
        items += [col_tile("hy_in", wi, j) for j in range(6)]
        items += [col_tile("q_in", wi, 6 + j) for j in range(2)]
        items += [col_tile("k_in", wi, 8 + j) for j in range(2)]
        items += half_tiles("v_in", wi, 5 * CH)
        items += row_tiles("mix", A["w_mix_out"][0])
        for j in range(FF // 256):
            items += [col_tile("ffn_up", A["ffn_w1"][0], j), col_tile("ffn_up", A["ffn_w3"][0], j)]
        items += row_tiles("ffn_down", A["ffn_w2"][0])
        items += row_tiles("four", A["w_fourier"][0])
        sa = Stream(items, [sem(f"landed_a{i}") for i in range(RING)], sem("tiles_done_a"))
        moe_first = len(items)
        moe_tiles = moe_order()
        assert len(moe_tiles) % RING == 0

        wb = A["ada_w_2"]
        ri, wu, wd = A["ret_w_in_2"][0], A["ffn_w_up_2"], A["ffn_w_down_2"]

        def conv_ffn_tiles(layer):
            tiles = []
            for j in range(FF // 256):
                tiles += [col_tile(f"cf_up{layer}", wu[layer], FF // 256 + j), col_tile(f"cf_up{layer}", wu[layer], j)]
            return tiles + row_tiles(f"cf_down{layer}", wd[layer])

        items = [col_tile("ret_qk", ri, j) for j in range(8)]
        for n in range(8):
            items += half_tiles("ret_vg", ri, 2048 + BANK * n)
        items += row_tiles("ret_out", A["ret_w_out_2"][0])
        items += conv_ffn_tiles(0)
        items += [col_tile("s5_in", A["s5_w_in_2"][0], j) for j in range(4)]
        items += row_tiles("glu", A["s5_w_glu_2"][0])
        items += conv_ffn_tiles(1)
        sbm = Stream(items, [sem(f"landed_b{i}") for i in range(RING)], sem("tiles_done_b"))

        ring = sb("ring", [P, RING, TILE])
        X = sb("X", [P, TT, D])
        H = sb("H", [P, TT, D])
        HT = sb("HT", [P, KD, SEQ])
        AD = sb("AD", [P, N_MOD * D])
        G = sb("G", [P, D])
        BB = sb("BB", [P, BANK])
        CB = sb("CB", [P, KD, P])
        ident = sb("ident", [P, P])
        ones = sb("ones", [P, P])
        vec = sb("vec", [P, 360])
        small = sb("small", [P, 160])
        small_i = sb("small_i", [P, 16], I32)
        ARENA = 22528
        arena = sb("arena", [P, ARENA])
        PS = [ctx.enter_context(nc.psum_tensor(f"bank{i}", [P, BANK], F32)) for i in range(8)]

        def at(off, *shape, parts=P):
            n = int(np.prod(shape))
            assert off + n <= ARENA
            v = arena[0:parts, off:off + n]
            names = "abcd"[:len(shape)]
            if len(shape) > 1:
                v = v.rearrange(f"p ({' '.join(names)}) -> p {' '.join(names)}",
                                **{k: s for k, s in zip(names[1:], shape[1:])})
            return v

        def slot(i):
            return ring[:, i % RING, :]

        def cols_of(i, k):
            return slot(i).rearrange("p (k n) -> p k n", k=k)

        def bank(i, a=None):
            return PS[i][:, :] if a is None else PS[i][:, :].rearrange("p (a b) -> p a b", a=a)

        def over(ap, n):
            return ap.unsqueeze(1).to_broadcast([ap.shape[0], n, ap.shape[1]])

        def along(ap, n):
            return ap.unsqueeze(2).to_broadcast([ap.shape[0], ap.shape[1], n])

        c_vec, cx_vec, c2_vec = vec[:, 0:8], vec[:, 8:16], vec[:, 16:24]
        short_w = vec[:, 24:60].rearrange("p (t m) -> p t m", t=3)
        short_b = vec[:, 60:72]
        skip = vec[:, 72:80]
        lam_re, lam_im, log_dt, s5_d = vec[:, 80:112], vec[:, 112:144], vec[:, 144:176], vec[:, 176:184]
        conv_w = [vec[:, 184 + 66 * l:250 + 66 * l].rearrange("p (t m) -> p t m", t=3) for l in range(2)]
        conv_b = [vec[:, 316 + 22 * l:338 + 22 * l] for l in range(2)]

        ss, std, rinv = small[:, 0:2], small[:, 2:4], small[:, 4:6]
        csil = small[:, 6:30]
        sk_rn = small[:, 30:38]
        rsum, rsum_inv = small[:, 38:70], small[:, 70:102]
        mx = small[:, 102:104]
        bn6 = small[:, 104:116].rearrange("p (t s) -> p t s", t=2)
        bn2 = small[:, 116:120].rearrange("p (t s) -> p t s", t=2)
        gstd, grstd = small[:, 120:122], small[:, 122:124]

        def ada_part(i):
            return AD[:, D * i:D * (i + 1)]

        ZC = at(0, HY_CHUNKS, SEQ)
        ACX = at(0, 2 * D)
        CBX = at(2 * D, KD, P)
        QT = at(3072, 4, SEQ)
        KT = at(4096, 4, SEQ)
        KCT = at(5120, 4, SEQ)
        V = at(6144, TT, CH)
        VC = at(7168, TT, CH)
        FW3 = at(3072, 4 * CH, parts=HY_HID)
        FEATS = at(5120, SEQ, parts=HY_EMB)
        FW1 = at(5376, HY_HID, parts=HY_EMB)
        FW2 = at(5440, HY_HID, parts=HY_HID)
        FV = at(5504, 4, parts=HY_HID)
        FA = [at(5632 + 256 * i, SEQ, parts=HY_HID) for i in range(5)]
        YT = at(8192, KD, SEQ)
        CX = at(8192, TT, D)
        HCT = at(8192, KD, SEQ)
        KS = at(10240, 2, 4, CH)
        DFTF = at(14336, TT, 2 * SEQ)
        IDFT = at(15360, 4, SEQ)
        FH = at(16384, TT, 4, CH)
        DFTB = at(20480, TT, 2 * SEQ)
        DEC = at(21504, TT, CH)
        BIA = [at(16384 + 1024 * i, 4, GRID_R, GRID_W) for i in range(2)]
        WIN = at(18432, GRID_W)
        NS = [at(18496 + 512 * i, 512) for i in range(2)]
        NP = [at(19520 + 512 * i, 512) for i in range(2)]
        NPT = [at(20544 + 512 * i, 4, P) for i in range(2)]
        VT = H[:, 0, :].rearrange("p (t n) -> p t n", t=TT)
        NO = H[:, 1, :].rearrange("p (t n) -> p t n", t=TT)
        YF = HT[:, :, :].rearrange("p a b -> p (a b)").rearrange("p (i n) -> p i n", i=4)
        HYT = [at(20544 + 512 * i, CH) for i in range(2)]
        XT_MIX = at(18496, BANK)
        eps = small[:, 124:125]
        HID = at(0, FF_CHUNKS, SEQ)
        SIL = [at(5632 + 512 * i, 2, SEQ) for i in range(2)]
        XT = at(6656, BANK)
        GC = [at(7168 + 512 * i, 2, SEQ) for i in range(2)]
        ADA_SLOTS, ADA_N = 3, N_MOD * D // BANK
        ADA_ACC = {1: at(10240, N_MOD * D), 2: at(16384, N_MOD * D), 3: at(16384, N_MOD * D)}
        ADA_W = {1: wa[1], 2: wb[0], 3: wb[1]}
        ADA_RING = {1: at(7168, ADA_SLOTS, 2, BANK), 2: at(7168, ADA_SLOTS, 2, BANK), 3: at(8192, ADA_SLOTS, 2, BANK)}
        ADA_HALVES = [(a, n, q) for a in (1, 2, 3) for n in range(ADA_N) for q in range(KD // 2)]

        def ada_plan(first, last):
            tiles, begin = 3 * (FF // 256), RING - 1
            return {i: begin + (i - first) * (tiles - begin) // (last - first) for i in range(first, last)}

        ADA_PLAN = {"ffn": ada_plan(0, 2 * 4 * ADA_N), "cf0": ada_plan(2 * 4 * ADA_N, 3 * 4 * ADA_N)}

        FOD = at(8192, TT, 2 * SEQ)
        FOL = at(9216, 2, TT, SEQ)
        FAB = at(10240, TT, 4, 2 * SEQ)
        FYT = at(14336, KD, SEQ)

        def bcast(row):
            return row.partition_broadcast(P)

        NORM = {n: i for i, n in enumerate(["hy", "ctx", "ffn", "four", "moe", "fin0", "ret", "cf0", "s5", "cf1", "fin1"])}
        TURN = {n: i for i, n in enumerate(["hy", "ctx", "ffn", "four", "moe", "ret", "cf0", "s5", "cf1"])}
        GB_LOADS = {n: i for i, n in enumerate(["hy", "ctx", "ffn", "four", "moe", "fin0", "fin1"])}
        RET_TILES = 2 * RET_HEADS
        HID_FFN, HID_CF = 0, [FF // 256, 2 * (FF // 256)]

        GAIN_USES = {"ctx": 1, "ffn": 2, "four": 3, "moe": 4, "fin0": 5, "fin1": 9}
        MO = 0
        XG = at(0, KD, P)
        PM = at(1024, TT, P)
        PG = at(1280, TT, P)
        PGT = at(1536, SEQ)
        MS = [at(1792 + 512 * i, BANK) for i in range(2)]
        MH = [at(2816 + 512 * i, BANK) for i in range(2)]
        MHT = [at(3840 + 512 * i, 4, P) for i in range(2)]
        YE = at(4864, D)
        ACC = at(5888, TT, D)
        WR = at(7936, KD, EXPERTS)
        BR8 = at(8000, EXPERTS)
        IOTA = at(8008, P)
        BEFORE = at(8136, P)
        LG = at(8264, TT, EXPERTS)
        M8 = at(8280, TT, EXPERTS)
        IDX = at(8296, TT, EXPERTS).bitcast(U32)
        IDXF = at(8312, TT, EXPERTS)
        OH = [at(8328 + 16 * i, TT, EXPERTS) for i in range(2)]
        MASK = at(8360, TT, EXPERTS)
        MSUM = at(8376, EXPERTS)
        PW = at(8384, 6, TT)
        EXTRA = SEQ * 2 // (P + 1)
        NX = EXPERTS + EXTRA + 1
        SLOT = at(8400, TT, NX)
        GATE = at(8424, TT, NX)
        CUR = at(8448, 4)
        GT1 = at(8452, TT, EXPERTS)
        OVER, OVER_N, OVER_J, OVER_T = (at(8468 + 8 * i, EXPERTS) for i in range(4))
        EIDF = at(8500, NX)
        NT = len(moe_tiles)
        tile_at = {t: i for i, t in enumerate(moe_tiles)}

        def rounds(eng):
            eng.wait_ge(sem("rounds_ready"), 1)
            return eng.value_load(small_i[0:1, NX:NX + 1], min_val=EXPERTS, max_val=EXPERTS + EXTRA)

        def landed_wait(pe, g, i):
            j = moe_first + i
            pe.wait_ge(sa.landed[j % RING], g * (16 * NT // RING) + 16 * (j // RING + 1))

        def done_wait(eng, g, i):
            eng.wait_ge(sa.done, g * NT + (moe_first + i + 1))

        def moe_sync(sp):
            w1 = A["moe_w1"][0].rearrange("e r n -> (e r) n")
            w3 = A["moe_w3"][0].rearrange("e r n -> (e r) n")
            w2 = A["moe_w2"][0].rearrange("e r n -> (e r) n")
            n = rounds(sp)
            with sp.Fori(0, n) as g:
                e = sp.value_load(small_i[0:1, bass.ds(g, 1)], min_val=0, max_val=EXPERTS - 1)
                for i, (kind, c, h) in enumerate(moe_tiles):
                    sp.wait_ge(sa.done, g * NT + (moe_first + i - RING + 1))
                    if kind == "w2":
                        src = w2[bass.ds(e * FFE + (BANK * c + 256 * h), 256), :]
                    else:
                        src = (w1 if kind == "w1" else w3)[bass.ds(e * D + BANK * h, BANK), BANK * c:BANK * (c + 1)]
                    k = 2 if kind == "w2" else 4
                    j = moe_first + i
                    sp.dma_start(cols_of(j, k), src.rearrange("(k p) n -> p k n", p=P)).then_inc(sa.landed[j % RING], 16)

        def moe_pool(pool, gain):
            pool.wait_ge(sem("x_ready"), 3)
            pool.dma_start(WR, A["w_router"]).then_inc(sem("route_landed"), 16)
            pool.dma_start(BR8, bcast(A["b_router"][0])).then_inc(sem("route_landed"), 16)
            pool.dma_start(IOTA, A["t_iota"]).then_inc(sem("route_landed"), 16)
            pool.dma_start(BEFORE, A["t_before"]).then_inc(sem("route_landed"), 16)
            gain("moe", A["norm_g"][1, 1])
            gain("fin0", A["final_g"])

        def moe_tensor(pe):
            pe.wait_ge(sem("route_landed"), 64)
            for t in range(TT):
                for k in range(KD):
                    mm = pe.matmul(PS[0][:, 8 * t:8 * t + 8], HT[:, k, P * t:P * t + P], WR[:, k, :], start=k == 0, stop=k == KD - 1)
            mm.then_inc(sem("logits_done"), 1)
            pe.wait_ge(sem("mask_ready"), 1)
            pe.matmul(PS[1][:, 0:8], BEFORE, MASK[:, 0, :], start=True, stop=True)
            pe.matmul(PS[1][:, 8:16], BEFORE, MASK[:, 1, :], start=True, stop=False)
            pe.matmul(PS[1][:, 8:16], ones[:, :], MASK[:, 0, :], start=False, stop=True)
            pe.matmul(PS[1][:, 16:24], ones[:, :], MSUM, start=True, stop=True).then_inc(sem("count_done"), 1)

            def gather():
                for k in range(KD):
                    for t in range(TT):
                        mm = pe.matmul(PS[5 + k // 4][:, P * (k % 4):P * (k % 4) + P], H[:, t, P * k:P * k + P], PM[:, t, :],
                                       start=t == 0, stop=t == TT - 1)
                mm.then_inc(sem("gather_done"), 1)
                for t in range(TT):
                    mm = pe.transpose(PS[7][:, P * t:P * t + P], PG[:, t, :], ident[:, :])
                mm.then_inc(sem("gate_turned"), 1)

            pe.wait_ge(sem("pick_ready"), 2)
            gather()
            n = rounds(pe)
            with pe.Fori(0, n) as g:
                for c in range(MOE_CHUNKS + 1):
                    if c == 0:
                        pe.wait_ge(sem("xg_ready"), g + 1)
                        pe.wait_ge(sem("xg_ready_d"), g + 1)
                        pe.wait_ge(sem("pgt_ready"), g + 1)
                    if c < MOE_CHUNKS:
                        for h in range(2):
                            i = tile_at["w1", c, h]
                            landed_wait(pe, g, i)
                            if c and h == 0:
                                pe.wait_ge(sem("moe_silu"), g * MOE_CHUNKS + c)
                            w = cols_of(moe_first + i, 4)
                            for k in range(4):
                                mm = pe.matmul(bank(0), XG[:, 4 * h + k, :], w[:, k, :], start=h + k == 0, stop=h == 1 and k == 3)
                            mm.then_inc(sa.done, 1)
                    if c >= 1:
                        pe.wait_ge(sem("moe_hid"), g * MOE_CHUNKS + c)
                        if c >= 2:
                            pe.wait_ge(sem("moe_hidT"), g * MOE_CHUNKS + (c - 1))
                        for q in range(4):
                            mm = pe.transpose(PS[2][:, P * q:P * q + P], MH[(c - 1) % 2][:, P * q:P * q + P], ident[:, :])
                        mm.then_inc(sem("moe_turned"), 1)
                    if c < MOE_CHUNKS:
                        for h in range(2):
                            i = tile_at["w3", c, h]
                            landed_wait(pe, g, i)
                            w = cols_of(moe_first + i, 4)
                            for k in range(4):
                                mm = pe.matmul(bank(1), XG[:, 4 * h + k, :], w[:, k, :], start=h + k == 0, stop=h == 1 and k == 3)
                            mm.then_inc(sa.done, 1)
                    if c == MOE_CHUNKS - 1:
                        pe.wait_ge(sem("pick_ready"), g * 2 + 4)
                        gather()
                    if c >= 1:
                        pe.wait_ge(sem("moe_hidT"), g * MOE_CHUNKS + c)
                        for h in range(2):
                            i = tile_at["w2", c - 1, h]
                            landed_wait(pe, g, i)
                            w = cols_of(moe_first + i, 2)
                            for k in range(2):
                                for nn in range(2):
                                    mm = pe.matmul(bank(3 + nn), MHT[(c - 1) % 2][:, 2 * h + k, :], w[:, k, BANK * nn:BANK * nn + BANK],
                                                   start=c == 1 and h + k == 0, stop=c == MOE_CHUNKS and h + k == 2)
                            mm.then_inc(sa.done, 1)
                pe.wait_ge(sem("ye_act"), g + 1)
                pe.wait_ge(sem("ye_dve"), g + 1)
                for t in range(TT):
                    for nn in range(2):
                        b = 2 * t + nn
                        mm = pe.matmul(bank(b), PGT[:, P * t:P * t + P], YE[:, BANK * nn:BANK * nn + BANK], start=True, stop=True)
                mm.then_inc(sem("scattered"), 1)
                pe.wait_ge(sem("acc_added"), g + 1)
            pe.matmul(PS[0][:, 0:1], ident[:, :], ones[:, 0:1], start=True, stop=True).then_inc(sem("moe_scattered"), 1)

        def moe_scalar(act, ch):
            act.wait_ge(sem("top_ready"), 1)
            for t in range(TT):
                ch.step(act.activation(PW[:, 1, t:t + 1], M8[:, t, 1:2], ACT.Exp, bias=PW[:, 0, t:t + 1]), sem("pair_exp"))
            act.wait_ge(sem("gather_done"), 1)
            act.activation(XG[:, 0:4, :], bank(5, 4), ACT.Copy).then_inc(sem("xg_ready"), 1)
            n = rounds(act)
            with act.Fori(0, n) as g:
                for c in range(MOE_CHUNKS):
                    done_wait(act, g, tile_at["w1", c, 1])
                    if c >= 2:
                        act.wait_ge(sem("moe_hid"), g * MOE_CHUNKS + (c - 1))
                    act.activation(MS[c % 2], bank(0), ACT.Silu).then_inc(sem("moe_silu"), 1)
                    if c >= 1:
                        hid_turn(act, g, c - 1)
                done_wait(act, g, tile_at["w3", MOE_CHUNKS - 1, 1])
                act.wait_ge(sem("gather_done"), g + 2)
                act.activation(XG[:, 0:4, :], bank(5, 4), ACT.Copy).then_inc(sem("xg_ready"), 1)
                hid_turn(act, g, MOE_CHUNKS - 1)
                done_wait(act, g, tile_at["w2", MOE_CHUNKS - 1, 1])
                act.activation(YE[:, 0:BANK], bank(3), ACT.Copy).then_inc(sem("ye_act"), 1)

        def hid_turn(act, g, c):
            act.wait_ge(sem("moe_turned"), g * MOE_CHUNKS + (c + 1))
            if c >= 2:
                done_wait(act, g, tile_at["w2", c - 2, 1])
            act.activation(MHT[c % 2], bank(2, 4), ACT.Copy).then_inc(sem("moe_hidT"), 1)

        def moe_vector(dve, ch):
            link = ch.link
            dve.wait_ge(sem("logits_done"), 1)
            dve.wait_ge(sem("route_landed"), 64)
            for t in range(TT):
                link(dve.tensor_tensor(out=LG[:, t, :], in0=PS[0][:, 8 * t:8 * t + 8], in1=BR8, op=ALU.add))
                link(dve.max(M8[:, t, :], LG[:, t, :]))
                link(dve.max_index(IDX[:, t, :], M8[:, t, :], LG[:, t, :]))
                link(dve.tensor_copy(IDXF[:, t, :], IDX[:, t, :]))
                for j in range(2):
                    link(dve.tensor_scalar(OH[j][:, t, :], IOTA[:, 0:EXPERTS], IDXF[:, t, j:j + 1], None, ALU.is_equal))
            link(dve.tensor_scalar(PW[:, 0, :], M8[:, :, 0], -1.0, None, ALU.mult), sem("top_ready"))
            link(dve.tensor_tensor(out=MASK, in0=OH[0], in1=OH[1], op=ALU.add))
            link(dve.tensor_tensor(out=MSUM, in0=MASK[:, 0, :], in1=MASK[:, 1, :], op=ALU.add), sem("mask_ready"))
            dve.wait_ge(sem("pair_exp"), 2)
            link(dve.tensor_scalar(PW[:, 2, :], PW[:, 1, :], 1.0, None, ALU.add))
            link(dve.reciprocal(PW[:, 3, :], PW[:, 2, :]))
            link(dve.tensor_tensor(out=PW[:, 4, :], in0=PW[:, 3, :], in1=PW[:, 1, :], op=ALU.mult))
            for t in range(TT):
                link(dve.tensor_scalar(GT1[:, t, :], OH[0][:, t, :], PW[:, 3, t:t + 1], None, ALU.mult))
                link(dve.scalar_tensor_tensor(out=GATE[:, t, 0:EXPERTS], in0=OH[1][:, t, :],
                                              scalar=PW[:, 4, t:t + 1], in1=GT1[:, t, :], op0=ALU.mult, op1=ALU.add))
            link(dve.memset(GATE[:, :, NX - 1:NX], 0.0))
            link(dve.memset(SLOT[:, :, NX - 1:NX], -1.0))
            link(dve.memset(ACC, 0.0))
            dve.wait_ge(sem("count_done"), 1)
            for t in range(TT):
                link(dve.scalar_tensor_tensor(out=SLOT[:, t, 0:EXPERTS], in0=PS[1][:, 8 * t:8 * t + 8], scalar=1.0, in1=MASK[:, t, :],
                                              op0=ALU.add, op1=ALU.mult))
                link(dve.tensor_scalar(SLOT[:, t, 0:EXPERTS], SLOT[:, t, 0:EXPERTS], -1.0, None, ALU.add))
            link(dve.tensor_scalar(OVER, PS[1][:, 16:24], P + 0.5, None, ALU.is_gt))
            link(dve.tensor_tensor_scan(OVER_N, ones[:, 0:EXPERTS], OVER, 0.0, ALU.mult, ALU.add))
            link(dve.tensor_copy(EIDF[:, 0:EXPERTS], IOTA[:, 0:EXPERTS]))
            for j in range(EXTRA):
                r = EXPERTS + j
                link(dve.scalar_tensor_tensor(out=OVER_J, in0=OVER_N, scalar=float(j + 1), in1=OVER, op0=ALU.is_equal, op1=ALU.mult))
                link(dve.tensor_tensor(out=OVER_T, in0=OVER_J, in1=IOTA[:, 0:EXPERTS], op=ALU.mult))
                link(dve.tensor_reduce(EIDF[:, r:r + 1], OVER_T, AX.X, ALU.add))
                for t in range(TT):
                    link(dve.scalar_tensor_tensor(out=OVER_T, in0=SLOT[:, t, 0:EXPERTS], scalar=float(1 - P), in1=OVER_J,
                                                  op0=ALU.add, op1=ALU.mult))
                    link(dve.tensor_reduce(SLOT[:, t, r:r + 1], OVER_T, AX.X, ALU.add))
                    link(dve.tensor_scalar(SLOT[:, t, r:r + 1], SLOT[:, t, r:r + 1], -1.0, None, ALU.add))
                    link(dve.tensor_tensor(out=OVER_T, in0=GATE[:, t, 0:EXPERTS], in1=OVER_J, op=ALU.mult))
                    link(dve.tensor_reduce(GATE[:, t, r:r + 1], OVER_T, AX.X, ALU.add))
            link(dve.tensor_scalar(EIDF[:, NX - 1:NX], OVER_N[:, EXPERTS - 1:EXPERTS], float(EXPERTS), None, ALU.add))
            link(dve.tensor_copy(small_i[:, 0:NX - 1], EIDF[:, 0:NX - 1]))
            link(dve.tensor_copy(small_i[:, NX:NX + 1], EIDF[:, NX - 1:NX]), sem("rounds_ready"))

            def pick(lk, col):
                for t in range(TT):
                    lk(dve.tensor_copy(CUR[:, t:t + 1], SLOT[:, t, col]))
                    lk(dve.tensor_copy(CUR[:, 2 + t:3 + t], GATE[:, t, col]))
                for t in range(TT):
                    lk(dve.tensor_scalar(PG[:, t, :], IOTA, CUR[:, t:t + 1], CUR[:, 2 + t:3 + t], ALU.is_equal, ALU.mult))
                    dve.tensor_scalar(PM[:, t, :], IOTA, CUR[:, t:t + 1], None, ALU.is_equal).then_inc(sem("pick_ready"), 1)

            pick(link, slice(0, 1))
            dve.wait_ge(sem("gather_done"), 1)
            dve.tensor_copy(XG[:, 4:8, :], bank(6, 4)).then_inc(sem("xg_ready_d"), 1)
            dve.wait_ge(sem("gate_turned"), 1)
            dve.tensor_copy(PGT, PS[7][:, 0:SEQ]).then_inc(sem("pgt_ready"), 1)
            n = rounds(dve)
            with dve.Fori(0, n) as g:
                lc = LoopChain(dve, sem("moe_chain"), g, 6)
                for c in range(MOE_CHUNKS):
                    done_wait(dve, g, tile_at["w3", c, 1])
                    dve.wait_ge(sem("moe_silu"), g * MOE_CHUNKS + (c + 1))
                    if c >= 2:
                        dve.wait_ge(sem("moe_turned"), g * MOE_CHUNKS + (c - 1))
                    dve.tensor_tensor(out=MH[c % 2], in0=MS[c % 2], in1=bank(1), op=ALU.mult).then_inc(sem("moe_hid"), 1)
                    if c == 0:
                        dve.wait_ge(sem("gate_turned"), g + 1)
                        pick(lc.link, bass.ds(g + 1, 1))
                dve.wait_ge(sem("gather_done"), g + 2)
                dve.tensor_copy(XG[:, 4:8, :], bank(6, 4)).then_inc(sem("xg_ready_d"), 1)
                done_wait(dve, g, tile_at["w2", MOE_CHUNKS - 1, 1])
                dve.tensor_copy(YE[:, BANK:D], bank(4)).then_inc(sem("ye_dve"), 1)
                dve.wait_ge(sem("scattered"), g + 1)
                for t in range(TT):
                    for nn in range(2):
                        a = ACC[:, t, BANK * nn:BANK * nn + BANK]
                        ins = dve.tensor_tensor(out=a, in0=a, in1=bank(2 * t + nn), op=ALU.add)
                ins.then_inc(sem("acc_added"), 1)
                dve.wait_ge(sem("gate_turned"), g + 2)
                dve.tensor_copy(PGT, PS[7][:, 0:SEQ]).then_inc(sem("pgt_ready"), 1)
            dve.wait_ge(sem("moe_scattered"), 1)
            for t in range(TT):
                link(dve.tensor_tensor(out=ACC[:, t, :], in0=ACC[:, t, :], in1=ada_part(5), op=ALU.mult))
                link(dve.tensor_tensor(out=X[:, t, :], in0=X[:, t, :], in1=ACC[:, t, :], op=ALU.add), sem("moe_x"))

        RT = at(0, RET_HEADS, 384)
        RCOS, RSIN = at(1536, SEQ), at(1792, SEQ)
        RM = [at(2048 + 512 * i, 2, SEQ) for i in range(2)]
        QR = at(3072, 2 * RET_HEADS, SEQ)
        KR = at(5120, 2 * RET_HEADS, SEQ)
        RV = at(7168, TT, RET_HEADS, RET_DV)
        SG = at(11264, TT, RET_HEADS, RET_DV)
        RS = [at(15360 + 384 * i, 384) for i in range(2)]
        RON = at(16128, BANK)
        OTT = at(16640, 4 * RET_HEADS, SEQ)
        RPOS = at(7168, SEQ).bitcast(I32)
        RANG = [at(7424 + 256 * i, SEQ) for i in range(4)]
        INVF = at(8448, 1)
        RXT = at(2048, BANK)

        UT = at(0, KD, SEQ)
        SBR, SBI = at(2048, KD, P), at(3072, KD, P)
        SCR, SCI = at(4096, S5_TILES, 32), at(5120, S5_TILES, 32)
        CFR, CFI = at(6144, S5_TILES, 32), at(7168, S5_TILES, 32)
        STMP = at(8192, S5_TILES, 32)
        SP = at(9216, 16, S5_TILES)
        EK = at(9728, 2, 9, S5_TILES)
        EA = at(10304, 4, 9, S5_TILES)
        TC, TS = at(11456, 8, SEQ), at(13504, 8, SEQ)
        TQ = [at(15552 + 1024 * i, 8, 128) for i in range(2)]
        SM = [at(17600 + 512 * i, 2, SEQ) for i in range(2)]
        SV = at(18624, 2, SEQ)
        SW = [at(19136 + 512 * i, 2, SEQ) for i in range(2)]
        SQ = [at(15552 + 512 * i, 2, SEQ) for i in range(2)]
        SS = [at(20160 + 512 * i, 2, SEQ) for i in range(2)]
        YG = at(21184, 1)
        S5Y = HT
        SU = at(8192, SEQ)
        GLS = at(4096, BANK)
        GLT = at(4608, BANK)

        def b2_pool(pool, ch, gain, ada_bias):
            pool.wait_ge(sem("x_ready"), 4)
            pool.dma_start(RT, A["t_ret"]).then_inc(sem("ret_landed"), 16)
            pool.dma_start(INVF, A["t_inv_freq"]).then_inc(sem("ret_landed"), 16)
            pool.dma_start(RPOS, bcast(A["pos_2"][0])).then_inc(sem("ret_landed"), 16)
            ada_bias(2, A["ada_b_2"][0])
            if STOP >= 7:
                ada_bias(3, A["ada_b_2"][1])
                pool.wait_ge(sem("x_ready"), 6)
                pool.dma_start(SBR, A["s5_b_re"]).then_inc(sem("s5_landed"), 16)
                pool.dma_start(SBI, A["s5_b_im"]).then_inc(sem("s5_landed"), 16)
                pool.dma_start(SCR, A["s5_c_re"]).then_inc(sem("s5_landed"), 16)
                pool.dma_start(SCI, A["s5_c_im"]).then_inc(sem("s5_landed"), 16)
                for j in range(S5_TILES):
                    q = j % 8
                    b = j % 2
                    pool.wait_ge(sem("s5_w"), j + 1)
                    if j >= 2:
                        pool.wait_ge(sem("s5_y"), j - 1)
                    ch.link(pool.tensor_tensor(out=SQ[0], in0=SW[b], in1=over(TC[:, q, :], 2), op=ALU.mult))
                    ch.link(pool.tensor_tensor(out=SQ[1], in0=SW[b], in1=over(TS[:, q, :], 2), op=ALU.mult))
                    pool.tensor_tensor(out=SS[b][:, 0, :], in0=SQ[0][:, 0, :], in1=SQ[1][:, 1, :], op=ALU.subtract)
                    ch.link(pool.tensor_tensor(out=SS[b][:, 1, :], in0=SQ[1][:, 0, :], in1=SQ[0][:, 1, :], op=ALU.add), sem("s5_s"))
            if STOP >= 8:
                gain("fin1", A["final_norm_g_2"])

        def ret_turn_evac(act, ch, h):
            for t in range(TT):
                act.wait_ge(sem("ret_turned"), 2 * h + t + 1)
                ch.step(act.activation(OTT[:, 4 * h:4 * h + 4, P * t:P * t + P], bank(4 + t, 4), ACT.Copy), sem("ott_ready"))


        def s5_vector(dve, ch, tt, ts, stt, to_period, scale_shift, turn_evac, ada_evac):
            link = ch.link
            dt, th, lrdt, mag, ar, ai, nr, den, fr, fi, t0, t1 = (SP[:, i, :] for i in range(12))
            dve.wait_ge(sem("s5_dt"), 1)
            tt(th, lam_im, dt, ALU.mult)
            tt(lrdt, lam_re, dt, ALU.mult)
            to_period(EA[:, 0, 0, :], th, t0, 0, None)
            for k in range(1, 9):
                ts(EA[:, 0, k, :], EA[:, 0, 0, :], float(2 ** k), None, ALU.mult)
            to_period(EA[:, 2], EA[:, 0], EA[:, 1], 0, None)
            to_period(EA[:, 3], EA[:, 0], EA[:, 1], 1, sem("s5_arg"))
            ada_evac(3)
            scale_shift("s5", X, "scale", ada_part(0), ada_part(1))
            turn_evac("s5", HT)
            dve.wait_ge(sem("s5_trig"), 3)
            tt(ar, mag, EK[:, 0, 0, :], ALU.mult)
            tt(ai, mag, EK[:, 1, 0, :], ALU.mult)
            ts(nr, ar, -1.0, None, ALU.add)
            tt(den, lam_re, lam_re, ALU.mult)
            tt(t0, lam_im, lam_im, ALU.mult)
            tt(den, den, t0, ALU.add)
            link(dve.reciprocal(den, den))
            tt(t0, nr, lam_re, ALU.mult)
            tt(t1, ai, lam_im, ALU.mult)
            tt(fr, t0, t1, ALU.add)
            tt(fr, fr, den, ALU.mult)
            tt(t0, ai, lam_re, ALU.mult)
            tt(t1, nr, lam_im, ALU.mult)
            tt(fi, t0, t1, ALU.subtract)
            tt(fi, fi, den, ALU.mult)
            dve.wait_ge(sem("s5_landed"), 64)
            tt(CFR, SCR, along(fr, 32), ALU.mult)
            tt(STMP, SCI, along(fi, 32), ALU.mult)
            tt(CFR, CFR, STMP, ALU.subtract, sem("s5_c"))
            tt(CFI, SCR, along(fi, 32), ALU.mult)
            tt(STMP, SCI, along(fr, 32), ALU.mult)
            stt(CFI, CFI, -1.0, STMP, ALU.mult, ALU.subtract, sem("s5_c"))
            for j in range(S5_TILES):
                q = j % 8
                if q == 0:
                    if j:
                        dve.wait_ge(sem("s5_s"), j)
                    link(dve.memset(TC[:, :, 0:1], 1.0))
                    link(dve.memset(TS[:, :, 0:1], 0.0))
                    for k in range(8):
                        n = 2 ** k
                        ck, sk = EK[:, 0, k, j:j + 8], EK[:, 1, k, j:j + 8]
                        a, b = TQ[0][:, :, 0:n], TQ[1][:, :, 0:n]
                        tt(a, TS[:, :, 0:n], along(sk, n), ALU.mult)
                        tt(b, TC[:, :, 0:n], along(ck, n), ALU.mult)
                        tt(TC[:, :, n:2 * n], b, a, ALU.subtract)
                        tt(a, TC[:, :, 0:n], along(sk, n), ALU.mult)
                        tt(b, TS[:, :, 0:n], along(ck, n), ALU.mult)
                        tt(TS[:, :, n:2 * n], b, a, ALU.add)
                dve.wait_ge(sem("s5_bu"), j + 1)
                tt(SM[0], bank(j % 2, 2), over(TC[:, q, :], 2), ALU.mult)
                tt(SM[1], bank(j % 2, 2), over(TS[:, q, :], 2), ALU.mult, sem("s5_rot"))
                tt(SV[:, 0, :], SM[0][:, 0, :], SM[1][:, 1, :], ALU.add)
                tt(SV[:, 1, :], SM[0][:, 1, :], SM[1][:, 0, :], ALU.subtract)
                if j >= 2:
                    dve.wait_ge(sem("s5_s"), j - 1)
                for s in range(2):
                    link(dve.tensor_tensor_scan(SW[j % 2][:, s, :], mag[:, j:j + 1].to_broadcast([P, SEQ]), SV[:, s, :], 0.0,
                                                ALU.mult, ALU.add), sem("s5_w") if s else None)
                if j % 4 == 3:
                    k = j // 4
                    dve.wait_ge(sem("s5_y"), j + 1)
                    if k:
                        dve.wait_ge(sem("s5_gelu"), k)
                    stt(SU, UT[:, k, :], s5_d[:, k:k + 1], PS[2 + k % 2][:, 0:SEQ], ALU.mult, ALU.add, sem("s5_du"))
            for t in range(TT):
                for n in range(2):
                    c = slice(BANK * n, BANK * n + BANK)
                    dve.wait_ge(sem("glu_sig"), 2 * t + n + 1)
                    tt(GLT, bank(4 * t + n), GLS, ALU.mult, sem("glu_used"))
                    tt(GLT, GLT, AD[:, 2 * D + BANK * n:2 * D + BANK * n + BANK], ALU.mult)
                    tt(X[:, t, c], X[:, t, c], GLT, ALU.add, sem("x_ready") if t + n == 2 else None)
        block = ctx.enter_context(nc.Block())

        @block.sync
        def _(sp):
            def load(st, i, after=None):
                if i >= RING:
                    sp.wait_ge(st.done, i - RING + 1)
                name, src, k = st.items[i]
                sp.dma_start(slot(i).rearrange("p (k n) -> p k n", k=k),
                             src.rearrange("(k p) n -> p k n", p=P)).then_inc(st.landed[i % RING], 16)

            na = len(sa.items) if STOP >= 4 else min(len(sa.items), {1: sa.first["ffn_up"], 2: sa.first["four"], 3: moe_first}[STOP])
            def load_ada(i):
                a, n, q = ADA_HALVES[i]
                if i >= ADA_SLOTS:
                    sp.wait_ge(sem("ada_added"), i - ADA_SLOTS + 1)
                sp.dma_start(ADA_RING[a][:, i % ADA_SLOTS],
                             ADA_W[a][256 * q:256 * (q + 1), BANK * n:BANK * (n + 1)].rearrange("(k p) n -> p k n", p=P))\
                    .then_inc(sem(f"ada_landed{i % ADA_SLOTS}"), 16)

            def load_with_ada(st, i, base, plan, x_count):
                load(st, i)
                halves = [k for k, after in plan.items() if after == i - base]
                if halves and i - base == RING - 1:
                    sp.wait_ge(sem("x_ready"), x_count)
                for k in halves:
                    load_ada(k)

            ffn_tiles = range(sa.first["ffn_up"], sa.first["four"])
            for i in range(na):
                if i in ffn_tiles:
                    load_with_ada(sa, i, ffn_tiles[0], ADA_PLAN["ffn"], 1)
                else:
                    load(sa, i)
            if STOP >= 4:
                moe_sync(sp)
                sp.wait_ge(sem("moe_scattered"), 1)
                nb = {4: 0, 5: sbm.first["cf_up0"], 6: sbm.first["s5_in"], 7: sbm.first["cf_up1"]}.get(STOP, len(sbm.items))
                cf_tiles = range(sbm.first["cf_up0"], sbm.first["s5_in"])
                for i in range(nb):
                    if i in cf_tiles:
                        load_with_ada(sbm, i, cf_tiles[0], ADA_PLAN["cf0"], 5)
                    else:
                        load(sbm, i)
            sp.wait_ge(sem("out_ready"), 1)
            sp.dma_start(out.rearrange("b (t p) d -> p (b t) d", p=P), H[:, :, :]).then_inc(sem("stored"), 16)
            sp.wait_ge(sem("stored"), 16)

        @block.gpsimd
        def _(pool):
            ch = Chain(pool, sem("pool_chain"))
            pool.dma_start(vec[:, :], A["vectors"]).then_inc(sem("vec_landed"), 16)
            pool.dma_start(FW1, A["hy_f_w1"][0]).then_inc(sem("filter_landed"), 16)
            pool.dma_start(FEATS, A["t_feats"]).then_inc(sem("filter_landed"), 16)
            pool.dma_start(FW2, A["hy_f_w2"][0]).then_inc(sem("filter_landed"), 16)
            pool.dma_start(FV, A["filter_vectors"]).then_inc(sem("filter_landed"), 16)
            pool.dma_start(FW3, A["hy_f_w3"][0]).then_inc(sem("filter_landed"), 16)
            pool.dma_start(DEC, A["t_decay"]).then_inc(sem("filter_landed"), 16)
            pool.dma_start(DFTF, A["t_dft_fwd"]).then_inc(sem("filter_landed"), 16)
            pool.dma_start(DFTB, A["t_dft_bwd"]).then_inc(sem("filter_landed"), 16)
            pool.dma_start(IDFT, A["t_idft"]).then_inc(sem("filter_landed"), 16)
            pool.dma_start(ident[:, :], A["t_ident"]).then_inc(sem("ident_landed"), 16)
            pool.dma_start(X[:, :, :], A["x"][0].rearrange("(t p) d -> p t d", p=P)).then_inc(sem("x_landed"), 16)
            pool.dma_start(CX, A["ctx"][0].rearrange("(t p) d -> p t d", p=P)).then_inc(sem("ctx_landed"), 16)
            pool.memset(ones[:, :], 1.0).then_inc(sem("ones_set"), 1)

            def gain(name, row):
                i = GB_LOADS[name]
                if i:
                    pool.wait_ge(sem("gain_used"), GAIN_USES[name])
                pool.dma_start(G[:, :], bcast(row)).then_inc(sem("gain_landed"), 16)

            def ada_bias(a, row):
                for n in range(N_MOD * D // BANK):
                    m = N_MOD * D // BANK * a + n
                    if m:
                        pool.wait_ge(sem("ada_evac"), m)
                    pool.dma_start(BB[:, :], bcast(row[BANK * n:BANK * (n + 1)])).then_inc(sem("bias_landed"), 16)

            gain("hy", A["norm_g"][0, 0])
            ada_bias(0, A["b_ada"][0])
            gain("ctx", A["norm_g"][0, 0])
            pool.wait_ge(sem("ks_ready"), 8)
            pool.dma_start(WIN, A["t_window"]).then_inc(sem("win_landed"), 16)
            for gi in range(8):
                t, h0 = gi // 4, 4 * (gi % 4)
                if gi >= 2:
                    pool.wait_ge(sem("na_max"), 4 * (gi - 1))
                for rr in range(2):
                    for h in range(4):
                        off = ((h0 + h) * RPB_R + WIN_R - 1 - (2 * t + rr)) * RPB_C + WIN_C - GRID_W
                        src = bass.AP(A["na_rpb"].tensor, off, [[1, GRID_W], [RPB_C, GRID_R], [1, GRID_W]])
                        pool.dma_start(BIA[gi % 2][64 * rr:64 * rr + 64, h], src).then_inc(sem(f"rpb_landed{gi % 2}"), 16)
                if gi == 0:
                    pool.wait_ge(sem("win_landed"), 16)
                pool.wait_ge(sem(f"rpb_landed{gi % 2}"), 128 * (gi // 2 + 1))
                b = BIA[gi % 2].rearrange("p h r k -> p (h r) k")
                pool.tensor_tensor(out=b, in0=b, in1=over(WIN, 4 * GRID_R), op=ALU.add).then_inc(sem("rpb_ready"), 1)
            if STOP >= 2:
                gain("ffn", A["norm_g"][0, 1])
            if STOP >= 3:
                ada_bias(1, A["b_ada"][1])
                gain("four", A["norm_g"][1, 0])
                pool.wait_ge(sem("x_ready"), 2)
                pool.dma_start(FOD, A["t_four_d"]).then_inc(sem("four_landed"), 16)
                pool.dma_start(FOL, A["t_four_l"]).then_inc(sem("four_landed"), 16)
            if STOP >= 4:
                moe_pool(pool, gain)
            if STOP >= 5:
                b2_pool(pool, ch, gain, ada_bias)


        @block.tensor
        def _(pe):
            def turn(name):
                i = TURN[name]
                for t in range(TT):
                    pe.wait_ge(sem("norm_h"), 2 * i + t + 1)
                    for half in range(2):
                        for q in range(4):
                            k = 4 * half + q
                            mm = pe.transpose(PS[2 * t + half][:, P * q:P * q + P], H[:, t, P * k:P * k + P], ident[:, :])
                        mm.then_inc(sem("norm_turned"), 1)

            def turned(name):
                i = TURN[name]
                pe.wait_ge(sem("ht_act"), 2 * (i + 1))
                pe.wait_ge(sem("ht_dve"), 2 * (i + 1))

            def ada(a, st):
                base = st.first[f"ada{a}"]
                pe.wait_ge(sem("cb_ready"), 2)
                for n in range(N_MOD * D // BANK):
                    m = N_MOD * D // BANK * a + n
                    if n >= 2:
                        pe.wait_ge(sem("ada_evac"), m - 1)
                    for h in range(2):
                        i = base + 2 * n + h
                        st.need(pe, i)
                        w = cols_of(i, 4)
                        if a == 0 and n < 4:
                            for k in range(4):
                                pe.matmul(bank(2 + n % 2), CBX[:, 4 * h + k, :], w[:, k, :], start=h + k == 0, stop=h == 1 and k == 3)
                        for k in range(4):
                            mm = pe.matmul(bank(n % 2), CB[:, 4 * h + k, :], w[:, k, :], start=h + k == 0, stop=h == 1 and k == 3)
                        mm.then_inc(st.done, 1)

            def ada_sum(a):
                pe.wait_ge(sem("ada_added"), 4 * ADA_N * a)
                for n in range(ADA_N):
                    m = ADA_N * a + n
                    if n >= 2:
                        pe.wait_ge(sem("ada_evac"), m - 1)
                    pe.matmul(bank(n % 2), ones[:, :], ADA_ACC[a][:, BANK * n:BANK * (n + 1)], start=True, stop=True)\
                        .then_inc(sem("ada_summed"), 1)

            def columns(st, i, b, src):
                w = cols_of(i, 8)
                for m in range(2):
                    for k in range(KD):
                        mm = pe.matmul(PS[b][:, SEQ * m:SEQ * m + SEQ], w[:, k, P * m:P * m + P], src[:, k, :],
                                       start=k == 0, stop=k == KD - 1)
                return mm

            def rows_out(st, name, lhs, tiles, wait=None):
                base = st.first[name]
                for j in range(tiles):
                    if wait:
                        wait(j)
                    i = base + j
                    st.need(pe, i)
                    w = cols_of(i, 2)
                    for k in range(2):
                        for t in range(TT):
                            for n in range(2):
                                mm = pe.matmul(bank(4 + 2 * t + n), lhs(2 * j + k)[:, P * t:P * t + P], w[:, k, BANK * n:BANK * n + BANK],
                                               start=j + k == 0, stop=j == tiles - 1 and k == 1)
                    mm.then_inc(st.done, 1)

            def gated_ffn(st, up, down, hid_base):
                base = st.first[up]
                for j in range(FF // 256):
                    if j >= 2:
                        pe.wait_ge(sem("hid_ready"), hid_base + j - 1)
                    for s in range(2):
                        i = base + 2 * j + s
                        st.need(pe, i)
                        columns(st, i, 2 * (j % 2) + s, HT).then_inc(st.done, 1)
                rows_out(st, down, lambda k: HID[:, k, :], FF // 256,
                         lambda j: pe.wait_ge(sem("hid_ready"), hid_base + j + 1))

            pe.wait_ge(sem("filter_landed"), 144)
            pe.matmul(PS[0][0:HY_HID, 0:SEQ], FW1, FEATS, start=True, stop=True).then_inc(sem("filter_h"), 1)
            pe.wait_ge(sem("filter_sin"), 1)
            pe.matmul(PS[1][0:HY_HID, 0:SEQ], FW2, FA[3], start=True, stop=True).then_inc(sem("filter_h"), 1)
            pe.wait_ge(sem("filter_sin"), 2)
            for t in range(TT):
                for n in range(4):
                    b = (2 + 4 * t + n) % 8
                    pe.matmul(bank(b), FA[4][:, P * t:P * t + P], FW3[:, CH * n:CH * n + CH], start=True, stop=True)\
                        .then_inc(sem("filter_raw"), 1)
            pe.wait_ge(sem("filter_abs"), 2)
            pe.wait_ge(sem("ones_set"), 1)
            for o in range(2):
                absf = (HT[:, :, :] if o == 0 else H[:, :, :]).rearrange("p a b -> p (a b)").rearrange("p (t d n) -> p t d n", t=TT, d=2)
                for c in range(4):
                    for s in range(4):
                        mm = pe.matmul(PS[0][:, 4 * o + c:4 * o + c + 1], absf[:, s // 2, s % 2, P * c:P * c + P], ones[:, 0:1],
                                       start=s == 0, stop=s == 3)
            mm.then_inc(sem("filter_sum"), 1)
            for o in range(2):
                for i in range(4):
                    b = 1 + (4 * o + i) % 4
                    if o:
                        pe.wait_ge(sem("ks_ready"), i + 1)
                    for s in range(4):
                        basis = DFTF if s < 2 else DFTB
                        mm = pe.matmul(bank(b), basis[:, s % 2, P * i:P * i + P], FH[:, s % 2, 2 * o + s // 2, :], start=s == 0, stop=s == 3)
                    mm.then_inc(sem("ks_done"), 1)
            pe.wait_ge(sem("ks_ready"), 8)
            pe.wait_ge(sem("filter_norm"), 1)

            ada(0, sa)
            pe.wait_ge(sem("ident_landed"), 16)
            turn("hy")
            pe.wait_ge(sem("ht_act"), 2)
            pe.wait_ge(sem("ht_dve"), 2)
            turn("ctx")
            turned("ctx")
            base = sa.first["hy_in"]
            for j in range(6):
                if j >= 4:
                    pe.wait_ge(sem("zc_ready"), j - 3)
                sa.need(pe, base + j)
                columns(sa, base + j, j % 4, HT).then_inc(sa.done, 1)
            base = sa.first["q_in"]
            for j in range(2):
                sa.need(pe, base + j)
                columns(sa, base + j, 4 + j, HT).then_inc(sa.done, 1)
            base = sa.first["k_in"]
            for j in range(2):
                if j:
                    pe.wait_ge(sem("zc_ready"), 6)
                sa.need(pe, base + j)
                columns(sa, base + j, 6 if j == 0 else 0, HT)
                columns(sa, base + j, 7 if j == 0 else 1, HCT).then_inc(sa.done, 1)
            base = sa.first["v_in"]
            pe.wait_ge(sem("qkv_ready"), 2)
            for h in range(2):
                sa.need(pe, base + h)
                w = cols_of(base + h, 4)
                for s in range(4):
                    src = HT if s < 2 else HCT
                    for k in range(4):
                        mm = pe.matmul(bank(2 + s), src[:, 4 * h + k, P * (s % 2):P * (s % 2) + P], w[:, k, :],
                                       start=h + k == 0, stop=h == 1 and k == 3)
                mm.then_inc(sa.done, 1)
            for o in range(2):
                if o == 0:
                    pe.wait_ge(sem("zc_ready"), 6)
                    pe.wait_ge(sem("qkv_ready"), 10)
                else:
                    pe.wait_ge(sem("hy_out"), 4)
                for t in range(TT):
                    for c in range(4):
                        mm = pe.transpose(PS[t][:, P * c:P * c + P], ZC[:, c, P * t:P * t + P], ident[:, :])
                    mm.then_inc(sem("hy_turned"), 1)
                pe.wait_ge(sem("hy_vt"), 2 * (o + 1))
                for i in range(4):
                    for t in range(TT):
                        mm = pe.matmul(bank(2 + i), DFTF[:, t, P * i:P * i + P], VT[:, t, :], start=t == 0, stop=t == 1)
                mm.then_inc(sem("hy_spec"), 1)
                pe.wait_ge(sem("hy_prod"), o + 1)
                for c in range(4):
                    for i in range(4):
                        mm = pe.matmul(PS[6 + c // 2][:, SEQ * (c % 2):SEQ * (c % 2) + SEQ], YF[:, i, P * c:P * c + P], IDFT[:, i, :],
                                       start=i == 0, stop=i == 3)
                    mm.then_inc(sem("hy_conv"), 1)
            NA = TT * HEADS

            def scores(it):
                t, h = it // HEADS, it % HEADS
                r, c = 32 * (h % 4), h // 4
                if it >= 2:
                    pe.wait_ge(sem("na_max"), it - 1)
                pe.matmul(PS[it % 2][:, 0:SEQ], QT[r:r + 32, c, P * t:P * t + P], KT[r:r + 32, c, :], start=True, stop=True)
                pe.matmul(PS[it % 2][:, SEQ:2 * SEQ], QT[r:r + 32, c, P * t:P * t + P], KCT[r:r + 32, c, :], start=True, stop=True)\
                    .then_inc(sem("na_scores"), 1)

            def weigh(it):
                t, h = it // HEADS, it % HEADS
                pe.wait_ge(sem("na_pt"), it + 1)
                for kc in range(4):
                    v = V if kc < 2 else VC
                    mm = pe.matmul(PS[4 + t][:, 32 * h:32 * h + 32], NPT[it % 2][:, kc, :], v[:, kc % 2, 32 * h:32 * h + 32],
                                   start=kc == 0, stop=kc == 3)
                mm.then_inc(sem("na_out"), 1)

            scores(0)
            for it in range(NA):
                if it + 1 < NA:
                    scores(it + 1)
                pe.wait_ge(sem("na_exp"), it + 1)
                if it >= 2:
                    pe.wait_ge(sem("na_pt"), it - 1)
                for kc in range(4):
                    mm = pe.transpose(PS[2 + it % 2][:, P * kc:P * kc + P], NP[it % 2][:, P * kc:P * kc + P], ident[:, :])
                mm.then_inc(sem("na_turned"), 1)
                if it >= 1:
                    weigh(it - 1)
            weigh(NA - 1)
            pe.wait_ge(sem("hy_out"), 8)
            for t in range(TT):
                pe.wait_ge(sem("na_norm"), t + 1)
                for k in range(4):
                    mm = pe.transpose(PS[6 + t][:, P * k:P * k + P], NO[:, t, P * k:P * k + P], ident[:, :])
                mm.then_inc(sem("na_o_turned"), 1)
            pe.wait_ge(sem("yt_na"), 2)
            rows_out(sa, "mix", lambda k: YT[:, k, :], 4)
            if STOP >= 2:
                turn("ffn")
                turned("ffn")
                gated_ffn(sa, "ffn_up", "ffn_down", HID_FFN)
            if STOP >= 3:
                ada_sum(1)
                turn("four")
                turned("four")
                pe.wait_ge(sem("four_landed"), 32)
                for t in range(TT):
                    for g in range(4):
                        b = 4 * t + g
                        for k in range(2):
                            mm = pe.matmul(bank(b), HT[:, 2 * g + k, P * t:P * t + P], FOD[:, k, :], start=k == 0, stop=k == 1)
                        mm.then_inc(sem("four_feat"), 1)
                pe.wait_ge(sem("four_ab_act"), 4)
                pe.wait_ge(sem("four_ab_dve"), 4)
                for f in range(KD):
                    g, half = f // 2, f % 2
                    for s in range(4):
                        t, im = s % 2, s // 2
                        mm = pe.matmul(PS[f // 2][:, SEQ * half:SEQ * half + SEQ],
                                       FAB[:, t, g, SEQ * im + P * half:SEQ * im + P * half + P], FOL[:, im, t, :],
                                       start=s == 0, stop=s == 3)
                    if half:
                        mm.then_inc(sem("four_tok"), 1)
                rows_out(sa, "four", lambda k: FYT[:, k, :], 4, lambda j: pe.wait_ge(sem("four_yt"), j + 1))
            if STOP >= 4:
                turn("moe")
                turned("moe")
                moe_tensor(pe)
            if STOP >= 5:
                ada_sum(2)
                turn("ret")
                turned("ret")
                base = sbm.first["ret_qk"]
                for j in range(RET_TILES):
                    if j >= 2:
                        pe.wait_ge(sem("rot_done"), j - 1)
                    sbm.need(pe, base + j)
                    columns(sbm, base + j, j % 2, HT).then_inc(sbm.done, 1)
                base = sbm.first["ret_vg"]
                for n in range(8):
                    if n >= 2:
                        pe.wait_ge(sem("vg_ready"), 2 * (n - 1))
                    for h in range(2):
                        i = base + 2 * n + h
                        sbm.need(pe, i)
                        w = cols_of(i, 4)
                        for t in range(TT):
                            for k in range(4):
                                mm = pe.matmul(bank(2 + 2 * (n % 2) + t), HT[:, 4 * h + k, P * t:P * t + P], w[:, k, :],
                                               start=h + k == 0, stop=h == 1 and k == 3)
                        mm.then_inc(sbm.done, 1)
                pe.wait_ge(sem("rot_out"), RET_TILES)
                pe.wait_ge(sem("vg_ready"), 16)

                def ret_scores(h):
                    b = 6 + h % 2
                    if h >= 2:
                        pe.wait_ge(sem("ret_decayed"), h - 1)
                    for k in range(2):
                        pe.matmul(PS[b][:, 0:SEQ], KR[:, 2 * h + k, 0:P], QR[:, 2 * h + k, :], start=k == 0, stop=k == 1)
                    for k in range(2):
                        mm = pe.matmul(PS[b][:, SEQ:SEQ + P], KR[:, 2 * h + k, P:SEQ], QR[:, 2 * h + k, P:SEQ], start=k == 0, stop=k == 1)
                    mm.then_inc(sem("ret_scored"), 1)

                def ret_turn(h):
                    pe.wait_ge(sem("ret_gated"), 2 * (h + 1))
                    for t in range(TT):
                        if h >= 1:
                            pe.wait_ge(sem("ott_ready"), 2 * (h - 1) + t + 1)
                        for q in range(4):
                            mm = pe.transpose(PS[4 + t][:, P * q:P * q + P], SG[:, t, h, P * q:P * q + P], ident[:, :])
                        mm.then_inc(sem("ret_turned"), 1)

                ret_scores(0)
                for h in range(RET_HEADS):
                    if h + 1 < RET_HEADS:
                        ret_scores(h + 1)
                    pe.wait_ge(sem("ret_decayed"), h + 1)
                    if h >= 2:
                        pe.wait_ge(sem("ret_gated"), 2 * (h - 1))
                    s = RS[h % 2]
                    pe.matmul(bank(2 * (h % 2)), s[:, 0:P], RV[:, 0, h, :], start=True, stop=True)
                    pe.matmul(bank(2 * (h % 2) + 1), s[:, P:2 * P], RV[:, 0, h, :], start=True, stop=False)
                    pe.matmul(bank(2 * (h % 2) + 1), s[:, 2 * P:3 * P], RV[:, 1, h, :], start=False, stop=True).then_inc(sem("ret_o"), 1)
                    if h >= 1:
                        ret_turn(h - 1)
                ret_turn(RET_HEADS - 1)
                pe.wait_ge(sem("ott_ready"), 2 * RET_HEADS)
                rows_out(sbm, "ret_out", lambda k: OTT[:, k, :], 8)
            if STOP >= 6:
                turn("cf0")
                turned("cf0")
                gated_ffn(sbm, "cf_up0", "cf_down0", HID_CF[0])
            if STOP >= 7:
                ada_sum(3)
                turn("s5")
                turned("s5")
                base = sbm.first["s5_in"]
                for j in range(4):
                    sbm.need(pe, base + j)
                    columns(sbm, base + j, 4 + j, HT).then_inc(sbm.done, 1)
                pe.wait_ge(sem("s5_landed"), 64)
                pe.wait_ge(sem("s5_u"), 4)
                pe.wait_ge(sem("s5_c"), 2)

                def s5_in(j):
                    r = 32 * (j % 4)
                    if j >= 2:
                        pe.wait_ge(sem("s5_rot"), j - 1)
                    pe.matmul(PS[j % 2][:, 0:SEQ], SBR[r:r + 32, j // 4, :], UT[r:r + 32, j // 4, :], start=True, stop=True)
                    pe.matmul(PS[j % 2][:, SEQ:2 * SEQ], SBI[r:r + 32, j // 4, :], UT[r:r + 32, j // 4, :], start=True, stop=True)\
                        .then_inc(sem("s5_bu"), 1)

                s5_in(0)
                s5_in(1)
                for j in range(S5_TILES):
                    q, r = j // 4, 32 * (j % 4)
                    if j % 4 == 0 and q >= 2:
                        pe.wait_ge(sem("s5_du"), q - 1)
                    pe.wait_ge(sem("s5_s"), j + 1)
                    pe.matmul(PS[2 + q % 2][r:r + 32, 0:SEQ], CFR[:, j, :], SS[j % 2][:, 0, :], start=True, stop=False)
                    pe.matmul(PS[2 + q % 2][r:r + 32, 0:SEQ], CFI[:, j, :], SS[j % 2][:, 1, :], start=False, stop=True).then_inc(sem("s5_y"), 1)
                    if j + 2 < S5_TILES:
                        s5_in(j + 2)
                pe.wait_ge(sem("s5_gelu"), KD)
                base = sbm.first["glu"]
                for k in range(KD):
                    i = base + k
                    sbm.need(pe, i)
                    for t in range(TT):
                        for n in range(4):
                            mm = pe.matmul(bank(4 * t + n), S5Y[:, k, P * t:P * t + P], slot(i)[:, BANK * n:BANK * n + BANK],
                                           start=k == 0, stop=k == KD - 1)
                    mm.then_inc(sbm.done, 1)
            if STOP >= 8:
                turn("cf1")
                turned("cf1")
                gated_ffn(sbm, "cf_up1", "cf_down1", HID_CF[1])

        @block.scalar
        def _(act):
            ch = Chain(act, sem("act_chain"))

            def norm_stats(name, x, junk=H):
                for t in range(TT):
                    ch.step(act.activation(junk[:, t, :], x[:, t, :], ACT.Square, accum_out=ss[:, t:t + 1]))
                act.wait_ge(ch.own, ch.n[ch.own.name])
                ch.link(act.activation(std, ss, ACT.Sqrt, scale=1.0 / D, bias=eps), sem("norm_std"))

            def turn_evac(name, dst):
                i = TURN[name]
                for t in range(TT):
                    act.wait_ge(sem("norm_turned"), 4 * i + 2 * t + 1)
                    ch.step(act.activation(dst[:, 0:4, P * t:P * t + P], bank(2 * t, 4), ACT.Copy), sem("ht_act"))

            def gated_ffn(st, up, hid_base, conv=None):
                base = st.first[up]
                for j in range(FF // 256):
                    b = 2 * (j % 2)
                    st.wait_done(act, base + 2 * j)
                    if j >= 2:
                        act.wait_ge(sem("hid_ready"), hid_base + j - 1)
                    if conv is None:
                        ch.step(act.activation(SIL[j % 2], bank(b, 2), ACT.Silu), sem("silu_done"))
                    else:
                        for m in range(2):
                            ch.step(act.activation(GC[j % 2][:, m, :], PS[b][:, SEQ * m:SEQ * m + SEQ], ACT.Identity,
                                                   scale=conv_w[conv][:, 2, 2 * j + m:2 * j + m + 1],
                                                   bias=conv_b[conv][:, 2 * j + m:2 * j + m + 1]), sem("conv_tap"))
                        act.wait_ge(sem("conv_done"), (FF // 256) * conv + j + 1)
                        ch.step(act.activation(SIL[j % 2], GC[j % 2], ACT.Silu), sem("silu_done"))

            act.wait_ge(sem("eps_set"), 1)
            act.wait_ge(sem("vec_landed"), 16)
            ch.step(act.activation(csil, vec[:, 0:24], ACT.Silu), sem("c_silu"))
            for l in range(2):
                act.wait_ge(sem("filter_arg"), l + 1)
                ch.step(act.activation(FA[3 + l], FA[2], ACT.Sin), sem("filter_sin"))
            act.wait_ge(sem("filter_ready"), 9)
            for o in range(2):
                absf = (HT[:, :, :] if o == 0 else H[:, :, :]).rearrange("p a b -> p (a b)").rearrange("p (t n) -> p t n", t=TT)
                fo = FH.rearrange("p t o n -> p t (o n)")[:, :, 2 * CH * o:2 * CH * (o + 1)]
                ch.step(act.activation(absf, fo, ACT.Abs), sem("filter_abs"))
            for i in range(8):
                act.wait_ge(sem("ks_done"), i + 1)
                ch.step(act.activation(KS[:, i // 4, i % 4, :], bank(1 + i % 4), ACT.Copy), sem("ks_ready"))
            act.wait_ge(sem("filter_sum"), 1)
            act.wait_ge(sem("x_landed"), 16)
            norm_stats("hy", X)
            turn_evac("hy", HT)
            act.wait_ge(sem("norm_turned"), 4)
            act.wait_ge(sem("ctx_landed"), 16)
            norm_stats("ctx", CX)
            turn_evac("ctx", HCT)
            base = sa.first["hy_in"]
            for j in range(6):
                sa.wait_done(act, base + j)
                if j == 0:
                    act.wait_ge(sem("norm_h"), 4)
                for m in range(2):
                    c = 2 * j + m
                    ch.step(act.activation(ZC[:, c, :], PS[j % 4][:, SEQ * m:SEQ * m + SEQ], ACT.Identity,
                                           scale=short_w[:, 1, c:c + 1], bias=short_b[:, c:c + 1]), sem("zc_tap"))
            base = sa.first["q_in"]
            for j in range(2):
                sa.wait_done(act, base + j)
                for m in range(2):
                    src = PS[4 + j][:, SEQ * m:SEQ * m + SEQ].rearrange("p (r c) -> p r c", c=GRID_W)
                    dst = QT[:, 2 * j + m, :].rearrange("p (r c) -> p r c", c=GRID_W)[:, :, ::-1]
                    ins = act.activation(dst, src, ACT.Copy)
                ch.step(ins, sem("qkv_ready"))
            base = sa.first["k_in"]
            for j in range(2):
                sa.wait_done(act, base + j)
                for s, dst in enumerate((KT, KCT)):
                    ch.step(act.activation(dst[:, 2 * j:2 * j + 2, :], bank((6 if j == 0 else 0) + s, 2), ACT.Copy), sem("qkv_ready"))
            sa.wait_done(act, sa.first["v_in"] + 1)
            for s in range(4):
                ch.step(act.activation((V if s < 2 else VC)[:, s % 2, :], bank(2 + s), ACT.Copy), sem("qkv_ready"))
            for o in range(2):
                for t in range(TT):
                    act.wait_ge(sem("hy_turned"), 2 * o + t + 1)
                    ch.step(act.activation(VT[:, t, :], bank(t), ACT.Copy), sem("hy_vt"))
            for it in range(TT * HEADS):
                act.wait_ge(sem("na_scores"), it + 1)
                if it >= 2:
                    act.wait_ge(sem("na_exp"), it - 1)
                ch.step(act.activation(NS[it % 2][:, SEQ:2 * SEQ], PS[it % 2][:, SEQ:2 * SEQ], ACT.Copy, scale=HEAD_DIM ** -0.5), sem("na_ctx"))
                act.wait_ge(sem("na_max"), it + 1)
                if it >= 2:
                    act.wait_ge(sem("na_turned"), it - 1)
                ch.step(act.activation(NP[it % 2], NS[it % 2], ACT.Exp, bias=mx[:, it % 2:it % 2 + 1],
                                       accum_out=rsum[:, it:it + 1]), sem("na_exp"))
                act.wait_ge(sem("na_turned"), it + 1)
                if it >= 2:
                    act.wait_ge(sem("na_out"), it - 1)
                ch.step(act.activation(NPT[it % 2], bank(2 + it % 2, 4), ACT.Copy), sem("na_pt"))
            for t in range(TT):
                act.wait_ge(sem("na_o_turned"), t + 1)
                for k in range(4):
                    src = PS[6 + t][:, P * k:P * k + P].rearrange("p (r c) -> p r c", c=GRID_W)
                    dst = YT[:, 4 + k, P * t:P * t + P].rearrange("p (r c) -> p r c", c=GRID_W)[:, :, ::-1]
                    ins = act.activation(dst, src, ACT.Copy)
                ch.step(ins, sem("yt_na"))
            if STOP >= 2:
                act.wait_ge(sem("x_ready"), 1)
                norm_stats("ffn", X)
                turn_evac("ffn", HT)
                gated_ffn(sa, "ffn_up", HID_FFN)
            if STOP >= 3:
                act.wait_ge(sem("x_ready"), 2)
                norm_stats("four", X)
                turn_evac("four", HT)
                for i in range(0, 8, 2):
                    act.wait_ge(sem("four_feat"), i + 1)
                    ch.step(act.activation(FAB[:, i // 4, i % 4, :], bank(i), ACT.Copy), sem("four_ab_act"))
                for f in range(4):
                    act.wait_ge(sem("four_tok"), f + 1)
                    ch.step(act.activation(FYT[:, 2 * f:2 * f + 2, :], bank(f, 2), ACT.Copy), sem("four_yt"))
            if STOP >= 4:
                act.wait_ge(sem("x_ready"), 3)
                norm_stats("moe", X)
                turn_evac("moe", HT)
                moe_scalar(act, ch)
                act.wait_ge(sem("moe_x"), 2)
                norm_stats("fin0", X)
            if STOP >= 5:
                act.wait_ge(sem("ret_arg"), 1)
                ch.step(act.activation(RSIN, RANG[2], ACT.Sin), sem("ret_table"))
                act.wait_ge(sem("ret_arg"), 2)
                ch.step(act.activation(RCOS, RANG[3], ACT.Sin), sem("ret_table"))
                norm_stats("ret", X)
                turn_evac("ret", HT)
                base = sbm.first["ret_vg"]
                for n in range(8):
                    sbm.wait_done(act, base + 2 * n + 1)
                    for t in range(TT):
                        dst = (RV if n < 4 else SG)[:, t, n % 4, :]
                        ch.step(act.activation(dst, bank(2 + 2 * (n % 2) + t), ACT.Copy if n < 4 else ACT.Silu), sem("vg_ready"))
                for h in range(RET_HEADS):
                    act.wait_ge(sem("ret_var"), h + 1)
                    ch.step(act.activation(gstd, bn2[:, :, 1], ACT.Sqrt, bias=eps), sem("ret_std"))
                    if h >= 1:
                        ret_turn_evac(act, ch, h - 1)
                ret_turn_evac(act, ch, RET_HEADS - 1)
            if STOP >= 6:
                act.wait_ge(sem("x_ready"), 5)
                norm_stats("cf0", X)
                turn_evac("cf0", HT)
                gated_ffn(sbm, "cf_up0", HID_CF[0], 0)
            if STOP >= 7:
                act.wait_ge(sem("x_ready"), 6)
                ch.step(act.activation(SP[:, 0, :], log_dt, ACT.Exp), sem("s5_dt"))
                act.wait_ge(sem("s5_arg"), 1)
                ch.step(act.activation(SP[:, 3, :], SP[:, 2, :], ACT.Exp), sem("s5_trig"))
                ch.step(act.activation(EK[:, 1], EA[:, 2], ACT.Sin), sem("s5_trig"))
                ch.step(act.activation(EK[:, 0], EA[:, 3], ACT.Sin), sem("s5_trig"))
                norm_stats("s5", X)
                turn_evac("s5", HT)
                base = sbm.first["s5_in"]
                for j in range(4):
                    sbm.wait_done(act, base + j)
                    ch.step(act.activation(UT[:, 2 * j:2 * j + 2, :], bank(4 + j, 2), ACT.Copy), sem("s5_u"))
                for q in range(KD):
                    act.wait_ge(sem("s5_du"), q + 1)
                    ch.step(act.activation(S5Y[:, q, :], SU, ACT.Gelu_apprx_tanh), sem("s5_gelu"))
                sbm.wait_done(act, sbm.first["glu"] + KD - 1)
                for t in range(TT):
                    for n in range(2):
                        i = 2 * t + n
                        if i:
                            act.wait_ge(sem("glu_used"), i)
                        ch.step(act.activation(GLS, bank(4 * t + 2 + n), ACT.Sigmoid), sem("glu_sig"))
            if STOP >= 8:
                act.wait_ge(sem("x_ready"), 7)
                norm_stats("cf1", X)
                turn_evac("cf1", HT)
                gated_ffn(sbm, "cf_up1", HID_CF[1], 1)
                act.wait_ge(sem("x_ready"), 8)
                norm_stats("fin1", X)

        @block.vector
        def _(dve):
            ch = Chain(dve, sem("dve_chain"))
            link = ch.link

            def tt(out, a, b, op, s=None):
                link(dve.tensor_tensor(out=out, in0=a, in1=b, op=op), s)

            def ts(out, a, s1, s2, op0, op1=ALU.bypass, s=None):
                if s2 is None:
                    link(dve.tensor_scalar(out, a, s1, None, op0), s)
                else:
                    link(dve.tensor_scalar(out, a, s1, s2, op0, op1), s)

            def stt(out, a, sc, b, op0, op1, s=None):
                link(dve.scalar_tensor_tensor(out=out, in0=a, scalar=sc, in1=b, op0=op0, op1=op1), s)

            def to_period(dst, x, tmp, quarter, s):
                ts(tmp, x, 1.0 / TWO_PI, 0.25 * quarter, ALU.mult, ALU.add)
                ts(tmp, tmp, MAGIC, None, ALU.add)
                ts(tmp, tmp, -MAGIC, None, ALU.add)
                stt(dst, tmp, -PI_A, x, ALU.mult, ALU.add)
                stt(dst, tmp, -PI_B, dst, ALU.mult, ALU.add)
                stt(dst, tmp, -PI_C, dst, ALU.mult, ALU.add)
                if quarter:
                    ts(dst, dst, 0.5 * math.pi * quarter, None, ALU.add)
                ts(dst, dst, PI_CLAMP, -PI_CLAMP, ALU.min, ALU.max, s)

            def scale_shift(name, x, gain, shift, scale):
                if gain == "load":
                    dve.wait_ge(sem("gain_landed"), 16 * (GB_LOADS[name] + 1))
                    stt(G[:, :], scale, 1.0, G[:, :], ALU.add, ALU.mult)
                elif gain == "scale":
                    ts(G[:, :], scale, 1.0, None, ALU.add)
                dve.wait_ge(sem("norm_std"), NORM[name] + 1)
                link(dve.reciprocal(rinv, std))
                for t in range(TT):
                    stt(H[:, t, :], x[:, t, :], rinv[:, t:t + 1], G[:, :], ALU.mult, ALU.mult, sem("gain_used") if t == TT - 1 else None)
                    tt(H[:, t, :], H[:, t, :], shift, ALU.add, sem("norm_h"))

            def turn_evac(name, dst):
                i = TURN[name]
                for t in range(TT):
                    dve.wait_ge(sem("norm_turned"), 4 * i + 2 * t + 2)
                    link(dve.tensor_copy(dst[:, 4:8, P * t:P * t + P], bank(2 * t + 1, 4)), sem("ht_dve"))

            def ada_evac(a):
                for n in range(ADA_N):
                    m = ADA_N * a + n
                    if a == 0:
                        sa.wait_done(dve, sa.first["ada0"] + 2 * n + 1)
                    else:
                        dve.wait_ge(sem("ada_summed"), m - ADA_N + 1)
                    dve.wait_ge(sem("bias_landed"), 16 * (m + 1))
                    if a == 0 and n < 4:
                        tt(ACX[:, BANK * n:BANK * (n + 1)], bank(2 + n % 2), BB[:, :], ALU.add)
                    tt(AD[:, BANK * n:BANK * (n + 1)], bank(n % 2), BB[:, :], ALU.add, sem("ada_evac"))

            def add_to_x(st, last, gate, tmp):
                st.wait_done(dve, last)
                for t in range(TT):
                    for n in range(2):
                        c = slice(BANK * n, BANK * n + BANK)
                        tt(tmp, bank(4 + 2 * t + n), gate[:, c], ALU.mult)
                        tt(X[:, t, c], X[:, t, c], tmp, ALU.add, sem("x_ready") if t + n == 2 else None)

            def ada_add(i):
                a, n, q = ADA_HALVES[i]
                acc, c0 = ADA_ACC[a][:, BANK * n:BANK * (n + 1)], 0 if a < 2 else 16
                dve.wait_ge(sem(f"ada_landed{i % ADA_SLOTS}"), 16 * (i // ADA_SLOTS + 1))
                for k in range(2):
                    w, c = ADA_RING[a][:, i % ADA_SLOTS, k, :], csil[:, c0 + 2 * q + k:c0 + 2 * q + k + 1]
                    if q + k == 0:
                        ts(acc, w, c, None, ALU.mult)
                    else:
                        stt(acc, w, c, acc, ALU.mult, ALU.add, sem("ada_added") if k else None)

            def gated_ffn(st, up, hid_base, conv=None, ada={}):
                base = st.first[up]
                for j in range(FF // 256):
                    b = 2 * (j % 2)
                    for i, after in ada.items():
                        if 2 * j - 2 < after <= 2 * j:
                            ada_add(i)
                    if conv is not None:
                        k = (FF // 256) * conv + j
                        dve.wait_ge(sem("conv_tap"), 2 * k + 2)
                        for m in range(2):
                            c = 2 * j + m
                            g, o = GC[j % 2][:, m, :], SEQ * m
                            stt(g[:, 2:SEQ], PS[b][:, o:o + SEQ - 2], conv_w[conv][:, 0, c:c + 1], g[:, 2:SEQ], ALU.mult, ALU.add)
                            stt(g[:, 1:SEQ], PS[b][:, o:o + SEQ - 1], conv_w[conv][:, 1, c:c + 1], g[:, 1:SEQ], ALU.mult, ALU.add,
                                sem("conv_done") if m else None)
                    st.wait_done(dve, base + 2 * j + 1)
                    dve.wait_ge(sem("silu_done"), hid_base + j + 1)
                    tt(HID[:, 2 * j:2 * j + 2, :], SIL[j % 2], bank(b + 1, 2), ALU.mult, sem("hid_ready"))
                for i, after in ada.items():
                    if after > 2 * (FF // 256) - 2:
                        ada_add(i)

            link(dve.memset(eps, EPS), sem("eps_set"))
            dve.wait_ge(sem("c_silu"), 1)
            link(dve.tensor_copy(CB[:, :, :], along(csil[:, 0:8], P)), sem("cb_ready"))
            link(dve.tensor_copy(CBX, along(csil[:, 8:16], P)), sem("cb_ready"))
            dve.wait_ge(sem("filter_landed"), 144)
            for l in range(2):
                dve.wait_ge(sem("filter_h"), l + 1)
                ts(FA[0], PS[l][0:HY_HID, 0:SEQ], FV[:, l:l + 1], FV[:, 2 + l:3 + l], ALU.add, ALU.mult)
                to_period(FA[2], FA[0], FA[1], 0, sem("filter_arg"))
            for i in range(8):
                t, n = i // 4, i % 4
                dve.wait_ge(sem("filter_raw"), i + 1)
                tt(FH[:, t, n, :], bank((2 + i) % 8), DEC[:, t, :], ALU.mult, sem("filter_ready"))
            link(dve.memset(FH[0:1, 0].rearrange("p (o d) n -> p o d n", d=2)[:, :, 1, :], 0.0), sem("filter_ready"))
            dve.wait_ge(sem("filter_sum"), 1)
            ts(sk_rn, PS[0][:, 0:8], EPS, None, ALU.add, s=sem("filter_norm"))
            link(dve.reciprocal(sk_rn, sk_rn))
            ada_evac(0)
            scale_shift("hy", X, "load", ada_part(0), ada_part(1))
            turn_evac("hy", HT)
            scale_shift("ctx", CX, "load", ACX[:, 0:D], ACX[:, D:2 * D])
            turn_evac("ctx", HCT)
            base = sa.first["hy_in"]
            for j in range(6):
                dve.wait_ge(sem("zc_tap"), 2 * j + 2)
                for m in range(2):
                    c, o = 2 * j + m, SEQ * m
                    stt(ZC[:, c, 1:SEQ], PS[j % 4][:, o:o + SEQ - 1], short_w[:, 0, c:c + 1], ZC[:, c, 1:SEQ], ALU.mult, ALU.add)
                    stt(ZC[:, c, 0:SEQ - 1], PS[j % 4][:, o + 1:o + SEQ], short_w[:, 2, c:c + 1], ZC[:, c, 0:SEQ - 1], ALU.mult, ALU.add,
                        sem("zc_ready") if m else None)
            T4 = HYT
            for o in range(2):
                dve.wait_ge(sem("hy_spec"), o + 1)
                if o:
                    dve.wait_ge(sem("hy_conv"), 4)
                for f in range(2):
                    ur, ui, kr, ki = bank(2 + f), bank(4 + f), KS[:, o, f, :], KS[:, o, 2 + f, :]
                    tt(YF[:, f, :], ur, kr, ALU.mult)
                    tt(T4[0], ui, ki, ALU.mult)
                    tt(YF[:, 2 + f, :], ur, ki, ALU.mult)
                    tt(T4[1], ui, kr, ALU.mult)
                    tt(YF[:, f, :], YF[:, f, :], T4[0], ALU.subtract)
                    tt(YF[:, 2 + f, :], YF[:, 2 + f, :], T4[1], ALU.add)
                tt(YF[0:1, 0, :], PS[2][0:1, :], KS[0:1, o, 0, :], ALU.mult)
                tt(YF[0:1, 2, :], PS[4][0:1, :], KS[0:1, o, 2, :], ALU.mult, sem("hy_prod"))
                for c in range(4):
                    dve.wait_ge(sem("hy_conv"), 4 * o + 2 * (c // 2) + 2)
                    y = PS[6 + c // 2][:, SEQ * (c % 2):SEQ * (c % 2) + SEQ]
                    tmp = T4[c % 2][:, 0:SEQ]
                    ts(tmp, y, sk_rn[:, 4 * o + c:4 * o + c + 1], None, ALU.mult)
                    stt(tmp, ZC[:, c, :], skip[:, 4 * o + c:4 * o + c + 1], tmp, ALU.mult, ALU.add)
                    tt((YT if o else ZC)[:, c, :], ZC[:, 4 * (o + 1) + c, :], tmp, ALU.mult, sem("hy_out"))
            for it in range(TT * HEADS):
                gi = it // 4
                dve.wait_ge(sem("na_scores"), it + 1)
                dve.wait_ge(sem("rpb_ready"), gi + 1)
                if it >= 2:
                    dve.wait_ge(sem("na_exp"), it - 1)
                dve.wait_ge(sem("na_ctx"), it + 1)
                stt(NS[it % 2][:, 0:SEQ], PS[it % 2][:, 0:SEQ], HEAD_DIM ** -0.5,
                    BIA[gi % 2][:, it % 4].rearrange("p r k -> p (r k)"), ALU.mult, ALU.add)
                link(dve.tensor_reduce(mx[:, it % 2:it % 2 + 1], NS[it % 2], AX.X, ALU.max, negate=True), sem("na_max"))
            dve.wait_ge(sem("na_exp"), TT * HEADS)
            link(dve.reciprocal(rsum_inv, rsum))
            for t in range(TT):
                dve.wait_ge(sem("na_out"), HEADS * (t + 1))
                tt(NO[:, t, :].rearrange("p (h d) -> p h d", d=HEAD_DIM), bank(4 + t, HEADS),
                   along(rsum_inv[:, HEADS * t:HEADS * t + HEADS], HEAD_DIM), ALU.mult, sem("na_norm"))
            add_to_x(sa, sa.first["mix"] + 3, ada_part(2), XT_MIX)
            if STOP >= 2:
                scale_shift("ffn", X, "load", ada_part(3), ada_part(4))
                turn_evac("ffn", HT)
                gated_ffn(sa, "ffn_up", HID_FFN, ada=ADA_PLAN["ffn"])
                add_to_x(sa, sa.first["ffn_down"] + FF // 256 - 1, ada_part(5), XT)
            if STOP >= 3:
                ada_evac(1)
                scale_shift("four", X, "load", ada_part(0), ada_part(1))
                turn_evac("four", HT)
                for i in range(1, 8, 2):
                    dve.wait_ge(sem("four_feat"), i + 1)
                    link(dve.tensor_copy(FAB[:, i // 4, i % 4, :], bank(i)), sem("four_ab_dve"))
                add_to_x(sa, sa.first["four"] + 3, ada_part(2), XT)
            if STOP >= 4:
                scale_shift("moe", X, "load", ada_part(3), ada_part(4))
                turn_evac("moe", HT)
                moe_vector(dve, ch)
                dve.wait_ge(sem("gain_landed"), 16 * (GB_LOADS["fin0"] + 1))
                dve.wait_ge(sem("norm_std"), NORM["fin0"] + 1)
                link(dve.reciprocal(rinv, std))
                for t in range(TT):
                    stt(X[:, t, :], X[:, t, :], rinv[:, t:t + 1], G[:, :], ALU.mult, ALU.mult, sem("x_ready") if t else None)
            if STOP >= 5:
                dve.wait_ge(sem("ret_landed"), 48)
                link(dve.tensor_copy(RANG[0], RPOS))
                ts(RANG[0], RANG[0], INVF, None, ALU.mult)
                to_period(RANG[2], RANG[0], RANG[1], 0, sem("ret_arg"))
                to_period(RANG[3], RANG[0], RANG[1], 1, sem("ret_arg"))
                ada_evac(2)
                scale_shift("ret", X, "scale", ada_part(0), ada_part(1))
                turn_evac("ret", HT)
                dve.wait_ge(sem("ret_table"), 2)
                base = sbm.first["ret_qk"]
                for j in range(RET_TILES):
                    dst = (QR if j < 4 else KR)[:, 2 * (j % 4):2 * (j % 4) + 2, :]
                    sbm.wait_done(dve, base + j)
                    tt(RM[0], bank(j % 2, 2), over(RCOS, 2), ALU.mult)
                    tt(RM[1], bank(j % 2, 2), over(RSIN, 2), ALU.mult, sem("rot_done"))
                    tt(dst[:, 0, :], RM[0][:, 0, :], RM[1][:, 1, :], ALU.subtract)
                    tt(dst[:, 1, :], RM[1][:, 0, :], RM[0][:, 1, :], ALU.add, sem("rot_out"))
                for h in range(RET_HEADS):
                    def decay(h):
                        dve.wait_ge(sem("ret_scored"), h + 1)
                        if h >= 2:
                            dve.wait_ge(sem("ret_o"), h - 1)
                        tt(RS[h % 2], PS[6 + h % 2][:, 0:384], RT[:, h, :], ALU.mult, sem("ret_decayed"))
                    if h == 0:
                        decay(0)
                    if h + 1 < RET_HEADS:
                        decay(h + 1)
                    dve.wait_ge(sem("ret_o"), h + 1)
                    for t in range(TT):
                        link(dve.bn_stats(bn6[:, t, :], bank(2 * (h % 2) + t)))
                        link(dve.bn_aggr(bn2[:, t, :], bn6[:, t, :]), sem("ret_var") if t else None)
                    dve.wait_ge(sem("ret_std"), h + 1)
                    link(dve.reciprocal(grstd, gstd))
                    for t in range(TT):
                        ts(RON, bank(2 * (h % 2) + t), bn2[:, t, 0:1], grstd[:, t:t + 1], ALU.subtract, ALU.mult)
                        tt(SG[:, t, h, :], SG[:, t, h, :], RON, ALU.mult, sem("ret_gated"))
                add_to_x(sbm, sbm.first["ret_out"] + 7, ada_part(2), RXT)
            if STOP >= 6:
                scale_shift("cf0", X, "scale", ada_part(3), ada_part(4))
                turn_evac("cf0", HT)
                gated_ffn(sbm, "cf_up0", HID_CF[0], 0, ADA_PLAN["cf0"])
                add_to_x(sbm, sbm.first["cf_down0"] + FF // 256 - 1, ada_part(5), XT)
            if STOP >= 7:
                s5_vector(dve, ch, tt, ts, stt, to_period, scale_shift, turn_evac, ada_evac)
            if STOP >= 8:
                scale_shift("cf1", X, "scale", ada_part(3), ada_part(4))
                turn_evac("cf1", HT)
                gated_ffn(sbm, "cf_up1", HID_CF[1], 1)
                add_to_x(sbm, sbm.first["cf_down1"] + FF // 256 - 1, ada_part(5), XT)
                dve.wait_ge(sem("gain_landed"), 16 * (GB_LOADS["fin1"] + 1))
                dve.wait_ge(sem("norm_std"), NORM["fin1"] + 1)
                link(dve.reciprocal(rinv, std))
                for t in range(TT):
                    stt(H[:, t, :], X[:, t, :], rinv[:, t:t + 1], G[:, :], ALU.mult, ALU.mult, sem("out_ready") if t else None)
            else:
                link(dve.tensor_copy(H[:, :, :], X[:, :, :]), sem("out_ready"))




def shape_tables():
    f32 = np.float32
    tab = {}
    n = SEQ
    t = np.linspace(0.0, 1.0, n, dtype=f32)[:, None]
    bands = np.linspace(1e-4, HY_BANDS - 1, HY_BANDS, dtype=f32)
    ang = (f32(2.0 * math.pi / n) * np.arange(n, dtype=f32)[:, None]) * bands[None, :]
    feats = np.concatenate([t, np.cos(ang), -np.sin(ang)], axis=-1).astype(f32)
    tab["t_feats"] = feats.T.copy()
    deltas = np.abs(np.linspace(math.log(1e-2) / 1.5, math.log(1e-2) / 0.3, CH, dtype=f32))
    decay = np.exp(-t * deltas[None, :]).astype(f32)
    tab["t_decay"] = decay.reshape(2, P, CH).transpose(1, 0, 2)
    f = np.arange(n)
    lag = np.arange(n)[:, None]
    phase = 2 * np.pi * ((lag * f[None, :]) % (2 * n)) / (2 * n)
    nyquist = np.where(np.arange(n) % 2 == 0, 1.0, -1.0)
    cos, sin = np.cos(phase), np.sin(phase)
    fwd_im, bwd_im = -sin, sin.copy()
    fwd_im[:, 0], bwd_im[:, 0] = nyquist, nyquist
    tab["t_dft_fwd"] = np.concatenate([cos, fwd_im], 1).astype(f32).reshape(2, P, 2 * n).transpose(1, 0, 2)
    tab["t_dft_bwd"] = np.concatenate([cos, bwd_im], 1).astype(f32).reshape(2, P, 2 * n).transpose(1, 0, 2)
    weight = np.where(f == 0, 1.0, 2.0)[:, None] / (2 * n)
    inv_re, inv_im = weight * cos.T, -weight * sin.T
    inv_im[0] = nyquist / (2 * n)
    tab["t_idft"] = np.concatenate([inv_re, inv_im], 0).astype(f32).reshape(4, P, n).transpose(1, 0, 2)
    q = 63 - (np.arange(P) % 64)
    start = np.clip(q - WIN_C // 2, 0, GRID_W - WIN_C)[:, None]
    key = np.arange(GRID_W)[None, :]
    tab["t_window"] = np.where((key >= start) & (key < start + WIN_C), 0.0, NEG).astype(f32)
    d = np.arange(n)
    ph = 2 * np.pi * ((d[:, None] * d[None, :]) % n) / n
    tab["t_four_d"] = np.concatenate([np.cos(ph), np.sin(ph)], 1).astype(f32).reshape(2, P, 2 * n).transpose(1, 0, 2)
    tab["t_four_l"] = np.stack([np.cos(ph) / n, -np.sin(ph) / n], 0).astype(f32).reshape(2, 2, P, n).transpose(2, 0, 1, 3)
    lg = np.log1p(-np.exp2(-5.0 - np.arange(RET_HEADS)))
    m = np.arange(n)[:, None]
    k = np.arange(n)[None, :]
    full = np.where(k >= m, np.exp(lg[:, None, None] * np.maximum(k - m, 0)), 0.0) * RET_DK ** -0.5
    tab["t_ret"] = np.concatenate([full[:, :P, :], full[:, P:, P:]], 2).astype(f32).transpose(1, 0, 2)
    half = RET_DK // 2
    tab["t_inv_freq"] = np.power(f32(10000.0), -np.arange(half, dtype=f32) / f32(half)).astype(f32)[:, None]
    tab["t_ident"] = np.eye(P, dtype=f32)
    tab["t_before"] = np.triu(np.ones((P, P), f32), 1)
    tab["t_iota"] = np.broadcast_to(np.arange(P, dtype=f32), (P, P))
    return {name: np.ascontiguousarray(a, dtype=f32) for name, a in tab.items()}


def by_partition(a, p=P):
    a = np.asarray(a)
    a = a.reshape(-1, a.shape[-1] // p, p)
    return a.transpose(2, 0, 1).reshape(p, -1)


def laid_out(x):
    out = {}
    for name in ("w_ada", "w_in", "w_mix_out", "ffn_w1", "ffn_w3", "ffn_w2", "w_fourier", "moe_w1", "moe_w3", "moe_w2",
                 "ada_w_2", "ret_w_in_2", "ret_w_out_2", "s5_w_in_2", "s5_w_glu_2", "ffn_w_up_2", "ffn_w_down_2",
                 "x", "ctx", "b_ada", "ada_b_2", "norm_g", "final_g", "final_norm_g_2", "na_rpb", "pos_2",
                 "hy_f_w1", "hy_f_w2", "hy_f_w3", "b_router"):
        out[name] = np.ascontiguousarray(x[name])
    out["filter_vectors"] = np.ascontiguousarray(np.stack(
        [x["hy_f_b1"][0], x["hy_f_b2"][0], x["hy_f_freq"][0, 0], x["hy_f_freq"][0, 1]], 1))
    router = np.asarray(x["w_router"])[0]
    out["w_router"] = np.ascontiguousarray(router.reshape(KD, P, EXPERTS).transpose(1, 0, 2))
    def states(a):
        return np.asarray(a).reshape(S5_TILES, 2, S5_STATE).transpose(1, 2, 0).reshape(P, S5_TILES)
    dt = np.repeat(np.asarray(x["s5_log_dt_2"])[0].reshape(S5_TILES, 2).T[:, None, :], S5_STATE, 1).reshape(P, S5_TILES)
    cols = [by_partition(x["c"]), by_partition(x["c_ctx"]), by_partition(x["c_2"]),
            by_partition(x["hy_short_w"][0]), by_partition(x["hy_short_b"]), by_partition(x["hy_skip"][0]),
            states(x["s5_lam_re_2"][0]), states(x["s5_lam_im_2"][0]), dt, by_partition(x["s5_d_2"]),
            by_partition(x["ffn_conv_w_2"][0, :, 0]), by_partition(x["ffn_conv_w_2"][1, :, 0]),
            by_partition(x["ffn_conv_b_2"])]
    out["vectors"] = np.ascontiguousarray(np.concatenate(cols, 1))
    for name, src in (("s5_b_re", "s5_b_re_2"), ("s5_b_im", "s5_b_im_2")):
        b = np.asarray(x[src])[0].reshape(KD, 4, 2, S5_STATE, S5_GROUP)
        blocks = np.zeros((4, 2, S5_GROUP, KD, 2, S5_STATE), b.dtype)
        for gp in range(2):
            blocks[:, gp, :, :, gp, :] = b[:, :, gp].transpose(1, 3, 0, 2)
        out[name] = blocks.reshape(P, KD, P)
    for name, src in (("s5_c_re", "s5_c_re_2"), ("s5_c_im", "s5_c_im_2")):
        c = np.asarray(x[src])[0].reshape(S5_TILES, 2, S5_GROUP, S5_STATE)
        blocks = np.zeros((2, S5_STATE, S5_TILES, 2, S5_GROUP), c.dtype)
        for gp in range(2):
            blocks[gp, :, :, gp, :] = c[:, gp].transpose(2, 0, 1)
        out[name] = blocks.reshape(P, S5_TILES, 2 * S5_GROUP)
    return out


def kernel(**inputs):
    import concourse.bacc as bacc
    from concourse.bass_utils import run_bass_kernel_spmd

    nc = bacc.Bacc("TRN2", target_bir_lowering=False, num_devices=1)
    arrays = {f"in_{name}": a for name, a in {**laid_out(inputs), **shape_tables()}.items()}
    given = {name[3:]: nc.dram_tensor(name, a.shape, mybir.dt.from_np(a.dtype), kind="ExternalInput").ap()
             for name, a in arrays.items()}
    out = nc.dram_tensor("out", (1, SEQ, D), F32, kind="ExternalOutput").ap()
    build(nc, given, out)
    result = run_bass_kernel_spmd(nc, [arrays], core_ids=[0])
    return result.results[0]["out"]
```

```python
import math
from contextlib import ExitStack

import numpy as np

import concourse.bass as bass
from concourse import mybir

F32 = mybir.dt.float32
F32R = mybir.dt.float32r
I32 = mybir.dt.int32
U32 = mybir.dt.uint32
ACT = mybir.ActivationFunctionType
ALU = mybir.AluOpType
AX = mybir.AxisListType

P = 128
D = 1024
KD = D // P
SEQ = 256
TT = SEQ // P
EPS = 1e-6
NEG = -1e30
BANK = 512
N_MOD = 6

CH = 512
HY_BANDS = 16
HY_EMB = 2 * HY_BANDS + 1
HY_HID = 64
HY_CHUNKS = 3 * CH // P
GRID_W = 64
GRID_R = SEQ // GRID_W
WIN_R, WIN_C = 8, 16
RPB_R, RPB_C = 2 * WIN_R - 1, 2 * WIN_C - 1
HEADS = 16
HEAD_DIM = 32
FF = 2816
FF_CHUNKS = FF // P
EXPERTS = 8
FFE = 3584
RET_HEADS = 4
RET_DK = 256
RET_DV = 512
S5_GROUP = 16
S5_STATE = 64
S5_TILES = D // S5_GROUP * S5_STATE // P

RING = 7
TILE = 2048

TWO_PI = 2 * math.pi
MAGIC = 1.5 * 2.0 ** 23
PI_CLAMP = 3.1415925
PI_A = 6.28125
PI_B = float(np.float32(math.floor((TWO_PI - PI_A) * 2 ** 21) / 2 ** 21))
PI_C = float(np.float32(TWO_PI - PI_A - PI_B))


class Chain:

    def __init__(self, eng, own):
        self.eng, self.own, self.n = eng, own, {}

    def step(self, ins, sem=None):
        sem = sem or self.own
        self.n[sem.name] = self.n.get(sem.name, 0) + 1
        ins.then_inc(sem, 1)
        return sem, self.n[sem.name]

    def link(self, ins, sem=None):
        self.eng.wait_ge(*self.step(ins, sem))


class LoopChain:

    def __init__(self, eng, own, rnd, per):
        self.eng, self.own, self.rnd, self.per, self.n = eng, own, rnd, per, 0

    def link(self, ins):
        self.n += 1
        ins.then_inc(self.own, 1)
        self.eng.wait_ge(self.own, self.rnd * self.per + self.n)


class Stream:

    def __init__(self, items, landed, done):
        self.items, self.landed, self.done = items, landed, done
        self.first = {}
        for i, it in enumerate(items):
            self.first.setdefault(it[0], i)

    def need(self, pe, i):
        pe.wait_ge(self.landed[i % RING], 16 * (i // RING + 1))

    def wait_done(self, eng, i):
        eng.wait_ge(self.done, i + 1)


def ada_tiles(name, w):
    return [(name, w[BANK * h:BANK * (h + 1), BANK * n:BANK * (n + 1)], 4) for n in range(N_MOD * D // BANK) for h in range(2)]


def col_tile(name, w, j):
    return (name, w[:, 256 * j:256 * (j + 1)], 8)


def half_tiles(name, w, col):
    return [(name, w[BANK * h:BANK * (h + 1), col:col + BANK], 4) for h in range(2)]


def row_tiles(name, w):
    rows = TILE * P // w.shape[1]
    return [(name, w[rows * j:rows * (j + 1), :], rows // P) for j in range(w.shape[0] // rows)]


MOE_CHUNKS = FFE // BANK
MOE_STEPS = MOE_CHUNKS + 2


def moe_order():
    order = []
    for c in range(MOE_STEPS):
        for name, chunk in (("w1", c), ("w2", c - 2), ("w3", c)):
            if 0 <= chunk < MOE_CHUNKS:
                order += [(name, chunk, 0), (name, chunk, 1)]
    return order


def build(nc, A, out):
    with ExitStack() as ctx:
        def sb(name, shape, dt=F32):
            return ctx.enter_context(nc.sbuf_tensor(name, shape, dt))

        sems = {}

        def sem(name):
            if name not in sems:
                sems[name] = ctx.enter_context(nc.semaphore(name))
            return sems[name]

        wa, wi = A["w_ada"], A["w_in"][0]
        items = ada_tiles("ada0", wa[0])
        items += [col_tile("hy_in", wi, j) for j in range(6)]
        items += [col_tile("q_in", wi, 6 + j) for j in range(2)]
        items += [col_tile("k_in", wi, 8 + j) for j in range(2)]
        items += half_tiles("v_in", wi, 5 * CH)
        items += row_tiles("mix", A["w_mix_out"][0])
        for j in range(FF // 256):
            items += [col_tile("ffn_up", A["ffn_w1"][0], j), col_tile("ffn_up", A["ffn_w3"][0], j)]
        items += row_tiles("ffn_down", A["ffn_w2"][0])
        items += row_tiles("four", A["w_fourier"][0])
        sa = Stream(items, [sem(f"landed_a{i}") for i in range(RING)], sem("tiles_done_a"))
        moe_first = len(items)
        moe_tiles = moe_order()
        assert len(moe_tiles) % RING == 0

        wb = A["ada_w_2"]
        ri, wu, wd = A["ret_w_in_2"][0], A["ffn_w_up_2"], A["ffn_w_down_2"]

        def conv_ffn_tiles(layer):
            tiles = []
            for j in range(FF // 256):
                tiles += [col_tile(f"cf_up{layer}", wu[layer], FF // 256 + j), col_tile(f"cf_up{layer}", wu[layer], j)]
            return tiles + row_tiles(f"cf_down{layer}", wd[layer])

        items = [col_tile("ret_qk", ri, j) for j in range(8)]
        for n in range(8):
            items += half_tiles("ret_vg", ri, 2048 + BANK * n)
        items += row_tiles("ret_out", A["ret_w_out_2"][0])
        items += conv_ffn_tiles(0)
        items += [col_tile("s5_in", A["s5_w_in_2"][0], j) for j in range(4)]
        items += row_tiles("glu", A["s5_w_glu_2"][0])
        items += conv_ffn_tiles(1)
        sbm = Stream(items, [sem(f"landed_b{i}") for i in range(RING)], sem("tiles_done_b"))

        ring = sb("ring", [P, RING, TILE])
        X = sb("X", [P, TT, D])
        H = sb("H", [P, TT, D])
        HT = sb("HT", [P, KD, SEQ])
        ad_at = nc.sbuf_base
        AD = sb("AD", [P, N_MOD * D])
        G = sb("G", [P, D])
        BB = sb("BB", [P, BANK])
        CB = sb("CB", [P, KD, P])
        ident = sb("ident", [P, P])
        ones = sb("ones", [P, P])
        vec = sb("vec", [P, 360])
        small = sb("small", [P, 160])
        small_i = sb("small_i", [P, 16], I32)
        ARENA = 22528
        arena_at = nc.sbuf_base
        arena = sb("arena", [P, ARENA])
        PS = [ctx.enter_context(nc.psum_tensor(f"bank{i}", [P, BANK], F32)) for i in range(8)]

        def at(off, *shape, parts=P):
            n = int(np.prod(shape))
            assert off + n <= ARENA
            v = arena[0:parts, off:off + n]
            names = "abcd"[:len(shape)]
            if len(shape) > 1:
                v = v.rearrange(f"p ({' '.join(names)}) -> p {' '.join(names)}",
                                **{k: s for k, s in zip(names[1:], shape[1:])})
            return v

        def slot(i):
            return ring[:, i % RING, :]

        def cols_of(i, k):
            return slot(i).rearrange("p (k n) -> p k n", k=k)

        def bank(i, a=None):
            return PS[i][:, :] if a is None else PS[i][:, :].rearrange("p (a b) -> p a b", a=a)

        def over(ap, n):
            return ap.unsqueeze(1).to_broadcast([ap.shape[0], n, ap.shape[1]])

        def along(ap, n):
            return ap.unsqueeze(2).to_broadcast([ap.shape[0], ap.shape[1], n])

        short_w = vec[:, 24:60].rearrange("p (t m) -> p t m", t=3)
        short_b = vec[:, 60:72]
        skip = vec[:, 72:80]
        lam_re, lam_im, log_dt, s5_d = vec[:, 80:112], vec[:, 112:144], vec[:, 144:176], vec[:, 176:184]
        conv_w = [vec[:, 184 + 66 * l:250 + 66 * l].rearrange("p (t m) -> p t m", t=3) for l in range(2)]
        conv_b = [vec[:, 316 + 22 * l:338 + 22 * l] for l in range(2)]

        ss, std, rinv = small[:, 126:130], small[:, 2:4], small[:, 4:6]
        csil = small[:, 6:30]
        sk_rn = small[:, 30:38]
        rsum, rsum_inv = small[:, 38:70], small[:, 70:102]
        mx = small[:, 102:104]
        bn6 = small[:, 104:116].rearrange("p (t s) -> p t s", t=2)
        bn2 = small[:, 116:120].rearrange("p (t s) -> p t s", t=2)
        gstd, grstd = small[:, 120:122], small[:, 122:124]

        def ada_part(i):
            return AD[:, D * i:D * (i + 1)]

        ZC = at(0, HY_CHUNKS, SEQ)
        ACX = at(0, 2 * D)
        CBX = at(2 * D, KD, P)
        QT = at(3072, 4, SEQ)
        KT = at(4096, 4, SEQ)
        KCT = at(5120, 4, SEQ)
        V = at(6144, TT, CH)
        VC = at(7168, TT, CH)
        FW3 = at(3072, 4 * CH, parts=HY_HID)
        FEATS = at(5120, SEQ, parts=HY_EMB)
        FW1 = at(5376, HY_HID, parts=HY_EMB)
        FW2 = at(5440, HY_HID, parts=HY_HID)
        FV = at(5504, 4, parts=HY_HID)
        FA = [at(5632 + 256 * i, SEQ, parts=HY_HID) for i in range(5)]
        YT = at(8192, KD, SEQ)
        CX = at(8192, TT, D)
        HCT = at(8192, KD, SEQ)
        KS = at(10240, 2, 4, CH)
        DFTF = at(14336, TT, 2 * SEQ)
        IDFT = at(15360, 4, SEQ)
        FH = at(16384, TT, 4, CH)
        DFTB = at(20480, TT, 2 * SEQ)
        DEC = at(21504, TT, CH)
        BIA = [at(16384 + 1024 * i, 4, GRID_R, GRID_W) for i in range(2)]
        WIN = at(18432, GRID_W)
        NS = [at(18496 + 512 * i, 512) for i in range(2)]
        NP = [at(19520 + 512 * i, 512) for i in range(2)]
        NPT = [at(20544 + 512 * i, 4, P) for i in range(2)]
        VT = H[:, 0, :].rearrange("p (t n) -> p t n", t=TT)
        NO = H[:, 1, :].rearrange("p (t n) -> p t n", t=TT)
        YF = HT[:, :, :].rearrange("p a b -> p (a b)").rearrange("p (i n) -> p i n", i=4)
        HYT = [at(20544 + 512 * i, CH) for i in range(2)]
        XT_MIX = at(18496, BANK)
        eps = small[:, 124:125]
        HID = at(0, FF_CHUNKS, SEQ)
        SIL = [at(5632 + 512 * i, 2, SEQ) for i in range(2)]
        XT = at(6656, BANK)
        GC = [at(7168 + 512 * i, 2, SEQ) for i in range(2)]
        ADA_SLOTS, ADA_N = 3, N_MOD * D // BANK
        ADA_ACC = {1: at(10240, N_MOD * D), 2: at(16384, N_MOD * D), 3: at(16384, N_MOD * D)}
        ADA_W = {1: wa[1], 2: wb[0], 3: wb[1]}
        ADA_RING = {1: at(7168, ADA_SLOTS, 2, BANK), 2: at(7168, ADA_SLOTS, 2, BANK), 3: at(8192, ADA_SLOTS, 2, BANK)}
        ADA_HALVES = [(a, n, q) for a in (1, 2, 3) for n in range(ADA_N) for q in range(KD // 2)]

        def ada_plan(first, last):
            tiles, begin = 3 * (FF // 256), RING - 1
            return {i: begin + (i - first) * (tiles - begin) // (last - first) for i in range(first, last)}

        ADA_PLAN = {"ffn": ada_plan(0, 2 * 4 * ADA_N), "cf0": ada_plan(2 * 4 * ADA_N, 3 * 4 * ADA_N)}

        FOD = at(8192, TT, 2 * SEQ)
        FOL = at(9216, 2, TT, SEQ)
        FAB = at(10240, TT, 4, 2 * SEQ)
        FYT = at(14336, KD, SEQ)

        def bcast(row):
            return row.partition_broadcast(P)

        NORM = {n: i for i, n in enumerate(["hy", "ctx", "ffn", "four", "moe", "fin0", "ret", "cf0", "s5", "cf1", "fin1"])}
        TURN = {n: i for i, n in enumerate(["hy", "ctx", "ffn", "four", "moe", "ret", "cf0", "s5", "cf1"])}
        GB_LOADS = {n: i for i, n in enumerate(["hy", "ctx", "ffn", "four", "moe", "fin0", "fin1"])}
        RET_TILES = 2 * RET_HEADS
        HID_FFN, HID_CF = 0, [FF // 256, 2 * (FF // 256)]

        GAIN_USES = {"ctx": 1, "ffn": 2, "four": 3, "moe": 4, "fin0": 5, "fin1": 9}
        def parts(name, at_byte, off, *shape):
            return nc.alloc_sbuf_tensor_at(name, [P, *shape], F32R, offset=at_byte + 4 * off)

        SPLIT = 4
        HALF = TILE // 2
        WH = [parts(f"w_high{i}", arena_at, HALF * i, HALF) for i in range(SPLIT)]
        WL = [parts(f"w_low{i}", arena_at, HALF * (SPLIT + i), HALF) for i in range(SPLIT)]
        MHTH = [[parts(f"hidden_high{i}{u}", arena_at, 8192 + 512 * (2 * i + u), 4, P) for u in range(2)] for i in range(2)]
        MHTL = [[parts(f"hidden_low{i}{u}", arena_at, 10240 + 512 * (2 * i + u), 4, P) for u in range(2)] for i in range(2)]
        XGH = [parts(f"tokens_high{u}", ad_at, D * u, KD, P) for u in range(2)]
        XGL = [parts(f"tokens_low{u}", ad_at, D * (2 + u), KD, P) for u in range(2)]
        PM = [at(12288 + 256 * u, TT, P) for u in range(2)]
        PG = [at(12800 + 256 * u, TT, P) for u in range(2)]
        PGT = [at(13312 + 256 * u, SEQ) for u in range(2)]
        YE = [at(13824 + D * u, D) for u in range(2)]
        WR = at(15872, KD, EXPERTS)
        BR8 = at(15936, EXPERTS)
        IOTA = at(15944, P)
        BEFORE = at(16072, P)
        CUR = at(16200, 6)
        PW = at(16208, 6, TT)
        MS = [[HT[:, 4 * i + 2 * u:4 * i + 2 * u + 2, :].rearrange("p a b -> p (a b)") for u in range(2)] for i in range(2)]

        def in_ad(off, *shape):
            n = int(np.prod(shape))
            v = AD[:, 4 * D + off:4 * D + off + n]
            return v if len(shape) == 1 else v.rearrange("p (a b) -> p a b", b=shape[1])

        E8 = EXPERTS
        LG, M8, IDXF, MASK = (in_ad(TT * E8 * i, TT, E8) for i in range(4))
        IDX = in_ad(TT * E8 * 4, TT, E8).bitcast(U32)
        OH = [in_ad(TT * E8 * (5 + i), TT, E8) for i in range(2)]
        SLOT, GATE, GT1 = (in_ad(TT * E8 * (7 + i), TT, E8) for i in range(3))
        MSUM, OVER, OVER_N, FROM_E, POS = (in_ad(160 + E8 * i, E8) for i in range(5))
        AT_POS, AT_TMP = in_ad(208, E8, E8), in_ad(272, E8, E8)
        OVER_MAX = SEQ * 2 // (P + 1)
        COLS = E8 + OVER_MAX
        SLOT_R, GATE_R = in_ad(336, TT, COLS), in_ad(336 + TT * COLS, TT, COLS)
        EIDF = in_ad(336 + 2 * TT * COLS, E8 + 2)

        NT = len(moe_tiles)
        HALVES = 2 * NT
        tile_at = {t: i for i, t in enumerate(moe_tiles)}
        LO_FREE, USED_FREE = 2 * RING, SPLIT

        def half_of(kind, c, q):
            return 2 * tile_at[kind, c, 0] + q

        def all_rounds(eng, body):
            eng.wait_ge(sem("rounds_ready"), 2)
            one = eng.value_load(small_i[0:1, E8:E8 + 1], min_val=E8 - OVER_MAX, max_val=E8 - 1)
            two = eng.value_load(small_i[0:1, E8 + 1:E8 + 2], min_val=1, max_val=OVER_MAX)
            with eng.Fori(0, one) as g:
                body(g, 1, None)
            with eng.Fori(0, two) as j:
                body(one + j, 2, j)

        def used_wait(eng, g, half):
            eng.wait_ge(sem("w_used"), g * HALVES + (USED_FREE + half + 1))

        def moe_sync(sp):
            w1 = A["moe_w1"][0].rearrange("e r n -> (e r) n")
            w3 = A["moe_w3"][0].rearrange("e r n -> (e r) n")
            w2 = A["moe_w2"][0].rearrange("e r n -> (e r) n")
            sp.wait_ge(sem("rounds_ready"), 2)
            with sp.Fori(0, EXPERTS) as g:
                e = sp.value_load(small_i[0:1, bass.ds(g, 1)], min_val=0, max_val=EXPERTS - 1)
                for i, (kind, c, h) in enumerate(moe_tiles):
                    if i < RING:
                        sp.wait_ge(sa.done, moe_first + i - RING + 1)
                    sp.wait_ge(sem("w_lo"), g * HALVES + (LO_FREE + 2 * (i - RING) + 2))
                    if kind == "w2":
                        src = w2[bass.ds(e * FFE + (BANK * c + 256 * h), 256), :]
                    else:
                        src = (w1 if kind == "w1" else w3)[bass.ds(e * D + BANK * h, BANK), BANK * c:BANK * (c + 1)]
                    k = 2 if kind == "w2" else 4
                    j = moe_first + i
                    sp.dma_start(cols_of(j, k), src.rearrange("(k p) n -> p k n", p=P)).then_inc(sa.landed[j % RING], 16)

        def moe_pool(pool, gain):
            gain("moe", A["norm_g"][1, 1])
            pool.wait_ge(sem("x_ready"), 3)
            pool.dma_start(WR, A["w_router"]).then_inc(sem("route_landed"), 16)
            pool.dma_start(BR8, bcast(A["b_router"][0])).then_inc(sem("route_landed"), 16)
            pool.dma_start(IOTA, A["t_iota"]).then_inc(sem("route_landed"), 16)
            pool.dma_start(BEFORE, A["t_before"]).then_inc(sem("route_landed"), 16)
            gain("fin0", A["final_g"])

        def moe_tensor(pe):
            pe.wait_ge(sem("route_landed"), 64)
            for t in range(TT):
                for k in range(KD):
                    mm = pe.matmul(PS[0][:, 8 * t:8 * t + 8], HT[:, k, P * t:P * t + P], WR[:, k, :], start=k == 0, stop=k == KD - 1)
            mm.then_inc(sem("logits_done"), 1)
            pe.wait_ge(sem("mask_ready"), 1)
            pe.matmul(PS[1][:, 0:8], BEFORE, MASK[:, 0, :], start=True, stop=True)
            pe.matmul(PS[1][:, 8:16], BEFORE, MASK[:, 1, :], start=True, stop=False)
            pe.matmul(PS[1][:, 8:16], ones[:, :], MASK[:, 0, :], start=False, stop=True)
            pe.matmul(PS[1][:, 16:24], ones[:, :], MSUM, start=True, stop=True).then_inc(sem("count_done"), 1)
            pe.matmul(PS[4][:, 0:1], ident[:, :], ones[:, 0:1], start=True, stop=True).then_inc(sem("w_used"), USED_FREE)

            def gather(u, done):
                for k in range(KD):
                    for t in range(TT):
                        mm = pe.matmul(PS[k // 4][:, P * (k % 4):P * (k % 4) + P], H[:, t, P * k:P * k + P], PM[u][:, t, :],
                                       start=t == 0, stop=t == TT - 1)
                mm.then_inc(sem(done), 1)

            def turn_gates(u, done):
                for t in range(TT):
                    mm = pe.transpose(PS[2 + u][:, P * t:P * t + P], PG[u][:, t, :], ident[:, :])
                mm.then_inc(sem(done), 1)

            pe.wait_ge(sem("pick_ready"), 4)
            gather(0, "gather_done")
            turn_gates(0, "gate_turned")
            for i in range(4):
                mm = pe.matmul(bank(4 + i), PGT[0][:, 0:P], H[:, 0, 0:BANK], start=True, stop=True)
            mm.then_inc(sem("scattered"), 1)

            def body(g, groups, j):
                def product(kind, c, q, out_banks, high, low):
                    half = half_of(kind, c, q)
                    w_high, w_low = WH[half % SPLIT], WL[half % SPLIT]
                    pe.wait_ge(sem("w_lo"), g * HALVES + (LO_FREE + half + 1))
                    for u in range(groups):
                        for s in range(2):
                            if kind == "w2":
                                k, n = q, s
                                first, last = c == 0 and q == 0, c == MOE_CHUNKS - 1 and q == 3
                            else:
                                k, n = 2 * q + s, 0
                                first, last = k == 0, k == KD - 1
                            cols = slice(BANK * s, BANK * s + BANK)
                            o = bank(out_banks[u] + n)
                            pe.matmul(o, low[u][:, k, :], w_high[:, cols], start=first, stop=False)
                            pe.matmul(o, high[u][:, k, :], w_high[:, cols], start=False, stop=False)
                            mm = pe.matmul(o, high[u][:, k, :], w_low[:, cols], start=False, stop=last)
                    mm.then_inc(sem("w_used"), 1)

                pe.wait_ge(sem("xg_high"), g + 1)
                pe.wait_ge(sem("xg_low"), g + 1)
                if groups == 2:
                    gather(1, "gather1_done")
                    turn_gates(1, "gate1_turned")
                    pe.wait_ge(sem("xg1_high"), j + 1)
                    pe.wait_ge(sem("xg1_low"), j + 1)
                for c in range(MOE_STEPS):
                    if c < MOE_CHUNKS:
                        if c:
                            pe.wait_ge(sem("moe_silu"), g * MOE_CHUNKS + c)
                        for q in range(4):
                            product("w1", c, q, [0, 1], XGH, XGL)
                    if c == MOE_CHUNKS:
                        pe.wait_ge(sem("moe_silu"), g * MOE_CHUNKS + c)
                        pe.wait_ge(sem("pick_ready"), g * 4 + 8)
                        gather(0, "gather_done")
                    if 1 <= c <= MOE_CHUNKS:
                        pe.wait_ge(sem("moe_hid"), g * MOE_CHUNKS + c)
                        for u in range(groups):
                            for q in range(4):
                                mm = pe.transpose(PS[2 + u][:, P * q:P * q + P], MS[(c - 1) % 2][u][:, P * q:P * q + P], ident[:, :])
                        mm.then_inc(sem("moe_turned"), 1)
                    if c >= 2:
                        if c == 2:
                            pe.wait_ge(sem("x_added"), g + 1)
                        if c == MOE_STEPS - 1:
                            pe.wait_ge(sem("hid_low"), g * MOE_CHUNKS + MOE_CHUNKS)
                            turn_gates(0, "gate_turned")
                        pe.wait_ge(sem("hid_low"), g * MOE_CHUNKS + (c - 1))
                        for q in range(4):
                            product("w2", c - 2, q, [4, 6], MHTH[c % 2], MHTL[c % 2])
                    if c < MOE_CHUNKS:
                        if c == 0:
                            pe.wait_ge(sem("pgt_ready"), g + 1)
                            if groups == 2:
                                pe.wait_ge(sem("pgt1_ready"), j + 1)
                        else:
                            pe.wait_ge(sem("hid_low"), g * MOE_CHUNKS + c)
                        for q in range(4):
                            product("w3", c, q, [2, 3], XGH, XGL)
                pe.wait_ge(sem("ye_ready"), g + 1)
                for t in range(TT):
                    for n in range(2):
                        for u in range(groups):
                            mm = pe.matmul(bank(4 + 2 * t + n), PGT[u][:, P * t:P * t + P], YE[u][:, BANK * n:BANK * n + BANK],
                                           start=u == 0, stop=u == groups - 1)
                mm.then_inc(sem("scattered"), 1)

            all_rounds(pe, body)
            pe.wait_ge(sem("xg_low"), EXPERTS + 1)

        def moe_scalar(act, ch):
            act.wait_ge(sem("top_ready"), 1)
            for t in range(TT):
                ch.step(act.activation(PW[:, 1, t:t + 1], M8[:, t, 1:2], ACT.Exp, bias=PW[:, 0, t:t + 1]), sem("pair_exp"))

            def tokens_high(u, done):
                act.activation(XGH[u][:, 0:4, :], bank(0, 4), ACT.Copy)
                act.activation(XGH[u][:, 4:8, :], bank(1, 4), ACT.Copy).then_inc(sem(done), 1)

            act.wait_ge(sem("gather_done"), 1)
            tokens_high(0, "xg_high")

            def body(g, groups, j):
                def split(kind, c, first=0, last=4):
                    for q in range(first, last):
                        half = half_of(kind, c, q)
                        i = moe_first + half // 2
                        if half % 2 == 0:
                            act.wait_ge(sa.landed[i % RING], g * (16 * NT // RING) + 16 * (i // RING + 1))
                        used_wait(act, g, half - SPLIT)
                        act.activation(WH[half % SPLIT][:, :], slot(i)[:, HALF * (half % 2):HALF * (half % 2) + HALF], ACT.Copy)\
                            .then_inc(sem("w_high"), 1)

                def silu(c):
                    if c < MOE_CHUNKS:
                        used_wait(act, g, half_of("w1", c, 3))
                        if c >= 2:
                            act.wait_ge(sem("moe_turned"), g * MOE_CHUNKS + (c - 1))
                        for u in range(groups):
                            ins = act.activation(MS[c % 2][u], bank(u), ACT.Silu)
                        ins.then_inc(sem("moe_silu"), 1)

                def hidden_high(c):
                    if 1 <= c <= MOE_CHUNKS:
                        act.wait_ge(sem("moe_turned"), g * MOE_CHUNKS + c)
                        if c >= 3:
                            used_wait(act, g, half_of("w2", c - 3, 3))
                        for u in range(groups):
                            ins = act.activation(MHTH[(c - 1) % 2][u][:, :, :], bank(2 + u, 4), ACT.Copy)
                        ins.then_inc(sem("hid_high"), 1)

                if groups == 2:
                    act.wait_ge(sem("gather1_done"), j + 1)
                    tokens_high(1, "xg1_high")
                for c in range(MOE_STEPS):
                    if c < MOE_CHUNKS:
                        split("w1", c)
                    if c >= 2:
                        split("w2", c - 2)
                        if c == MOE_CHUNKS:
                            used_wait(act, g, half_of("w3", MOE_CHUNKS - 1, 3))
                            act.wait_ge(sem("gather_done"), g + 2)
                            tokens_high(0, "xg_high")
                        silu(c)
                        hidden_high(c)
                    if c == 1:
                        split("w3", c, 0, 2)
                        hidden_high(c)
                        split("w3", c, 2, 4)
                    elif c < MOE_CHUNKS:
                        split("w3", c)
                    if c < 2:
                        silu(c)

            all_rounds(act, body)

        def moe_vector(dve, ch):
            link = ch.link
            dve.wait_ge(sem("logits_done"), 1)
            dve.wait_ge(sem("route_landed"), 64)
            for t in range(TT):
                link(dve.tensor_tensor(out=LG[:, t, :], in0=PS[0][:, 8 * t:8 * t + 8], in1=BR8, op=ALU.add))
                link(dve.max(M8[:, t, :], LG[:, t, :]))
                link(dve.max_index(IDX[:, t, :], M8[:, t, :], LG[:, t, :]))
                link(dve.tensor_copy(IDXF[:, t, :], IDX[:, t, :]))
                for j in range(2):
                    link(dve.tensor_scalar(OH[j][:, t, :], IOTA[:, 0:EXPERTS], IDXF[:, t, j:j + 1], None, ALU.is_equal))
            link(dve.tensor_scalar(PW[:, 0, :], M8[:, :, 0], -1.0, None, ALU.mult), sem("top_ready"))
            link(dve.tensor_tensor(out=MASK, in0=OH[0], in1=OH[1], op=ALU.add))
            link(dve.tensor_tensor(out=MSUM, in0=MASK[:, 0, :], in1=MASK[:, 1, :], op=ALU.add), sem("mask_ready"))
            dve.wait_ge(sem("pair_exp"), 2)
            link(dve.tensor_scalar(PW[:, 2, :], PW[:, 1, :], 1.0, None, ALU.add))
            link(dve.reciprocal(PW[:, 3, :], PW[:, 2, :]))
            link(dve.tensor_tensor(out=PW[:, 4, :], in0=PW[:, 3, :], in1=PW[:, 1, :], op=ALU.mult))
            for t in range(TT):
                link(dve.tensor_scalar(GT1[:, t, :], OH[0][:, t, :], PW[:, 3, t:t + 1], None, ALU.mult))
                link(dve.scalar_tensor_tensor(out=GATE[:, t, :], in0=OH[1][:, t, :],
                                              scalar=PW[:, 4, t:t + 1], in1=GT1[:, t, :], op0=ALU.mult, op1=ALU.add))
            link(dve.memset(GATE_R[:, :, E8:COLS], 0.0))
            link(dve.memset(SLOT_R[:, :, E8:COLS], -1.0))
            link(dve.memset(PGT[0], 0.0))
            dve.memset(YE[0][:, 0:1], 0.0).then_inc(sem("w_lo"), LO_FREE)
            dve.wait_ge(sem("count_done"), 1)
            for t in range(TT):
                link(dve.scalar_tensor_tensor(out=SLOT[:, t, :], in0=PS[1][:, 8 * t:8 * t + 8], scalar=1.0, in1=MASK[:, t, :],
                                              op0=ALU.add, op1=ALU.mult))
                link(dve.tensor_scalar(SLOT[:, t, :], SLOT[:, t, :], -1.0, None, ALU.add))
            iota8 = IOTA[:, 0:E8]
            link(dve.tensor_scalar(OVER, PS[1][:, 16:24], P + 0.5, None, ALU.is_gt))
            link(dve.tensor_tensor_scan(OVER_N, ones[:, 0:E8], OVER, 0.0, ALU.mult, ALU.add))
            link(dve.tensor_tensor(out=FROM_E, in0=iota8, in1=OVER_N, op=ALU.subtract))
            link(dve.tensor_tensor(out=POS, in0=OVER_N, in1=FROM_E, op=ALU.subtract))
            link(dve.tensor_scalar(POS, POS, OVER_N[:, E8 - 1:E8], float(E8 - 1), ALU.subtract, ALU.add))
            link(dve.tensor_tensor(out=POS, in0=POS, in1=OVER, op=ALU.mult))
            link(dve.tensor_tensor(out=POS, in0=POS, in1=FROM_E, op=ALU.add))
            link(dve.tensor_tensor(out=AT_POS, in0=over(POS, E8), in1=along(iota8, E8), op=ALU.is_equal))

            def by_round(dst, values):
                link(dve.tensor_tensor(out=AT_TMP, in0=AT_POS, in1=over(values, E8), op=ALU.mult))
                link(dve.tensor_reduce(dst, AT_TMP, AX.X, ALU.add))

            by_round(EIDF[:, 0:E8], iota8)
            link(dve.tensor_scalar(EIDF[:, E8 + 1:E8 + 2], OVER_N[:, E8 - 1:E8], 1.0, None, ALU.max))
            link(dve.tensor_scalar(EIDF[:, E8:E8 + 1], EIDF[:, E8 + 1:E8 + 2], -1.0, float(E8), ALU.mult, ALU.add))
            link(dve.tensor_copy(small_i[:, 0:E8], EIDF[:, 0:E8]), sem("rounds_ready"))
            link(dve.tensor_copy(small_i[:, E8:E8 + 2], EIDF[:, E8:E8 + 2]), sem("rounds_ready"))
            for t in range(TT):
                by_round(SLOT_R[:, t, 0:E8], SLOT[:, t, :])
                by_round(GATE_R[:, t, 0:E8], GATE[:, t, :])

            def pick(lk, col):
                for t in range(TT):
                    lk(dve.tensor_copy(CUR[:, t:t + 1], SLOT_R[:, t, col]))
                    lk(dve.tensor_copy(CUR[:, 4 + t:5 + t], GATE_R[:, t, col]))
                    lk(dve.tensor_scalar(CUR[:, 2 + t:3 + t], CUR[:, t:t + 1], float(-P), None, ALU.add))
                for u in range(2):
                    for t in range(TT):
                        i = 2 * u + t
                        lk(dve.tensor_scalar(PG[u][:, t, :], IOTA, CUR[:, i:i + 1], CUR[:, 4 + t:5 + t], ALU.is_equal, ALU.mult))
                        dve.tensor_scalar(PM[u][:, t, :], IOTA, CUR[:, i:i + 1], None, ALU.is_equal).then_inc(sem("pick_ready"), 1)

            PICK_LINKS = 10

            def tokens_low(u, done):
                dve.tensor_tensor(out=XGL[u][:, 0:4, :], in0=bank(0, 4), in1=XGH[u][:, 0:4, :], op=ALU.subtract)
                dve.tensor_tensor(out=XGL[u][:, 4:8, :], in0=bank(1, 4), in1=XGH[u][:, 4:8, :], op=ALU.subtract).then_inc(sem(done), 1)

            pick(link, slice(0, 1))
            dve.wait_ge(sem("xg_high"), 1)
            tokens_low(0, "xg_low")

            def add_round(g):
                dve.wait_ge(sem("scattered"), g + 1)
                for t in range(TT):
                    for n in range(2):
                        x = X[:, t, BANK * n:BANK * n + BANK]
                        ins = dve.tensor_tensor(out=x, in0=x, in1=bank(4 + 2 * t + n), op=ALU.add)
                ins.then_inc(sem("x_added"), 1)

            def body(g, groups, j):
                lc = LoopChain(dve, sem("moe_chain"), g, PICK_LINKS)

                def split(kind, c, first=0, last=4):
                    for q in range(first, last):
                        half = half_of(kind, c, q)
                        i = moe_first + half // 2
                        dve.wait_ge(sem("w_high"), g * HALVES + (half + 1))
                        dve.tensor_tensor(out=WL[half % SPLIT][:, :], in0=slot(i)[:, HALF * (half % 2):HALF * (half % 2) + HALF],
                                          in1=WH[half % SPLIT][:, :], op=ALU.subtract).then_inc(sem("w_lo"), 1)

                def hidden_low(c):
                    dve.wait_ge(sem("hid_high"), g * MOE_CHUNKS + (c + 1))
                    for u in range(groups):
                        ins = dve.tensor_tensor(out=MHTL[c % 2][u][:, :, :], in0=bank(2 + u, 4), in1=MHTH[c % 2][u][:, :, :], op=ALU.subtract)
                    ins.then_inc(sem("hid_low"), 1)

                if groups == 2:
                    dve.wait_ge(sem("xg1_high"), j + 1)
                    tokens_low(1, "xg1_low")
                for c in range(MOE_STEPS):
                    if c < MOE_CHUNKS:
                        split("w1", c)
                    if c == 0:
                        add_round(g)
                        dve.wait_ge(sem("gate_turned"), g + 1)
                        dve.tensor_copy(PGT[0], PS[2][:, 0:SEQ]).then_inc(sem("pgt_ready"), 1)
                        if groups == 2:
                            dve.wait_ge(sem("gate1_turned"), j + 1)
                            dve.tensor_copy(PGT[1], PS[3][:, 0:SEQ]).then_inc(sem("pgt1_ready"), 1)
                    if 1 <= c <= MOE_CHUNKS:
                        used_wait(dve, g, half_of("w3", c - 1, 3))
                        dve.wait_ge(sem("moe_silu"), g * MOE_CHUNKS + c)
                        for u in range(groups):
                            m = MS[(c - 1) % 2][u]
                            ins = dve.tensor_tensor(out=m, in0=m, in1=bank(2 + u), op=ALU.mult)
                        ins.then_inc(sem("moe_hid"), 1)
                    if c >= 2:
                        split("w2", c - 2)
                        if c == MOE_CHUNKS:
                            dve.wait_ge(sem("xg_high"), g + 2)
                            tokens_low(0, "xg_low")
                        if c <= MOE_CHUNKS:
                            hidden_low(c - 1)
                    if c == 1:
                        split("w3", c, 0, 2)
                        hidden_low(0)
                        split("w3", c, 2, 4)
                    elif c < MOE_CHUNKS:
                        split("w3", c)
                    if c == 3:
                        dve.wait_ge(sem("gate_turned"), g + 1)
                        if groups == 2:
                            dve.wait_ge(sem("gate1_turned"), j + 1)
                        pick(lc.link, bass.ds(g + 1, 1))
                used_wait(dve, g, HALVES - 1)
                for u in range(groups):
                    for n in range(2):
                        c = slice(BANK * n, BANK * n + BANK)
                        ins = dve.tensor_tensor(out=YE[u][:, c], in0=bank(4 + 2 * u + n), in1=ada_part(5)[:, c], op=ALU.mult)
                ins.then_inc(sem("ye_ready"), 1)
                dve.wait_ge(sem("x_added"), g + 1)

            all_rounds(dve, body)
            add_round(EXPERTS)
            dve.wait_ge(sem("x_added"), 1 + EXPERTS)

        RT = at(0, RET_HEADS, 384)
        RCOS, RSIN = at(1536, SEQ), at(1792, SEQ)
        RM = [at(2048 + 512 * i, 2, SEQ) for i in range(2)]
        QR = at(3072, 2 * RET_HEADS, SEQ)
        KR = at(5120, 2 * RET_HEADS, SEQ)
        RV = at(7168, TT, RET_HEADS, RET_DV)
        SG = at(11264, TT, RET_HEADS, RET_DV)
        RS = [at(15360 + 384 * i, 384) for i in range(2)]
        RON = at(16128, BANK)
        OTT = at(16640, 4 * RET_HEADS, SEQ)
        RPOS = at(7168, SEQ).bitcast(I32)
        RANG = [at(7424 + 256 * i, SEQ) for i in range(4)]
        INVF = at(8448, 1)
        RXT = at(2048, BANK)

        UT = at(0, KD, SEQ)
        SBR, SBI = at(2048, KD, P), at(3072, KD, P)
        SCR, SCI = at(4096, S5_TILES, 32), at(5120, S5_TILES, 32)
        CFR, CFI = at(6144, S5_TILES, 32), at(7168, S5_TILES, 32)
        STMP = at(20160, S5_TILES, 32)
        SP = at(8192, 16, S5_TILES)
        EK = at(8704, 2, 9, S5_TILES)
        EA = at(11840, 4, 9, S5_TILES)
        TC, TS = at(11840, 8, SEQ), at(13888, 8, SEQ)
        STEP = 16
        TMP_T = [at(9280 + 256 * i, SEQ // STEP, STEP) for i in range(2)]
        CAB, SAB = at(9792, 2, S5_TILES, STEP), at(10816, 2, S5_TILES, STEP)
        SM = [at(18112 + 512 * i, 2, SEQ) for i in range(2)]
        SV = at(17408, 2, SEQ)
        SW = [at(o, 2, SEQ) for o in (19136, 19648, 16384, 16896)]
        SQ = [[at(20160 + 1024 * i + 512 * j, 2, SEQ) for j in range(2)] for i in range(2)]
        NCFR = SCR
        S5_AHEAD, S5_BANKS = 4, [0, 1, 4, 5]
        S5_TABLES, TABLE_AHEAD = 8, 4
        DVE_TABLES = [j for j in range(S5_TABLES, S5_TILES) if j % 8 in (0, 1, 3, 5, 6)]
        TMP_D = [at(5120 + 256 * i, SEQ // STEP, STEP) for i in range(2)]

        def s5_table(eng, j):
            on_dve = j in DVE_TABLES
            done, tmp = (sem("s5_table_d"), TMP_D) if on_dve else (sem("s5_table_p"), TMP_T)
            built = sum((i in DVE_TABLES) == on_dve for i in range(j))
            grid = [v[:, j % S5_TABLES, :].rearrange("p (a b) -> p a b", b=STEP) for v in (TC, TS)]
            ca, sa16 = along(CAB[:, 0, j, :], STEP), along(SAB[:, 0, j, :], STEP)
            cb, sb1 = over(CAB[:, 1, j, :], SEQ // STEP), over(SAB[:, 1, j, :], SEQ // STEP)
            if built:
                eng.wait_ge(done, 2 * built)
            eng.tensor_tensor(out=grid[0], in0=ca, in1=cb, op=ALU.mult)
            eng.tensor_tensor(out=tmp[0], in0=sa16, in1=sb1, op=ALU.mult)
            eng.tensor_tensor(out=grid[1], in0=sa16, in1=cb, op=ALU.mult)
            eng.tensor_tensor(out=tmp[1], in0=ca, in1=sb1, op=ALU.mult).then_inc(done, 1)
            eng.wait_ge(done, 2 * built + 1)
            eng.tensor_tensor(out=grid[0], in0=grid[0], in1=tmp[0], op=ALU.subtract)
            eng.tensor_tensor(out=grid[1], in0=grid[1], in1=tmp[1], op=ALU.add).then_inc(done, 1)

        def table_ready(eng, j):
            on_dve = sum(i in DVE_TABLES for i in range(j + 1))
            eng.wait_ge(sem("s5_table_p"), 2 * (j + 1 - on_dve))
            if on_dve:
                eng.wait_ge(sem("s5_table_d"), 2 * on_dve)

        S5Y = HT
        SU = at(5632, SEQ)
        GLS = at(4096, BANK)
        GLT = at(4608, BANK)

        def b2_pool(pool, ch, gain, ada_start):
            pool.wait_ge(sem("x_ready"), 4)
            pool.dma_start(RT, A["t_ret"]).then_inc(sem("ret_landed"), 16)
            pool.dma_start(INVF, A["t_inv_freq"]).then_inc(sem("ret_landed"), 16)
            pool.dma_start(RPOS, bcast(A["pos_2"][0])).then_inc(sem("ret_landed"), 16)
            pool.wait_ge(sem("x_ready"), 5)
            ada_start(3, A["ada_b_2"][1:2])
            pool.wait_ge(sem("s5_trig"), 3)
            pool.memset(CAB[:, :, :, 0:1], 1.0)
            ch.link(pool.memset(SAB[:, :, :, 0:1], 0.0))
            for k in range(4):
                n = 2 ** k
                for i, kk in ((0, k + 4), (1, k)):
                    ck, sk = along(EK[:, 0, kk, :], n), along(EK[:, 1, kk, :], n)
                    a, b = (TMP_T[m].rearrange("p a b -> p (a b)")[:, 0:S5_TILES * n].rearrange("p (a b) -> p a b", b=n) for m in range(2))
                    c0, s0, c1, s1 = CAB[:, i, :, 0:n], SAB[:, i, :, 0:n], CAB[:, i, :, n:2 * n], SAB[:, i, :, n:2 * n]
                    pool.tensor_tensor(out=a, in0=s0, in1=sk, op=ALU.mult)
                    pool.tensor_tensor(out=c1, in0=c0, in1=ck, op=ALU.mult)
                    pool.tensor_tensor(out=b, in0=c0, in1=sk, op=ALU.mult)
                    ch.link(pool.tensor_tensor(out=s1, in0=s0, in1=ck, op=ALU.mult))
                    pool.tensor_tensor(out=c1, in0=c1, in1=a, op=ALU.subtract)
                    ch.link(pool.tensor_tensor(out=s1, in0=s1, in1=b, op=ALU.add))

            for j in range(S5_TABLES):
                s5_table(pool, j)
            pool.wait_ge(sem("x_ready"), 6)
            pool.dma_start(SBR, A["s5_b_re"]).then_inc(sem("s5_landed"), 16)
            pool.dma_start(SBI, A["s5_b_im"]).then_inc(sem("s5_landed"), 16)
            pool.dma_start(SCR, A["s5_c_re"]).then_inc(sem("s5_landed"), 16)
            pool.dma_start(SCI, A["s5_c_im"]).then_inc(sem("s5_landed"), 16)
            for j in range(S5_TILES):
                q, b = j % S5_TABLES, j % 2
                pool.wait_ge(sem("s5_w"), j + 1)
                if j >= 2:
                    pool.wait_ge(sem("s5_y"), j - 1)
                table_ready(pool, j)
                pool.tensor_tensor(out=SQ[b][0], in0=SW[j % 4], in1=over(TC[:, q, :], 2), op=ALU.mult)
                pool.tensor_tensor(out=SQ[b][1], in0=SW[j % 4], in1=over(TS[:, q, :], 2), op=ALU.mult).then_inc(sem("s5_s"), 1)
                new = j + TABLE_AHEAD
                if S5_TABLES <= new < S5_TILES and new not in DVE_TABLES:
                    s5_table(pool, new)
            gain("fin1", A["final_norm_g_2"])

        def ret_turn_evac(act, ch, h):
            for t in range(TT):
                act.wait_ge(sem("ret_turned"), 2 * h + t + 1)
                ch.step(act.activation(OTT[:, 4 * h:4 * h + 4, P * t:P * t + P], bank(4 + t, 4), ACT.Copy), sem("ott_ready"))


        def s5_angles(dve, tt, ts, to_period):
            dt, th, lrdt, t0 = (SP[:, i, :] for i in (0, 1, 2, 10))
            dve.wait_ge(sem("s5_dt"), 1)
            tt(th, lam_im, dt, ALU.mult)
            tt(lrdt, lam_re, dt, ALU.mult)
            to_period(EA[:, 0, 0, :], th, t0, 0, None)
            for k in range(1, 9):
                ts(EA[:, 0, k, :], EA[:, 0, 0, :], float(2 ** k), None, ALU.mult)
            to_period(EA[:, 2], EA[:, 0], EA[:, 1], 0, None)
            to_period(EA[:, 3], EA[:, 0], EA[:, 1], 1, sem("s5_arg"))

        def s5_vector(dve, ch, tt, ts, stt, to_period, gain_of, scale_shift, turn_evac, ada_evac):
            link = ch.link
            mag, ar, ai, nr, den, fr, fi, t0, t1 = (SP[:, i, :] for i in range(3, 12))
            ada_evac(3)
            gain_of("s5", "scale", ada_part(1))
            scale_shift("s5", X, ada_part(0))
            turn_evac("s5", HT)
            dve.wait_ge(sem("s5_trig"), 3)
            tt(ar, mag, EK[:, 0, 0, :], ALU.mult)
            tt(ai, mag, EK[:, 1, 0, :], ALU.mult)
            ts(nr, ar, -1.0, None, ALU.add)
            tt(den, lam_re, lam_re, ALU.mult)
            tt(t0, lam_im, lam_im, ALU.mult)
            tt(den, den, t0, ALU.add)
            link(dve.reciprocal(den, den))
            tt(t0, nr, lam_re, ALU.mult)
            tt(t1, ai, lam_im, ALU.mult)
            tt(fr, t0, t1, ALU.add)
            tt(fr, fr, den, ALU.mult)
            tt(t0, ai, lam_re, ALU.mult)
            tt(t1, nr, lam_im, ALU.mult)
            tt(fi, t0, t1, ALU.subtract)
            tt(fi, fi, den, ALU.mult)
            dve.wait_ge(sem("s5_landed"), 64)
            tt(CFI, SCR, along(fi, 32), ALU.mult)
            tt(STMP, SCI, along(fr, 32), ALU.mult)
            stt(CFI, CFI, -1.0, STMP, ALU.mult, ALU.subtract, sem("s5_c"))
            tt(CFR, SCR, along(fr, 32), ALU.mult)
            tt(STMP, SCI, along(fi, 32), ALU.mult)
            tt(CFR, CFR, STMP, ALU.subtract, sem("s5_c"))
            ts(NCFR, CFR, -1.0, None, ALU.mult, s=sem("s5_c"))

            def skip_term(k):
                dve.wait_ge(sem("s5_y"), 4 * (k + 1))
                if k:
                    dve.wait_ge(sem("s5_gelu"), k)
                stt(SU, UT[:, k, :], s5_d[:, k:k + 1], PS[2 + k % 2][:, 0:SEQ], ALU.mult, ALU.add, sem("s5_du"))

            for j in range(S5_TILES):
                q = j % S5_TABLES
                dve.wait_ge(sem("s5_bu"), j + 1)
                table_ready(dve, j)
                bu = bank(S5_BANKS[j % S5_AHEAD], 2)
                dve.tensor_tensor(out=SM[0], in0=bu, in1=over(TC[:, q, :], 2), op=ALU.mult)
                tt(SM[1], bu, over(TS[:, q, :], 2), ALU.mult, sem("s5_rot"))
                if j:
                    dve.wait_ge(sem("s5_w"), j)
                dve.tensor_tensor(out=SV[:, 0, :], in0=SM[0][:, 0, :], in1=SM[1][:, 1, :], op=ALU.add)
                tt(SV[:, 1, :], SM[0][:, 1, :], SM[1][:, 0, :], ALU.subtract)
                if j >= 4:
                    dve.wait_ge(sem("s5_s"), j - 3)
                for s in range(2):
                    ins = dve.tensor_tensor_scan(SW[j % 4][:, s, :], mag[:, j:j + 1].to_broadcast([P, SEQ]), SV[:, s, :], 0.0,
                                                 ALU.mult, ALU.add)
                ins.then_inc(sem("s5_w"), 1)
                if j + TABLE_AHEAD in DVE_TABLES:
                    s5_table(dve, j + TABLE_AHEAD)
                if j % 4 == 1 and j > 4:
                    skip_term(j // 4 - 1)
            skip_term(KD - 1)
            gain_of("cf1", "scale", ada_part(4))
            for t in range(TT):
                for n in range(2):
                    c = slice(BANK * n, BANK * n + BANK)
                    dve.wait_ge(sem("glu_sig"), 2 * t + n + 1)
                    tt(GLT, bank(4 * t + n), GLS, ALU.mult, sem("glu_used"))
                    tt(GLT, GLT, AD[:, 2 * D + BANK * n:2 * D + BANK * n + BANK], ALU.mult)
                    tt(X[:, t, c], X[:, t, c], GLT, ALU.add, sem("x_ready") if t + n == 2 else None)
        block = ctx.enter_context(nc.Block())

        @block.sync
        def _(sp):
            def load(st, i, after=None):
                if i >= RING:
                    sp.wait_ge(st.done, i - RING + 1)
                name, src, k = st.items[i]
                sp.dma_start(slot(i).rearrange("p (k n) -> p k n", k=k),
                             src.rearrange("(k p) n -> p k n", p=P)).then_inc(st.landed[i % RING], 16)

            def load_ada(i):
                a, n, q = ADA_HALVES[i]
                if i >= ADA_SLOTS:
                    sp.wait_ge(sem("ada_added"), i - ADA_SLOTS + 1)
                sp.dma_start(ADA_RING[a][:, i % ADA_SLOTS],
                             ADA_W[a][256 * q:256 * (q + 1), BANK * n:BANK * (n + 1)].rearrange("(k p) n -> p k n", p=P))\
                    .then_inc(sem(f"ada_landed{i % ADA_SLOTS}"), 16)

            def load_with_ada(st, i, base, plan, x_count):
                load(st, i)
                halves = [k for k, after in plan.items() if after == i - base]
                if halves and i - base == RING - 1:
                    sp.wait_ge(sem("x_ready"), x_count)
                for k in halves:
                    load_ada(k)

            ffn_tiles = range(sa.first["ffn_up"], sa.first["four"])
            for i in range(len(sa.items)):
                if i in ffn_tiles:
                    load_with_ada(sa, i, ffn_tiles[0], ADA_PLAN["ffn"], 1)
                else:
                    load(sa, i)
            moe_sync(sp)
            sp.wait_ge(sem("w_lo"), LO_FREE + EXPERTS * HALVES)
            cf_tiles = range(sbm.first["cf_up0"], sbm.first["s5_in"])
            for i in range(len(sbm.items)):
                if i in cf_tiles:
                    load_with_ada(sbm, i, cf_tiles[0], ADA_PLAN["cf0"], 5)
                else:
                    load(sbm, i)
            sp.wait_ge(sem("out_ready"), 1)
            sp.dma_start(out.rearrange("b (t p) d -> p (b t) d", p=P), H[:, :, :]).then_inc(sem("stored"), 16)
            sp.wait_ge(sem("stored"), 16)

        @block.gpsimd
        def _(pool):
            ch = Chain(pool, sem("pool_chain"))
            pool.dma_start(vec[:, :], A["vectors"]).then_inc(sem("vec_landed"), 16)
            pool.dma_start(FW1, A["hy_f_w1"][0]).then_inc(sem("filter_landed"), 16)
            pool.dma_start(FEATS, A["t_feats"]).then_inc(sem("filter_landed"), 16)
            pool.dma_start(FW2, A["hy_f_w2"][0]).then_inc(sem("filter_landed"), 16)
            pool.dma_start(FV, A["filter_vectors"]).then_inc(sem("filter_landed"), 16)
            pool.dma_start(FW3, A["hy_f_w3"][0]).then_inc(sem("filter_landed"), 16)
            pool.dma_start(DEC, A["t_decay"]).then_inc(sem("filter_landed"), 16)
            pool.dma_start(DFTF, A["t_dft_fwd"]).then_inc(sem("filter_landed"), 16)
            pool.dma_start(DFTB, A["t_dft_bwd"]).then_inc(sem("filter_landed"), 16)
            pool.dma_start(IDFT, A["t_idft"]).then_inc(sem("filter_landed"), 16)
            pool.dma_start(ident[:, :], A["t_ident"]).then_inc(sem("ident_landed"), 16)
            pool.dma_start(X[:, :, :], A["x"][0].rearrange("(t p) d -> p t d", p=P)).then_inc(sem("x_landed"), 16)
            pool.dma_start(CX, A["ctx"][0].rearrange("(t p) d -> p t d", p=P)).then_inc(sem("ctx_landed"), 16)
            pool.memset(ones[:, :], 1.0).then_inc(sem("ones_set"), 1)

            def gain(name, row):
                i = GB_LOADS[name]
                if i:
                    pool.wait_ge(sem("gain_used"), GAIN_USES[name])
                pool.dma_start(G[:, :], bcast(row)).then_inc(sem("gain_landed"), 16)

            def ada_bias(row):
                for n in range(ADA_N):
                    if n:
                        pool.wait_ge(sem("ada_evac"), n)
                    pool.dma_start(BB[:, :], bcast(row[BANK * n:BANK * (n + 1)])).then_inc(sem("bias_landed"), 16)

            def ada_start(a, row):
                pool.memset(ADA_ACC[a], 0.0).then_inc(sem("ada_zeroed"), 1)
                pool.wait_ge(sem("ada_zeroed"), a)
                pool.dma_start(ADA_ACC[a][0:1, :], row).then_inc(sem(f"ada_started{a}"), 16)

            gain("hy", A["norm_g"][0, 0])
            ada_bias(A["b_ada"][0])
            gain("ctx", A["norm_g"][0, 0])
            pool.wait_ge(sem("ks_ready"), 8)
            pool.dma_start(WIN, A["t_window"]).then_inc(sem("win_landed"), 16)
            for gi in range(8):
                t, h0 = gi // 4, 4 * (gi % 4)
                if gi >= 2:
                    pool.wait_ge(sem("na_max"), 4 * (gi - 1))
                for rr in range(2):
                    for h in range(4):
                        off = ((h0 + h) * RPB_R + WIN_R - 1 - (2 * t + rr)) * RPB_C + WIN_C - GRID_W
                        src = bass.AP(A["na_rpb"].tensor, off, [[1, GRID_W], [RPB_C, GRID_R], [1, GRID_W]])
                        pool.dma_start(BIA[gi % 2][64 * rr:64 * rr + 64, h], src).then_inc(sem(f"rpb_landed{gi % 2}"), 16)
                if gi == 0:
                    pool.wait_ge(sem("win_landed"), 16)
                pool.wait_ge(sem(f"rpb_landed{gi % 2}"), 128 * (gi // 2 + 1))
                b = BIA[gi % 2].rearrange("p h r k -> p (h r) k")
                pool.tensor_tensor(out=b, in0=b, in1=over(WIN, 4 * GRID_R), op=ALU.add).then_inc(sem("rpb_ready"), 1)
            gain("ffn", A["norm_g"][0, 1])
            pool.wait_ge(sem("x_ready"), 1)
            ada_start(1, A["b_ada"][1:2])
            ada_start(2, A["ada_b_2"][0:1])
            gain("four", A["norm_g"][1, 0])
            pool.wait_ge(sem("x_ready"), 2)
            pool.dma_start(FOD, A["t_four_d"]).then_inc(sem("four_landed"), 16)
            pool.dma_start(FOL, A["t_four_l"]).then_inc(sem("four_landed"), 16)
            moe_pool(pool, gain)
            b2_pool(pool, ch, gain, ada_start)


        @block.tensor
        def _(pe):
            def turn(name):
                i = TURN[name]
                for t in range(TT):
                    pe.wait_ge(sem("norm_h"), 2 * i + t + 1)
                    for half in range(2):
                        for q in range(4):
                            k = 4 * half + q
                            mm = pe.transpose(PS[2 * t + half][:, P * q:P * q + P], H[:, t, P * k:P * k + P], ident[:, :])
                        mm.then_inc(sem("norm_turned"), 1)

            def turned(name):
                i = TURN[name]
                pe.wait_ge(sem("ht_act"), 2 * (i + 1))
                pe.wait_ge(sem("ht_dve"), 2 * (i + 1))

            def ada_chunks(first, last):
                base = sa.first["ada0"]
                for n in range(first, last):
                    if n >= 2:
                        pe.wait_ge(sem("ada_evac"), n - 1)
                    for h in range(2):
                        i = base + 2 * n + h
                        sa.need(pe, i)
                        w = cols_of(i, 4)
                        if n < 4:
                            for k in range(4):
                                pe.matmul(bank(2 + n % 2), CBX[:, 4 * h + k, :], w[:, k, :], start=h + k == 0, stop=h == 1 and k == 3)
                        for k in range(4):
                            mm = pe.matmul(bank(n % 2), CB[:, 4 * h + k, :], w[:, k, :], start=h + k == 0, stop=h == 1 and k == 3)
                        mm.then_inc(sa.done, 1)

            def ada_sum(a):
                pe.wait_ge(sem("ada_added"), 4 * ADA_N * a)
                for n in range(ADA_N):
                    if n >= 4:
                        pe.wait_ge(sem("ada_odd" if n % 2 else "ada_even"), ADA_N // 2 * (a - 1) + n // 2 - 1)
                    pe.matmul(bank(n % 4), ones[:, :], ADA_ACC[a][:, BANK * n:BANK * (n + 1)], start=True, stop=True)\
                        .then_inc(sem("ada_summed"), 1)

            def columns(st, i, b, src):
                w = cols_of(i, 8)
                for m in range(2):
                    for k in range(KD):
                        mm = pe.matmul(PS[b][:, SEQ * m:SEQ * m + SEQ], w[:, k, P * m:P * m + P], src[:, k, :],
                                       start=k == 0, stop=k == KD - 1)
                return mm

            def rows_out(st, name, lhs, tiles, wait=None):
                base = st.first[name]
                for j in range(tiles):
                    if wait:
                        wait(j)
                    i = base + j
                    st.need(pe, i)
                    w = cols_of(i, 2)
                    for t in range(TT):
                        for k in range(2):
                            for n in range(2):
                                mm = pe.matmul(bank(4 + 2 * t + n), lhs(2 * j + k)[:, P * t:P * t + P], w[:, k, BANK * n:BANK * n + BANK],
                                               start=j + k == 0, stop=j == tiles - 1 and k == 1)
                        if j == tiles - 1 and t == 0:
                            mm.then_inc(sem("rows_first"), 1)
                    mm.then_inc(st.done, 1)

            def gated_ffn(st, up, down, hid_base):
                base = st.first[up]
                for j in range(FF // 256):
                    if j >= 2:
                        pe.wait_ge(sem("hid_ready"), hid_base + j - 1)
                    for s in range(2):
                        i = base + 2 * j + s
                        st.need(pe, i)
                        columns(st, i, 2 * (j % 2) + s, HT).then_inc(st.done, 1)
                rows_out(st, down, lambda k: HID[:, k, :], FF // 256,
                         lambda j: pe.wait_ge(sem("hid_ready"), hid_base + j + 1))

            pe.wait_ge(sem("cb_ready"), 2)
            ada_chunks(0, 4)
            pe.wait_ge(sem("filter_landed"), 144)
            pe.matmul(PS[4][0:HY_HID, 0:SEQ], FW1, FEATS, start=True, stop=True).then_inc(sem("filter_h"), 1)
            ada_chunks(4, 5)
            pe.wait_ge(sem("filter_sin"), 1)
            pe.matmul(PS[5][0:HY_HID, 0:SEQ], FW2, FA[3], start=True, stop=True).then_inc(sem("filter_h"), 1)
            ada_chunks(5, 6)
            pe.wait_ge(sem("filter_sin"), 2)
            for t in range(TT):
                for n in range(4):
                    i = 4 * t + n
                    if i >= 4:
                        pe.wait_ge(sem("filter_ready"), i - 3)
                    pe.matmul(bank(4 + i % 4), FA[4][:, P * t:P * t + P], FW3[:, CH * n:CH * n + CH], start=True, stop=True)\
                        .then_inc(sem("filter_raw"), 1)
            ada_chunks(6, 8)
            pe.wait_ge(sem("filter_abs"), 2)
            pe.wait_ge(sem("ones_set"), 1)
            for o in range(2):
                absf = (HT[:, :, :] if o == 0 else H[:, :, :]).rearrange("p a b -> p (a b)").rearrange("p (t d n) -> p t d n", t=TT, d=2)
                for c in range(4):
                    for s in range(4):
                        mm = pe.matmul(PS[4][:, 4 * o + c:4 * o + c + 1], absf[:, s // 2, s % 2, P * c:P * c + P], ones[:, 0:1],
                                       start=s == 0, stop=s == 3)
            mm.then_inc(sem("filter_sum"), 1)
            ada_chunks(8, 9)
            pe.wait_ge(sem("filter_norm"), 1)
            for o in range(2):
                for i in range(4):
                    if o:
                        pe.wait_ge(sem("ks_ready"), i + 1)
                    for s in range(4):
                        basis = DFTF if s < 2 else DFTB
                        mm = pe.matmul(bank(4 + i), basis[:, s % 2, P * i:P * i + P], FH[:, s % 2, 2 * o + s // 2, :], start=s == 0, stop=s == 3)
                    mm.then_inc(sem("ks_done"), 1)
            ada_chunks(9, ADA_N)
            pe.wait_ge(sem("ks_ready"), 8)
            pe.wait_ge(sem("ident_landed"), 16)
            turn("hy")
            pe.wait_ge(sem("ht_act"), 2)
            pe.wait_ge(sem("ht_dve"), 2)
            turn("ctx")
            turned("ctx")
            base = sa.first["hy_in"]
            for j in range(6):
                if j >= 4:
                    pe.wait_ge(sem("zc_ready"), j - 3)
                sa.need(pe, base + j)
                columns(sa, base + j, j % 4, HT).then_inc(sa.done, 1)
            base = sa.first["q_in"]
            for j in range(2):
                sa.need(pe, base + j)
                columns(sa, base + j, 4 + j, HT).then_inc(sa.done, 1)
            base = sa.first["k_in"]
            for j in range(2):
                if j:
                    pe.wait_ge(sem("zc_ready"), 6)
                sa.need(pe, base + j)
                columns(sa, base + j, 6 if j == 0 else 0, HT)
                columns(sa, base + j, 7 if j == 0 else 1, HCT).then_inc(sa.done, 1)
            base = sa.first["v_in"]
            pe.wait_ge(sem("qkv_ready"), 2)
            for h in range(2):
                sa.need(pe, base + h)
                w = cols_of(base + h, 4)
                for s in range(4):
                    src = HT if s < 2 else HCT
                    for k in range(4):
                        mm = pe.matmul(bank(2 + s), src[:, 4 * h + k, P * (s % 2):P * (s % 2) + P], w[:, k, :],
                                       start=h + k == 0, stop=h == 1 and k == 3)
                mm.then_inc(sa.done, 1)
            for o in range(2):
                if o == 0:
                    pe.wait_ge(sem("zc_ready"), 6)
                    pe.wait_ge(sem("qkv_ready"), 10)
                else:
                    pe.wait_ge(sem("hy_out"), 4)
                for t in range(TT):
                    for c in range(4):
                        mm = pe.transpose(PS[t][:, P * c:P * c + P], ZC[:, c, P * t:P * t + P], ident[:, :])
                    mm.then_inc(sem("hy_turned"), 1)
                pe.wait_ge(sem("hy_vt"), 2 * (o + 1))
                for i in range(4):
                    for t in range(TT):
                        mm = pe.matmul(bank(2 + i), DFTF[:, t, P * i:P * i + P], VT[:, t, :], start=t == 0, stop=t == 1)
                mm.then_inc(sem("hy_spec"), 1)
                pe.wait_ge(sem("hy_prod"), o + 1)
                for c in range(4):
                    for i in range(4):
                        mm = pe.matmul(PS[6 + c // 2][:, SEQ * (c % 2):SEQ * (c % 2) + SEQ], YF[:, i, P * c:P * c + P], IDFT[:, i, :],
                                       start=i == 0, stop=i == 3)
                    mm.then_inc(sem("hy_conv"), 1)
            NA = TT * HEADS

            def scores(it):
                t, h = it // HEADS, it % HEADS
                r, c = 32 * (h % 4), h // 4
                if it >= 2:
                    pe.wait_ge(sem("na_max"), it - 1)
                pe.matmul(PS[it % 2][:, 0:SEQ], QT[r:r + 32, c, P * t:P * t + P], KT[r:r + 32, c, :], start=True, stop=True)
                pe.matmul(PS[it % 2][:, SEQ:2 * SEQ], QT[r:r + 32, c, P * t:P * t + P], KCT[r:r + 32, c, :], start=True, stop=True)\
                    .then_inc(sem("na_scores"), 1)

            def weigh(it):
                t, h = it // HEADS, it % HEADS
                pe.wait_ge(sem("na_pt"), it + 1)
                for kc in range(4):
                    v = V if kc < 2 else VC
                    mm = pe.matmul(PS[4 + t][:, 32 * h:32 * h + 32], NPT[it % 2][:, kc, :], v[:, kc % 2, 32 * h:32 * h + 32],
                                   start=kc == 0, stop=kc == 3)
                mm.then_inc(sem("na_out"), 1)

            scores(0)
            for it in range(NA):
                if it + 1 < NA:
                    scores(it + 1)
                pe.wait_ge(sem("na_exp"), it + 1)
                if it >= 2:
                    pe.wait_ge(sem("na_pt"), it - 1)
                for kc in range(4):
                    mm = pe.transpose(PS[2 + it % 2][:, P * kc:P * kc + P], NP[it % 2][:, P * kc:P * kc + P], ident[:, :])
                mm.then_inc(sem("na_turned"), 1)
                if it >= 1:
                    weigh(it - 1)
            weigh(NA - 1)
            pe.wait_ge(sem("hy_out"), 8)
            for t in range(TT):
                pe.wait_ge(sem("na_norm"), t + 1)
                for k in range(4):
                    mm = pe.transpose(PS[6 + t][:, P * k:P * k + P], NO[:, t, P * k:P * k + P], ident[:, :])
                mm.then_inc(sem("na_o_turned"), 1)
            pe.wait_ge(sem("yt_na"), 2)
            rows_out(sa, "mix", lambda k: YT[:, k, :], 4)
            turn("ffn")
            turned("ffn")
            gated_ffn(sa, "ffn_up", "ffn_down", HID_FFN)
            ada_sum(1)
            turn("four")
            turned("four")
            pe.wait_ge(sem("four_landed"), 32)
            for t in range(TT):
                for g in range(4):
                    b = 4 * t + g
                    for k in range(2):
                        mm = pe.matmul(bank(b), HT[:, 2 * g + k, P * t:P * t + P], FOD[:, k, :], start=k == 0, stop=k == 1)
                    mm.then_inc(sem("four_feat"), 1)
            pe.wait_ge(sem("four_ab_act"), 4)
            pe.wait_ge(sem("four_ab_dve"), 4)
            for f in range(KD):
                g, half = f // 2, f % 2
                for s in range(4):
                    t, im = s % 2, s // 2
                    mm = pe.matmul(PS[f // 2][:, SEQ * half:SEQ * half + SEQ],
                                   FAB[:, t, g, SEQ * im + P * half:SEQ * im + P * half + P], FOL[:, im, t, :],
                                   start=s == 0, stop=s == 3)
                if half:
                    mm.then_inc(sem("four_tok"), 1)
            rows_out(sa, "four", lambda k: FYT[:, k, :], 4, lambda j: pe.wait_ge(sem("four_yt"), j + 1))
            turn("moe")
            turned("moe")
            moe_tensor(pe)
            ada_sum(2)
            turn("ret")
            turned("ret")
            base = sbm.first["ret_qk"]
            for j in range(RET_TILES):
                if j >= 2:
                    pe.wait_ge(sem("rot_done"), j - 1)
                sbm.need(pe, base + j)
                columns(sbm, base + j, j % 2, HT).then_inc(sbm.done, 1)
            base = sbm.first["ret_vg"]
            for n in range(8):
                if n >= 2:
                    pe.wait_ge(sem("vg_ready"), 2 * (n - 1))
                for h in range(2):
                    i = base + 2 * n + h
                    sbm.need(pe, i)
                    w = cols_of(i, 4)
                    for t in range(TT):
                        for k in range(4):
                            mm = pe.matmul(bank(2 + 2 * (n % 2) + t), HT[:, 4 * h + k, P * t:P * t + P], w[:, k, :],
                                           start=h + k == 0, stop=h == 1 and k == 3)
                    mm.then_inc(sbm.done, 1)
            pe.wait_ge(sem("rot_out"), RET_TILES)
            pe.wait_ge(sem("vg_ready"), 16)

            def ret_scores(h):
                b = 6 + h % 2
                if h >= 2:
                    pe.wait_ge(sem("ret_decayed"), h - 1)
                for k in range(2):
                    pe.matmul(PS[b][:, 0:SEQ], KR[:, 2 * h + k, 0:P], QR[:, 2 * h + k, :], start=k == 0, stop=k == 1)
                for k in range(2):
                    mm = pe.matmul(PS[b][:, SEQ:SEQ + P], KR[:, 2 * h + k, P:SEQ], QR[:, 2 * h + k, P:SEQ], start=k == 0, stop=k == 1)
                mm.then_inc(sem("ret_scored"), 1)

            def ret_turn(h):
                pe.wait_ge(sem("ret_gated"), 2 * (h + 1))
                for t in range(TT):
                    if h >= 1:
                        pe.wait_ge(sem("ott_ready"), 2 * (h - 1) + t + 1)
                    for q in range(4):
                        mm = pe.transpose(PS[4 + t][:, P * q:P * q + P], SG[:, t, h, P * q:P * q + P], ident[:, :])
                    mm.then_inc(sem("ret_turned"), 1)

            ret_scores(0)
            for h in range(RET_HEADS):
                if h + 1 < RET_HEADS:
                    ret_scores(h + 1)
                pe.wait_ge(sem("ret_decayed"), h + 1)
                if h >= 2:
                    pe.wait_ge(sem("ret_gated"), 2 * (h - 1))
                s = RS[h % 2]
                pe.matmul(bank(2 * (h % 2)), s[:, 0:P], RV[:, 0, h, :], start=True, stop=True)
                pe.matmul(bank(2 * (h % 2) + 1), s[:, P:2 * P], RV[:, 0, h, :], start=True, stop=False)
                pe.matmul(bank(2 * (h % 2) + 1), s[:, 2 * P:3 * P], RV[:, 1, h, :], start=False, stop=True).then_inc(sem("ret_o"), 1)
                if h >= 1:
                    ret_turn(h - 1)
            ret_turn(RET_HEADS - 1)
            pe.wait_ge(sem("ott_ready"), 2 * RET_HEADS)
            rows_out(sbm, "ret_out", lambda k: OTT[:, k, :], 8)
            turn("cf0")
            turned("cf0")
            gated_ffn(sbm, "cf_up0", "cf_down0", HID_CF[0])
            ada_sum(3)
            turn("s5")
            turned("s5")
            base = sbm.first["s5_in"]
            for j in range(4):
                sbm.need(pe, base + j)
                columns(sbm, base + j, 4 + j, HT).then_inc(sbm.done, 1)
            pe.wait_ge(sem("s5_landed"), 64)
            pe.wait_ge(sem("s5_u"), 4)
            pe.wait_ge(sem("s5_c"), 3)

            def s5_in(j):
                r, b = 32 * (j % 4), S5_BANKS[j % S5_AHEAD]
                if j >= S5_AHEAD:
                    pe.wait_ge(sem("s5_rot"), j - S5_AHEAD + 1)
                pe.matmul(PS[b][:, 0:SEQ], SBR[r:r + 32, j // 4, :], UT[r:r + 32, j // 4, :], start=True, stop=True)
                pe.matmul(PS[b][:, SEQ:2 * SEQ], SBI[r:r + 32, j // 4, :], UT[r:r + 32, j // 4, :], start=True, stop=True)\
                    .then_inc(sem("s5_bu"), 1)

            for j in range(S5_AHEAD):
                s5_in(j)
            for j in range(S5_TILES):
                q, r, b = j // 4, 32 * (j % 4), j % 2
                if j % 4 == 0 and q >= 2:
                    pe.wait_ge(sem("s5_du"), q - 1)
                pe.wait_ge(sem("s5_s"), j + 1)
                y = PS[2 + q % 2][r:r + 32, 0:SEQ]
                pe.matmul(y, CFR[:, j, :], SQ[b][0][:, 0, :], start=True, stop=False)
                pe.matmul(y, NCFR[:, j, :], SQ[b][1][:, 1, :], start=False, stop=False)
                pe.matmul(y, CFI[:, j, :], SQ[b][1][:, 0, :], start=False, stop=False)
                pe.matmul(y, CFI[:, j, :], SQ[b][0][:, 1, :], start=False, stop=True).then_inc(sem("s5_y"), 1)
                if j + S5_AHEAD < S5_TILES:
                    s5_in(j + S5_AHEAD)
            pe.wait_ge(sem("s5_gelu"), KD)
            base = sbm.first["glu"]
            for k in range(KD):
                i = base + k
                sbm.need(pe, i)
                for t in range(TT):
                    for n in range(4):
                        mm = pe.matmul(bank(4 * t + n), S5Y[:, k, P * t:P * t + P], slot(i)[:, BANK * n:BANK * n + BANK],
                                       start=k == 0, stop=k == KD - 1)
                    if k == KD - 1 and t == 0:
                        mm.then_inc(sem("rows_first"), 1)
                mm.then_inc(sbm.done, 1)
            turn("cf1")
            turned("cf1")
            gated_ffn(sbm, "cf_up1", "cf_down1", HID_CF[1])

        @block.scalar
        def _(act):
            ch = Chain(act, sem("act_chain"))

            def norm_stats(x, count=None, addition=None):
                ch.step(act.activation(ss[:, 2:3], eps, ACT.Sqrt))
                for t in range(TT):
                    if addition is not None and t == 0:
                        act.wait_ge(sem("x_part"), 3 * addition + 2)
                    elif count is not None:
                        act.wait_ge(sem("x_ready"), count)
                    ch.link(act.activation(H[:, t, :], x[:, t, :], ACT.Square, accum_out=ss[:, t:t + 1]))
                    ch.step(act.activation(std[:, t:t + 1], ss[:, t:t + 1], ACT.Sqrt, scale=1.0 / D, bias=eps), sem("norm_std"))

            def turn_evac(name, dst):
                i = TURN[name]
                for t in range(TT):
                    act.wait_ge(sem("norm_turned"), 4 * i + 2 * t + 1)
                    ch.step(act.activation(dst[:, 0:4, P * t:P * t + P], bank(2 * t, 4), ACT.Copy), sem("ht_act"))

            def ada_evac(a):
                for n in range(1, ADA_N, 2):
                    act.wait_ge(sem("ada_summed"), ADA_N * (a - 1) + n + 1)
                    ch.step(act.activation(AD[:, BANK * n:BANK * (n + 1)], bank(n % 4), ACT.Copy), sem("ada_odd"))

            def gated_ffn(st, up, hid_base, conv=None):
                base = st.first[up]
                for j in range(FF // 256):
                    b = 2 * (j % 2)
                    st.wait_done(act, base + 2 * j)
                    if j >= 2:
                        act.wait_ge(sem("hid_ready"), hid_base + j - 1)
                    if conv is None:
                        ch.step(act.activation(SIL[j % 2], bank(b, 2), ACT.Silu), sem("silu_done"))
                    else:
                        for m in range(2):
                            ch.step(act.activation(GC[j % 2][:, m, :], PS[b][:, SEQ * m:SEQ * m + SEQ], ACT.Identity,
                                                   scale=conv_w[conv][:, 2, 2 * j + m:2 * j + m + 1],
                                                   bias=conv_b[conv][:, 2 * j + m:2 * j + m + 1]), sem("conv_tap"))
                        act.wait_ge(sem("conv_done"), (FF // 256) * conv + j + 1)
                        ch.step(act.activation(SIL[j % 2], GC[j % 2], ACT.Silu), sem("silu_done"))

            act.wait_ge(sem("eps_set"), 1)
            act.wait_ge(sem("vec_landed"), 16)
            ch.step(act.activation(csil, vec[:, 0:24], ACT.Silu), sem("c_silu"))
            for l in range(2):
                act.wait_ge(sem("filter_arg"), l + 1)
                ch.step(act.activation(FA[3 + l], FA[2], ACT.Sin), sem("filter_sin"))
            act.wait_ge(sem("filter_ready"), 9)
            for o in range(2):
                absf = (HT[:, :, :] if o == 0 else H[:, :, :]).rearrange("p a b -> p (a b)").rearrange("p (t n) -> p t n", t=TT)
                fo = FH.rearrange("p t o n -> p t (o n)")[:, :, 2 * CH * o:2 * CH * (o + 1)]
                ch.step(act.activation(absf, fo, ACT.Abs), sem("filter_abs"))
            for i in range(8):
                act.wait_ge(sem("ks_done"), i + 1)
                ch.step(act.activation(KS[:, i // 4, i % 4, :], bank(4 + i % 4), ACT.Copy), sem("ks_ready"))
            act.wait_ge(sem("filter_sum"), 1)
            act.wait_ge(sem("x_landed"), 16)
            norm_stats(X)
            turn_evac("hy", HT)
            act.wait_ge(sem("norm_turned"), 4)
            act.wait_ge(sem("ctx_landed"), 16)
            norm_stats(CX)
            turn_evac("ctx", HCT)
            base = sa.first["hy_in"]
            for j in range(6):
                sa.wait_done(act, base + j)
                if j == 0:
                    act.wait_ge(sem("norm_h"), 4)
                for m in range(2):
                    c = 2 * j + m
                    ch.step(act.activation(ZC[:, c, :], PS[j % 4][:, SEQ * m:SEQ * m + SEQ], ACT.Identity,
                                           scale=short_w[:, 1, c:c + 1], bias=short_b[:, c:c + 1]), sem("zc_tap"))
            base = sa.first["q_in"]
            for j in range(2):
                sa.wait_done(act, base + j)
                for m in range(2):
                    src = PS[4 + j][:, SEQ * m:SEQ * m + SEQ].rearrange("p (r c) -> p r c", c=GRID_W)
                    dst = QT[:, 2 * j + m, :].rearrange("p (r c) -> p r c", c=GRID_W)[:, :, ::-1]
                    ins = act.activation(dst, src, ACT.Copy)
                ch.step(ins, sem("qkv_ready"))
            base = sa.first["k_in"]
            for j in range(2):
                sa.wait_done(act, base + j)
                for s, dst in enumerate((KT, KCT)):
                    ch.step(act.activation(dst[:, 2 * j:2 * j + 2, :], bank((6 if j == 0 else 0) + s, 2), ACT.Copy), sem("qkv_ready"))
            sa.wait_done(act, sa.first["v_in"] + 1)
            for s in range(4):
                ch.step(act.activation((V if s < 2 else VC)[:, s % 2, :], bank(2 + s), ACT.Copy), sem("qkv_ready"))
            for o in range(2):
                for t in range(TT):
                    act.wait_ge(sem("hy_turned"), 2 * o + t + 1)
                    ch.step(act.activation(VT[:, t, :], bank(t), ACT.Copy), sem("hy_vt"))
            def context_scores(it):
                act.wait_ge(sem("na_scores"), it + 1)
                if it >= 2:
                    act.wait_ge(sem("na_exp"), it - 1)
                ch.step(act.activation(NS[it % 2][:, SEQ:2 * SEQ], PS[it % 2][:, SEQ:2 * SEQ], ACT.Copy, scale=HEAD_DIM ** -0.5), sem("na_ctx"))

            context_scores(0)
            for it in range(TT * HEADS):
                act.wait_ge(sem("na_max"), it + 1)
                if it >= 2:
                    act.wait_ge(sem("na_turned"), it - 1)
                ch.step(act.activation(NP[it % 2], NS[it % 2], ACT.Exp, bias=mx[:, it % 2:it % 2 + 1],
                                       accum_out=rsum[:, it:it + 1]), sem("na_exp"))
                if it + 1 < TT * HEADS:
                    context_scores(it + 1)
                act.wait_ge(sem("na_turned"), it + 1)
                if it >= 2:
                    act.wait_ge(sem("na_out"), it - 1)
                ch.step(act.activation(NPT[it % 2], bank(2 + it % 2, 4), ACT.Copy), sem("na_pt"))
            for t in range(TT):
                act.wait_ge(sem("na_o_turned"), t + 1)
                for k in range(4):
                    src = PS[6 + t][:, P * k:P * k + P].rearrange("p (r c) -> p r c", c=GRID_W)
                    dst = YT[:, 4 + k, P * t:P * t + P].rearrange("p (r c) -> p r c", c=GRID_W)[:, :, ::-1]
                    ins = act.activation(dst, src, ACT.Copy)
                ch.step(ins, sem("yt_na"))
            norm_stats(X, 1, 0)
            turn_evac("ffn", HT)
            gated_ffn(sa, "ffn_up", HID_FFN)
            norm_stats(X, 2, 1)
            ada_evac(1)
            turn_evac("four", HT)
            for i in range(0, 8, 2):
                act.wait_ge(sem("four_feat"), i + 1)
                ch.step(act.activation(FAB[:, i // 4, i % 4, :], bank(i), ACT.Copy), sem("four_ab_act"))
            for f in range(4):
                act.wait_ge(sem("four_tok"), f + 1)
                ch.step(act.activation(FYT[:, 2 * f:2 * f + 2, :], bank(f, 2), ACT.Copy), sem("four_yt"))
            norm_stats(X, 3, 2)
            turn_evac("moe", HT)
            moe_scalar(act, ch)
            act.wait_ge(sem("x_added"), 1 + EXPERTS)
            norm_stats(X)
            norm_stats(X, 4)
            ada_evac(2)
            turn_evac("ret", HT)
            act.wait_ge(sem("ret_arg"), 1)
            ch.step(act.activation(RSIN, RANG[2], ACT.Sin), sem("ret_table"))
            act.wait_ge(sem("ret_arg"), 2)
            ch.step(act.activation(RCOS, RANG[3], ACT.Sin), sem("ret_table"))
            base = sbm.first["ret_vg"]
            for n in range(8):
                sbm.wait_done(act, base + 2 * n + 1)
                for t in range(TT):
                    dst = (RV if n < 4 else SG)[:, t, n % 4, :]
                    ch.step(act.activation(dst, bank(2 + 2 * (n % 2) + t), ACT.Copy if n < 4 else ACT.Silu), sem("vg_ready"))
            for h in range(RET_HEADS):
                act.wait_ge(sem("ret_var"), h + 1)
                ch.step(act.activation(gstd, bn2[:, :, 1], ACT.Sqrt, bias=eps), sem("ret_std"))
                if h >= 1:
                    ret_turn_evac(act, ch, h - 1)
            ret_turn_evac(act, ch, RET_HEADS - 1)
            norm_stats(X, 5, 3)
            turn_evac("cf0", HT)
            gated_ffn(sbm, "cf_up0", HID_CF[0], 0)
            act.wait_ge(sem("ada_added"), 4 * ADA_N * 3)
            ch.step(act.activation(SP[:, 0, :], log_dt, ACT.Exp), sem("s5_dt"))
            act.wait_ge(sem("s5_arg"), 1)
            ch.step(act.activation(SP[:, 3, :], SP[:, 2, :], ACT.Exp), sem("s5_trig"))
            ch.step(act.activation(EK[:, 1], EA[:, 2], ACT.Sin), sem("s5_trig"))
            ch.step(act.activation(EK[:, 0], EA[:, 3], ACT.Sin), sem("s5_trig"))
            norm_stats(X, 6, 4)
            ada_evac(3)
            turn_evac("s5", HT)
            base = sbm.first["s5_in"]
            for j in range(4):
                sbm.wait_done(act, base + j)
                ch.step(act.activation(UT[:, 2 * j:2 * j + 2, :], bank(4 + j, 2), ACT.Copy), sem("s5_u"))
            for q in range(KD):
                act.wait_ge(sem("s5_du"), q + 1)
                ch.step(act.activation(S5Y[:, q, :], SU, ACT.Gelu_apprx_tanh), sem("s5_gelu"))
            for t in range(TT):
                if t == 0:
                    act.wait_ge(sem("rows_first"), 6)
                else:
                    sbm.wait_done(act, sbm.first["glu"] + KD - 1)
                for n in range(2):
                    i = 2 * t + n
                    if i:
                        act.wait_ge(sem("glu_used"), i)
                    ch.step(act.activation(GLS, bank(4 * t + 2 + n), ACT.Sigmoid), sem("glu_sig"))
            norm_stats(X, 7)
            turn_evac("cf1", HT)
            gated_ffn(sbm, "cf_up1", HID_CF[1], 1)
            norm_stats(X, 8, 5)

        @block.vector
        def _(dve):
            ch = Chain(dve, sem("dve_chain"))
            link = ch.link

            def tt(out, a, b, op, s=None):
                link(dve.tensor_tensor(out=out, in0=a, in1=b, op=op), s)

            def ts(out, a, s1, s2, op0, op1=ALU.bypass, s=None):
                if s2 is None:
                    link(dve.tensor_scalar(out, a, s1, None, op0), s)
                else:
                    link(dve.tensor_scalar(out, a, s1, s2, op0, op1), s)

            def stt(out, a, sc, b, op0, op1, s=None):
                link(dve.scalar_tensor_tensor(out=out, in0=a, scalar=sc, in1=b, op0=op0, op1=op1), s)

            def to_period(dst, x, tmp, quarter, s):
                ts(tmp, x, 1.0 / TWO_PI, 0.25 * quarter, ALU.mult, ALU.add)
                ts(tmp, tmp, MAGIC, None, ALU.add)
                ts(tmp, tmp, -MAGIC, None, ALU.add)
                stt(dst, tmp, -PI_A, x, ALU.mult, ALU.add)
                stt(dst, tmp, -PI_B, dst, ALU.mult, ALU.add)
                stt(dst, tmp, -PI_C, dst, ALU.mult, ALU.add)
                if quarter:
                    ts(dst, dst, 0.5 * math.pi * quarter, None, ALU.add)
                ts(dst, dst, PI_CLAMP, -PI_CLAMP, ALU.min, ALU.max, s)

            def gain_of(name, gain, scale):
                if gain == "load":
                    dve.wait_ge(sem("gain_landed"), 16 * (GB_LOADS[name] + 1))
                    stt(G[:, :], scale, 1.0, G[:, :], ALU.add, ALU.mult)
                else:
                    ts(G[:, :], scale, 1.0, None, ALU.add)

            def inverse_rms(name, t):
                dve.wait_ge(sem("norm_std"), TT * NORM[name] + t + 1)
                link(dve.reciprocal(rinv[:, t:t + 1], std[:, t:t + 1]))

            def scale_shift(name, x, shift):
                for t in range(TT):
                    inverse_rms(name, t)
                    stt(H[:, t, :], x[:, t, :], rinv[:, t:t + 1], G[:, :], ALU.mult, ALU.mult, sem("gain_used") if t == TT - 1 else None)
                    tt(H[:, t, :], H[:, t, :], shift, ALU.add, sem("norm_h"))

            def turn_evac(name, dst):
                i = TURN[name]
                for t in range(TT):
                    dve.wait_ge(sem("norm_turned"), 4 * i + 2 * t + 2)
                    link(dve.tensor_copy(dst[:, 4:8, P * t:P * t + P], bank(2 * t + 1, 4)), sem("ht_dve"))

            def ada_evac0(first, last):
                for n in range(first, last):
                    sa.wait_done(dve, sa.first["ada0"] + 2 * n + 1)
                    dve.wait_ge(sem("bias_landed"), 16 * (n + 1))
                    if n < 4:
                        tt(ACX[:, BANK * n:BANK * (n + 1)], bank(2 + n % 2), BB[:, :], ALU.add)
                    tt(AD[:, BANK * n:BANK * (n + 1)], bank(n % 2), BB[:, :], ALU.add, sem("ada_evac"))

            def ada_evac(a):
                for n in range(0, ADA_N, 2):
                    dve.wait_ge(sem("ada_summed"), ADA_N * (a - 1) + n + 1)
                    link(dve.tensor_copy(AD[:, BANK * n:BANK * (n + 1)], bank(n % 4)), sem("ada_even"))
                dve.wait_ge(sem("ada_odd"), ADA_N // 2 * a)

            def add_to_x(addition, st, last, gate, tmp):
                for t in range(TT):
                    if t == 0:
                        dve.wait_ge(sem("rows_first"), addition + (1 if addition < 5 else 2))
                    else:
                        st.wait_done(dve, last)
                    for n in range(2):
                        c = slice(BANK * n, BANK * n + BANK)
                        tt(tmp, bank(4 + 2 * t + n), gate[:, c], ALU.mult)
                        tt(X[:, t, c], X[:, t, c], tmp, ALU.add, sem("x_ready") if t + n == 2 else sem("x_part"))

            def ada_add(i):
                a, n, q = ADA_HALVES[i]
                acc, c0 = ADA_ACC[a][:, BANK * n:BANK * (n + 1)], 0 if a < 2 else 16
                dve.wait_ge(sem(f"ada_started{a}"), 16)
                dve.wait_ge(sem(f"ada_landed{i % ADA_SLOTS}"), 16 * (i // ADA_SLOTS + 1))
                for k in range(2):
                    w, c = ADA_RING[a][:, i % ADA_SLOTS, k, :], csil[:, c0 + 2 * q + k:c0 + 2 * q + k + 1]
                    stt(acc, w, c, acc, ALU.mult, ALU.add, sem("ada_added") if k else None)

            def gated_ffn(st, up, hid_base, conv=None, ada={}):
                base = st.first[up]
                for j in range(FF // 256):
                    b = 2 * (j % 2)
                    for i, after in ada.items():
                        if 2 * j - 2 < after - (RING - 1) <= 2 * j:
                            ada_add(i)
                    if conv is not None:
                        k = (FF // 256) * conv + j
                        dve.wait_ge(sem("conv_tap"), 2 * k + 2)
                        for m in range(2):
                            c = 2 * j + m
                            g, o = GC[j % 2][:, m, :], SEQ * m
                            stt(g[:, 2:SEQ], PS[b][:, o:o + SEQ - 2], conv_w[conv][:, 0, c:c + 1], g[:, 2:SEQ], ALU.mult, ALU.add)
                            stt(g[:, 1:SEQ], PS[b][:, o:o + SEQ - 1], conv_w[conv][:, 1, c:c + 1], g[:, 1:SEQ], ALU.mult, ALU.add,
                                sem("conv_done") if m else None)
                    st.wait_done(dve, base + 2 * j + 1)
                    dve.wait_ge(sem("silu_done"), hid_base + j + 1)
                    tt(HID[:, 2 * j:2 * j + 2, :], SIL[j % 2], bank(b + 1, 2), ALU.mult, sem("hid_ready"))
                for i, after in ada.items():
                    if after - (RING - 1) > 2 * (FF // 256) - 2:
                        ada_add(i)

            link(dve.memset(eps, EPS), sem("eps_set"))
            dve.wait_ge(sem("c_silu"), 1)
            link(dve.tensor_copy(CB[:, :, :], along(csil[:, 0:8], P)), sem("cb_ready"))
            link(dve.tensor_copy(CBX, along(csil[:, 8:16], P)), sem("cb_ready"))
            ada_evac0(0, 4)
            dve.wait_ge(sem("filter_landed"), 144)
            for l in range(2):
                dve.wait_ge(sem("filter_h"), l + 1)
                ts(FA[0], PS[4 + l][0:HY_HID, 0:SEQ], FV[:, l:l + 1], FV[:, 2 + l:3 + l], ALU.add, ALU.mult)
                to_period(FA[2], FA[0], FA[1], 0, sem("filter_arg"))
                ada_evac0(4 + l, 5 + l)
            for i in range(8):
                t, n = i // 4, i % 4
                dve.wait_ge(sem("filter_raw"), i + 1)
                tt(FH[:, t, n, :], bank(4 + i % 4), DEC[:, t, :], ALU.mult, sem("filter_ready"))
            link(dve.memset(FH[0:1, 0].rearrange("p (o d) n -> p o d n", d=2)[:, :, 1, :], 0.0), sem("filter_ready"))
            ada_evac0(6, 8)
            dve.wait_ge(sem("filter_sum"), 1)
            ts(sk_rn, PS[4][:, 0:8], EPS, None, ALU.add, s=sem("filter_norm"))
            link(dve.reciprocal(sk_rn, sk_rn))
            ada_evac0(8, ADA_N)
            gain_of("hy", "load", ada_part(1))
            scale_shift("hy", X, ada_part(0))
            turn_evac("hy", HT)
            gain_of("ctx", "load", ACX[:, D:2 * D])
            scale_shift("ctx", CX, ACX[:, 0:D])
            turn_evac("ctx", HCT)
            base = sa.first["hy_in"]
            for j in range(6):
                dve.wait_ge(sem("zc_tap"), 2 * j + 2)
                for m in range(2):
                    c, o = 2 * j + m, SEQ * m
                    stt(ZC[:, c, 1:SEQ], PS[j % 4][:, o:o + SEQ - 1], short_w[:, 0, c:c + 1], ZC[:, c, 1:SEQ], ALU.mult, ALU.add)
                    stt(ZC[:, c, 0:SEQ - 1], PS[j % 4][:, o + 1:o + SEQ], short_w[:, 2, c:c + 1], ZC[:, c, 0:SEQ - 1], ALU.mult, ALU.add,
                        sem("zc_ready") if m else None)
            T4 = HYT
            for o in range(2):
                dve.wait_ge(sem("hy_spec"), o + 1)
                if o:
                    dve.wait_ge(sem("hy_conv"), 4)
                for f in range(2):
                    ur, ui, kr, ki = bank(2 + f), bank(4 + f), KS[:, o, f, :], KS[:, o, 2 + f, :]
                    tt(YF[:, f, :], ur, kr, ALU.mult)
                    tt(T4[0], ui, ki, ALU.mult)
                    tt(YF[:, 2 + f, :], ur, ki, ALU.mult)
                    tt(T4[1], ui, kr, ALU.mult)
                    tt(YF[:, f, :], YF[:, f, :], T4[0], ALU.subtract)
                    tt(YF[:, 2 + f, :], YF[:, 2 + f, :], T4[1], ALU.add)
                tt(YF[0:1, 0, :], PS[2][0:1, :], KS[0:1, o, 0, :], ALU.mult)
                tt(YF[0:1, 2, :], PS[4][0:1, :], KS[0:1, o, 2, :], ALU.mult, sem("hy_prod"))
                for c in range(4):
                    dve.wait_ge(sem("hy_conv"), 4 * o + 2 * (c // 2) + 2)
                    y = PS[6 + c // 2][:, SEQ * (c % 2):SEQ * (c % 2) + SEQ]
                    tmp = T4[c % 2][:, 0:SEQ]
                    ts(tmp, y, sk_rn[:, 4 * o + c:4 * o + c + 1], None, ALU.mult)
                    stt(tmp, ZC[:, c, :], skip[:, 4 * o + c:4 * o + c + 1], tmp, ALU.mult, ALU.add)
                    tt((YT if o else ZC)[:, c, :], ZC[:, 4 * (o + 1) + c, :], tmp, ALU.mult, sem("hy_out"))
            for it in range(TT * HEADS):
                gi = it // 4
                dve.wait_ge(sem("na_scores"), it + 1)
                dve.wait_ge(sem("rpb_ready"), gi + 1)
                if it >= 2:
                    dve.wait_ge(sem("na_exp"), it - 1)
                dve.wait_ge(sem("na_ctx"), it + 1)
                stt(NS[it % 2][:, 0:SEQ], PS[it % 2][:, 0:SEQ], HEAD_DIM ** -0.5,
                    BIA[gi % 2][:, it % 4].rearrange("p r k -> p (r k)"), ALU.mult, ALU.add)
                link(dve.tensor_reduce(mx[:, it % 2:it % 2 + 1], NS[it % 2], AX.X, ALU.max, negate=True), sem("na_max"))
            dve.wait_ge(sem("na_exp"), TT * HEADS)
            link(dve.reciprocal(rsum_inv, rsum))
            for t in range(TT):
                dve.wait_ge(sem("na_out"), HEADS * (t + 1))
                tt(NO[:, t, :].rearrange("p (h d) -> p h d", d=HEAD_DIM), bank(4 + t, HEADS),
                   along(rsum_inv[:, HEADS * t:HEADS * t + HEADS], HEAD_DIM), ALU.mult, sem("na_norm"))
            gain_of("ffn", "load", ada_part(4))
            add_to_x(0, sa, sa.first["mix"] + 3, ada_part(2), XT_MIX)
            scale_shift("ffn", X, ada_part(3))
            turn_evac("ffn", HT)
            gated_ffn(sa, "ffn_up", HID_FFN, ada=ADA_PLAN["ffn"])
            add_to_x(1, sa, sa.first["ffn_down"] + FF // 256 - 1, ada_part(5), XT)
            ada_evac(1)
            gain_of("four", "load", ada_part(1))
            scale_shift("four", X, ada_part(0))
            turn_evac("four", HT)
            for i in range(1, 8, 2):
                dve.wait_ge(sem("four_feat"), i + 1)
                link(dve.tensor_copy(FAB[:, i // 4, i % 4, :], bank(i)), sem("four_ab_dve"))
            gain_of("moe", "load", ada_part(4))
            add_to_x(2, sa, sa.first["four"] + 3, ada_part(2), XT)
            scale_shift("moe", X, ada_part(3))
            turn_evac("moe", HT)
            moe_vector(dve, ch)
            dve.wait_ge(sem("gain_landed"), 16 * (GB_LOADS["fin0"] + 1))
            for t in range(TT):
                inverse_rms("fin0", t)
                stt(X[:, t, :], X[:, t, :], rinv[:, t:t + 1], G[:, :], ALU.mult, ALU.mult, sem("x_ready") if t else None)
            ada_evac(2)
            gain_of("ret", "scale", ada_part(1))
            scale_shift("ret", X, ada_part(0))
            turn_evac("ret", HT)
            dve.wait_ge(sem("ret_landed"), 48)
            link(dve.tensor_copy(RANG[0], RPOS))
            ts(RANG[0], RANG[0], INVF, None, ALU.mult)
            to_period(RANG[2], RANG[0], RANG[1], 0, sem("ret_arg"))
            to_period(RANG[3], RANG[0], RANG[1], 1, sem("ret_arg"))
            dve.wait_ge(sem("ret_table"), 2)
            base = sbm.first["ret_qk"]
            for j in range(RET_TILES):
                dst = (QR if j < 4 else KR)[:, 2 * (j % 4):2 * (j % 4) + 2, :]
                sbm.wait_done(dve, base + j)
                tt(RM[0], bank(j % 2, 2), over(RCOS, 2), ALU.mult)
                tt(RM[1], bank(j % 2, 2), over(RSIN, 2), ALU.mult, sem("rot_done"))
                tt(dst[:, 0, :], RM[0][:, 0, :], RM[1][:, 1, :], ALU.subtract)
                tt(dst[:, 1, :], RM[1][:, 0, :], RM[0][:, 1, :], ALU.add, sem("rot_out"))
            for h in range(RET_HEADS):
                def decay(h):
                    dve.wait_ge(sem("ret_scored"), h + 1)
                    if h >= 2:
                        dve.wait_ge(sem("ret_o"), h - 1)
                    tt(RS[h % 2], PS[6 + h % 2][:, 0:384], RT[:, h, :], ALU.mult, sem("ret_decayed"))
                if h == 0:
                    decay(0)
                if h + 1 < RET_HEADS:
                    decay(h + 1)
                dve.wait_ge(sem("ret_o"), h + 1)
                for t in range(TT):
                    link(dve.bn_stats(bn6[:, t, :], bank(2 * (h % 2) + t)))
                    link(dve.bn_aggr(bn2[:, t, :], bn6[:, t, :]), sem("ret_var") if t else None)
                dve.wait_ge(sem("ret_std"), h + 1)
                link(dve.reciprocal(grstd, gstd))
                for t in range(TT):
                    ts(RON, bank(2 * (h % 2) + t), bn2[:, t, 0:1], grstd[:, t:t + 1], ALU.subtract, ALU.mult)
                    tt(SG[:, t, h, :], SG[:, t, h, :], RON, ALU.mult, sem("ret_gated"))
            gain_of("cf0", "scale", ada_part(4))
            add_to_x(3, sbm, sbm.first["ret_out"] + 7, ada_part(2), RXT)
            scale_shift("cf0", X, ada_part(3))
            turn_evac("cf0", HT)
            gated_ffn(sbm, "cf_up0", HID_CF[0], 0, ADA_PLAN["cf0"])
            s5_angles(dve, tt, ts, to_period)
            add_to_x(4, sbm, sbm.first["cf_down0"] + FF // 256 - 1, ada_part(5), XT)
            s5_vector(dve, ch, tt, ts, stt, to_period, gain_of, scale_shift, turn_evac, ada_evac)
            scale_shift("cf1", X, ada_part(3))
            turn_evac("cf1", HT)
            gated_ffn(sbm, "cf_up1", HID_CF[1], 1)
            add_to_x(5, sbm, sbm.first["cf_down1"] + FF // 256 - 1, ada_part(5), XT)
            dve.wait_ge(sem("gain_landed"), 16 * (GB_LOADS["fin1"] + 1))
            for t in range(TT):
                inverse_rms("fin1", t)
                stt(H[:, t, :], X[:, t, :], rinv[:, t:t + 1], G[:, :], ALU.mult, ALU.mult, sem("out_ready") if t else None)



def shape_tables():
    f32 = np.float32
    tab = {}
    n = SEQ
    t = np.linspace(0.0, 1.0, n, dtype=f32)[:, None]
    bands = np.linspace(1e-4, HY_BANDS - 1, HY_BANDS, dtype=f32)
    ang = (f32(2.0 * math.pi / n) * np.arange(n, dtype=f32)[:, None]) * bands[None, :]
    feats = np.concatenate([t, np.cos(ang), -np.sin(ang)], axis=-1).astype(f32)
    tab["t_feats"] = feats.T.copy()
    deltas = np.abs(np.linspace(math.log(1e-2) / 1.5, math.log(1e-2) / 0.3, CH, dtype=f32))
    decay = np.exp(-t * deltas[None, :]).astype(f32)
    tab["t_decay"] = decay.reshape(2, P, CH).transpose(1, 0, 2)
    f = np.arange(n)
    lag = np.arange(n)[:, None]
    phase = 2 * np.pi * ((lag * f[None, :]) % (2 * n)) / (2 * n)
    nyquist = np.where(np.arange(n) % 2 == 0, 1.0, -1.0)
    cos, sin = np.cos(phase), np.sin(phase)
    fwd_im, bwd_im = -sin, sin.copy()
    fwd_im[:, 0], bwd_im[:, 0] = nyquist, nyquist
    tab["t_dft_fwd"] = np.concatenate([cos, fwd_im], 1).astype(f32).reshape(2, P, 2 * n).transpose(1, 0, 2)
    tab["t_dft_bwd"] = np.concatenate([cos, bwd_im], 1).astype(f32).reshape(2, P, 2 * n).transpose(1, 0, 2)
    weight = np.where(f == 0, 1.0, 2.0)[:, None] / (2 * n)
    inv_re, inv_im = weight * cos.T, -weight * sin.T
    inv_im[0] = nyquist / (2 * n)
    tab["t_idft"] = np.concatenate([inv_re, inv_im], 0).astype(f32).reshape(4, P, n).transpose(1, 0, 2)
    q = 63 - (np.arange(P) % 64)
    start = np.clip(q - WIN_C // 2, 0, GRID_W - WIN_C)[:, None]
    key = np.arange(GRID_W)[None, :]
    tab["t_window"] = np.where((key >= start) & (key < start + WIN_C), 0.0, NEG).astype(f32)
    d = np.arange(n)
    ph = 2 * np.pi * ((d[:, None] * d[None, :]) % n) / n
    tab["t_four_d"] = np.concatenate([np.cos(ph), np.sin(ph)], 1).astype(f32).reshape(2, P, 2 * n).transpose(1, 0, 2)
    tab["t_four_l"] = np.stack([np.cos(ph) / n, -np.sin(ph) / n], 0).astype(f32).reshape(2, 2, P, n).transpose(2, 0, 1, 3)
    lg = np.log1p(-np.exp2(-5.0 - np.arange(RET_HEADS)))
    m = np.arange(n)[:, None]
    k = np.arange(n)[None, :]
    full = np.where(k >= m, np.exp(lg[:, None, None] * np.maximum(k - m, 0)), 0.0) * RET_DK ** -0.5
    tab["t_ret"] = np.concatenate([full[:, :P, :], full[:, P:, P:]], 2).astype(f32).transpose(1, 0, 2)
    half = RET_DK // 2
    tab["t_inv_freq"] = np.power(f32(10000.0), -np.arange(half, dtype=f32) / f32(half)).astype(f32)[:, None]
    tab["t_ident"] = np.eye(P, dtype=f32)
    tab["t_before"] = np.triu(np.ones((P, P), f32), 1)
    tab["t_iota"] = np.broadcast_to(np.arange(P, dtype=f32), (P, P))
    return {name: np.ascontiguousarray(a, dtype=f32) for name, a in tab.items()}


def by_partition(a, p=P):
    a = np.asarray(a)
    a = a.reshape(-1, a.shape[-1] // p, p)
    return a.transpose(2, 0, 1).reshape(p, -1)


def laid_out(x):
    out = {}
    for name in ("w_ada", "w_in", "w_mix_out", "ffn_w1", "ffn_w3", "ffn_w2", "w_fourier", "moe_w1", "moe_w3", "moe_w2",
                 "ada_w_2", "ret_w_in_2", "ret_w_out_2", "s5_w_in_2", "s5_w_glu_2", "ffn_w_up_2", "ffn_w_down_2",
                 "x", "ctx", "b_ada", "ada_b_2", "norm_g", "final_g", "final_norm_g_2", "na_rpb", "pos_2",
                 "hy_f_w1", "hy_f_w2", "hy_f_w3", "b_router"):
        out[name] = np.ascontiguousarray(x[name])
    out["filter_vectors"] = np.ascontiguousarray(np.stack(
        [x["hy_f_b1"][0], x["hy_f_b2"][0], x["hy_f_freq"][0, 0], x["hy_f_freq"][0, 1]], 1))
    router = np.asarray(x["w_router"])[0]
    out["w_router"] = np.ascontiguousarray(router.reshape(KD, P, EXPERTS).transpose(1, 0, 2))
    def states(a):
        return np.asarray(a).reshape(S5_TILES, 2, S5_STATE).transpose(1, 2, 0).reshape(P, S5_TILES)
    dt = np.repeat(np.asarray(x["s5_log_dt_2"])[0].reshape(S5_TILES, 2).T[:, None, :], S5_STATE, 1).reshape(P, S5_TILES)
    cols = [by_partition(x["c"]), by_partition(x["c_ctx"]), by_partition(x["c_2"]),
            by_partition(x["hy_short_w"][0]), by_partition(x["hy_short_b"]), by_partition(x["hy_skip"][0]),
            states(x["s5_lam_re_2"][0]), states(x["s5_lam_im_2"][0]), dt, by_partition(x["s5_d_2"]),
            by_partition(x["ffn_conv_w_2"][0, :, 0]), by_partition(x["ffn_conv_w_2"][1, :, 0]),
            by_partition(x["ffn_conv_b_2"])]
    out["vectors"] = np.ascontiguousarray(np.concatenate(cols, 1))
    for name, src in (("s5_b_re", "s5_b_re_2"), ("s5_b_im", "s5_b_im_2")):
        b = np.asarray(x[src])[0].reshape(KD, 4, 2, S5_STATE, S5_GROUP)
        blocks = np.zeros((4, 2, S5_GROUP, KD, 2, S5_STATE), b.dtype)
        for gp in range(2):
            blocks[:, gp, :, :, gp, :] = b[:, :, gp].transpose(1, 3, 0, 2)
        out[name] = blocks.reshape(P, KD, P)
    for name, src in (("s5_c_re", "s5_c_re_2"), ("s5_c_im", "s5_c_im_2")):
        c = np.asarray(x[src])[0].reshape(S5_TILES, 2, S5_GROUP, S5_STATE)
        blocks = np.zeros((2, S5_STATE, S5_TILES, 2, S5_GROUP), c.dtype)
        for gp in range(2):
            blocks[gp, :, :, gp, :] = c[:, gp].transpose(2, 0, 1)
        out[name] = blocks.reshape(P, S5_TILES, 2 * S5_GROUP)
    return out


def kernel(**inputs):
    import concourse.bacc as bacc
    from concourse.bass_utils import run_bass_kernel_spmd

    nc = bacc.Bacc("TRN2", target_bir_lowering=False, num_devices=1)
    arrays = {f"in_{name}": a for name, a in {**laid_out(inputs), **shape_tables()}.items()}
    given = {name[3:]: nc.dram_tensor(name, a.shape, mybir.dt.from_np(a.dtype), kind="ExternalInput").ap()
             for name, a in arrays.items()}
    out = nc.dram_tensor("out", (1, SEQ, D), F32, kind="ExternalOutput").ap()
    build(nc, given, out)
    result = run_bass_kernel_spmd(nc, [arrays], core_ids=[0])
    return result.results[0]["out"]
```
